# Optimizing a Trainium2 kernel written in Bass

```python
import math
import jax, jax.numpy as jnp
from jax import lax
import numpy as np

D_MODEL = 1024
BATCH = 1
SEQ = 1024
DEPTH = 1

MIX_WIDTH = D_MODEL
DA_HEAD = 64
DA_VDIM = 2 * DA_HEAD
DA_WIDTH = MIX_WIDTH // 2
DA_HEADS = DA_WIDTH // DA_VDIM
CF_WIDTH = MIX_WIDTH // 4
CF_GROUPS = 4
CF_CONV = 31
SC_WIDTH = MIX_WIDTH // 4
SC_CONV = 3
IN_COLS = 3 * DA_WIDTH + 2 * CF_WIDTH + 3 * SC_WIDTH

Q_BLOCK = 128
RMS_EPS = 1e-6
LN_EPS = 1e-5

PEER_HEADS = 8
N_KEYS = 128
N_EXPERTS = N_KEYS * N_KEYS
PEER_QDIM = 256
PEER_TOPK = 16
PEER_CHUNK = 128

kernel_name = "hybrid_diffattn_conformer_shortconv_peer"

def rmsnorm(x, g):
    xf = x.astype(jnp.float32)
    y = xf * lax.rsqrt(jnp.mean(xf * xf, axis=-1, keepdims=True) + RMS_EPS)
    return (y * g.astype(jnp.float32)).astype(x.dtype)

def group_layernorm(x, g, b, groups):
    shp = x.shape
    xf = x.astype(jnp.float32).reshape(shp[:-1] + (groups, shp[-1] // groups))
    mu = jnp.mean(xf, axis=-1, keepdims=True)
    xc = xf - mu
    var = jnp.mean(xc * xc, axis=-1, keepdims=True)
    y = (xc * lax.rsqrt(var + LN_EPS)).reshape(shp)
    return (y * g.astype(jnp.float32) + b.astype(jnp.float32)).astype(x.dtype)

def causal_depthwise_conv(x, w):
    k, c = w.shape
    return lax.conv_general_dilated(
        x, w[:, None, :].astype(x.dtype), window_strides=(1,), padding=[(k - 1, 0)],
        dimension_numbers=("NWC", "WIO", "NWC"), feature_group_count=c)

def diff_attention(q, k, v, lam):
    b, s, h, _, d = q.shape
    nb = s // Q_BLOCK
    scale = d ** -0.5
    qb = q.reshape(b, nb, Q_BLOCK, h, 2, d).transpose(1, 0, 2, 3, 4, 5)
    kpos = jnp.arange(s)

    def block(args):
        q_blk, i = args
        qpos = i * Q_BLOCK + jnp.arange(Q_BLOCK)
        logits = jnp.einsum("bqhcd,bkhcd->bhcqk", q_blk, k,
                            preferred_element_type=jnp.float32) * scale
        mask = kpos[None, :] <= qpos[:, None]
        logits = jnp.where(mask, logits, -jnp.inf)
        p = jax.nn.softmax(logits, axis=-1)
        wts = p[:, :, 0] - lam * p[:, :, 1]
        return jnp.einsum("bhqk,bkhe->bqhe", wts.astype(v.dtype), v)

    out = lax.map(block, (qb, jnp.arange(nb)))
    return out.transpose(1, 0, 2, 3, 4).reshape(b, s, h, v.shape[-1])

def hybrid_mixer(h, w_in, q_norm_g, k_norm_g, lam_q1, lam_k1, lam_q2, lam_k2, lam_init,
                 subln_g, cf_dw, cf_dw_b, cf_ln_g, cf_ln_b, sc_w, w_out):
    b, s, _ = h.shape
    z = h @ w_in
    o1 = DA_WIDTH
    o2 = o1 + DA_WIDTH
    o3 = o2 + DA_WIDTH
    o4 = o3 + CF_WIDTH
    o5 = o4 + CF_WIDTH
    o6 = o5 + SC_WIDTH
    o7 = o6 + SC_WIDTH
    q, k, v, cf_a, cf_gate, sc_b, sc_c, sc_x = jnp.split(z, [o1, o2, o3, o4, o5, o6, o7], axis=-1)

    q = rmsnorm(q.reshape(b, s, DA_HEADS, 2, DA_HEAD), q_norm_g)
    k = rmsnorm(k.reshape(b, s, DA_HEADS, 2, DA_HEAD), k_norm_g)
    v = v.reshape(b, s, DA_HEADS, DA_VDIM)
    lam = (jnp.exp(jnp.sum(lam_q1.astype(jnp.float32) * lam_k1.astype(jnp.float32)))
           - jnp.exp(jnp.sum(lam_q2.astype(jnp.float32) * lam_k2.astype(jnp.float32)))
           + lam_init)
    a = diff_attention(q, k, v, lam)
    a = rmsnorm(a, subln_g) * (1.0 - lam_init)
    a = a.reshape(b, s, DA_WIDTH)

    u = cf_a * jax.nn.sigmoid(cf_gate)
    u = causal_depthwise_conv(u, cf_dw) + cf_dw_b
    u = jax.nn.silu(group_layernorm(u, cf_ln_g, cf_ln_b, CF_GROUPS))

    c = sc_b * causal_depthwise_conv(sc_c * sc_x, sc_w)

    return jnp.concatenate([a, u, c], axis=-1) @ w_out

def peer(h, wq, keys, u_tab, v_tab):
    b, s, d = h.shape
    hc = h.reshape((b * s) // PEER_CHUNK, PEER_CHUNK, d)

    def chunk(xc):
        q = (xc @ wq).reshape(PEER_CHUNK, PEER_HEADS, 2, PEER_QDIM // 2)
        sub = jnp.einsum("thcd,hcnd->thcn", q, keys, preferred_element_type=jnp.float32)
        s_top, i_top = lax.top_k(sub, PEER_TOPK)
        cand = s_top[:, :, 0, :, None] + s_top[:, :, 1, None, :]
        cand = cand.reshape(PEER_CHUNK, PEER_HEADS, PEER_TOPK * PEER_TOPK)
        sel_s, sel_i = lax.top_k(cand, PEER_TOPK)
        i1 = jnp.take_along_axis(i_top[:, :, 0], sel_i // PEER_TOPK, axis=-1)
        i2 = jnp.take_along_axis(i_top[:, :, 1], sel_i % PEER_TOPK, axis=-1)
        eid = i1 * N_KEYS + i2
        g = jax.nn.softmax(sel_s, axis=-1)
        ue = u_tab[eid]
        act = jax.nn.gelu(jnp.einsum("thkd,td->thk", ue, xc), approximate=False)
        ve = v_tab[eid]
        return jnp.einsum("thk,thkd->td", (g * act).astype(xc.dtype), ve)

    return lax.map(chunk, hc).reshape(b, s, d)

def setup_inputs(seed: int = 0) -> dict:
    key = jax.random.key(seed)
    ks = jax.random.split(key, 24)
    f32 = jnp.float32
    nrm = lambda k, shape, sc: jax.random.normal(k, shape, f32) * sc
    gain = lambda k, shape: 1.0 + 0.02 * jax.random.normal(k, shape, f32)
    L = DEPTH
    return {
        "x": jax.random.normal(ks[0], (BATCH, SEQ, D_MODEL), f32),
        "norm1_g": gain(ks[1], (L, D_MODEL)),
        "w_in": nrm(ks[2], (L, D_MODEL, IN_COLS), D_MODEL ** -0.5),
        "q_norm_g": gain(ks[3], (L, DA_HEAD)),
        "k_norm_g": gain(ks[4], (L, DA_HEAD)),
        "lam_q1": nrm(ks[5], (L, DA_HEAD), 0.1),
        "lam_k1": nrm(ks[6], (L, DA_HEAD), 0.1),
        "lam_q2": nrm(ks[7], (L, DA_HEAD), 0.1),
        "lam_k2": nrm(ks[8], (L, DA_HEAD), 0.1),
        "subln_g": gain(ks[9], (L, DA_VDIM)),
        "cf_dw": nrm(ks[10], (L, CF_CONV, CF_WIDTH), CF_CONV ** -0.5),
        "cf_dw_b": nrm(ks[11], (L, CF_WIDTH), 0.02),
        "cf_ln_g": gain(ks[12], (L, CF_WIDTH)),
        "cf_ln_b": nrm(ks[13], (L, CF_WIDTH), 0.02),
        "sc_w": nrm(ks[14], (L, SC_CONV, SC_WIDTH), SC_CONV ** -0.5),
        "w_out": nrm(ks[15], (L, MIX_WIDTH, D_MODEL), MIX_WIDTH ** -0.5),
        "norm2_g": gain(ks[16], (L, D_MODEL)),
        "peer_wq": nrm(ks[17], (L, D_MODEL, PEER_HEADS * PEER_QDIM), D_MODEL ** -0.5),
        "peer_keys": nrm(ks[18], (L, PEER_HEADS, 2, N_KEYS, PEER_QDIM // 2), (PEER_QDIM // 2) ** -0.5),
        "peer_u": nrm(ks[19], (L, N_EXPERTS, D_MODEL), D_MODEL ** -0.5),
        "peer_v": nrm(ks[20], (L, N_EXPERTS, D_MODEL), PEER_HEADS ** -0.5),
    }

def reference(x, norm1_g, w_in, q_norm_g, k_norm_g, lam_q1, lam_k1, lam_q2, lam_k2, subln_g,
              cf_dw, cf_dw_b, cf_ln_g, cf_ln_b, sc_w, w_out, norm2_g,
              peer_wq, peer_keys, peer_u, peer_v):
    for l in range(DEPTH):
        lam_init = 0.8 - 0.6 * math.exp(-0.3 * l)
        x = x + hybrid_mixer(rmsnorm(x, norm1_g[l]), w_in[l], q_norm_g[l], k_norm_g[l],
                             lam_q1[l], lam_k1[l], lam_q2[l], lam_k2[l], lam_init, subln_g[l],
                             cf_dw[l], cf_dw_b[l], cf_ln_g[l], cf_ln_b[l], sc_w[l], w_out[l])
        x = x + peer(rmsnorm(x, norm2_g[l]), peer_wq[l], peer_keys[l], peer_u[l], peer_v[l])
    return x


_drawn_inputs = setup_inputs


def setup_inputs(seed=0):
    import zlib

    import numpy as np

    out = dict(_drawn_inputs(seed))
    spreads = {}
    factors = {'q_norm_g': 2.98,
     'k_norm_g': 3.433,
     'lam_q1': 200.0,
     'subln_g': 10.788,
     'cf_dw_b': 3.331,
     'cf_ln_g': 14.608,
     'cf_ln_b': 17.998,
     'norm2_g': 7.635}
    for name, (base, spread) in spreads.items():
        noise = np.random.default_rng([zlib.crc32(name.encode()), seed]).standard_normal(out[name].shape)
        drawn = base * np.exp(spread * noise) if base else spread * noise
        out[name] = __import__('jax').numpy.asarray(drawn.astype(out[name].dtype))
    for name, factor in factors.items():
        out[name] = (out[name] * factor).astype(out[name].dtype)
    return out
```

```python
from contextlib import ExitStack

import numpy as np

import concourse.bass as bass
from concourse import mybir
from concourse.alu_op_type import AluOpType as ALU

ACT = mybir.ActivationFunctionType
AX = mybir.AxisListType
F32, F32R, BF16 = mybir.dt.float32, mybir.dt.float32r, mybir.dt.bfloat16
I32, U32, U16 = mybir.dt.int32, mybir.dt.uint32, mybir.dt.uint16

P = 128
SEQ = 1024
D = 1024
TT = SEQ // P
KT = D // P
HEADS = 4
DH = 64
DV = 2 * DH
DA = HEADS * DV
CONV = 256
CT = CONV // P
CF_TAPS = 31
SC_TAPS = 3
LN_GROUP = 64
N_KEYS = 128
PH = 8
TOPK = 16
RMS_EPS = 1e-6
LN_EPS = 1e-5
LAM_INIT = 0.8 - 0.6 * 1.0
MASKED = -1e30
TAKEN = -3.0e38
GB = 64


class Memory:

    def __init__(self, nc, start, end):
        self.nc, self.at, self.end = nc, start, end

    def sb(self, name, shape, dtype):
        size = int(np.prod(shape[1:])) * (2 if dtype in (BF16, U16) else 4)
        tensor = self.nc.alloc_sbuf_tensor_at(name, shape, dtype, offset=self.at)
        self.at += -(-size // 32) * 32
        assert self.at <= self.end, (name, self.at, self.end)
        return tensor


def project_phase(nc, mem, x, norm1_g, w_in, q_norm_g, k_norm_g, qT, kT, values, convT):
    QKV = 3 * DA
    GROUPS = 2 * DA // DH
    CONV_TILES = convT.shape[1]
    w_qkv = mem.sb("w_qkv", [P, KT, QKV], F32)
    w_conv = [mem.sb(f"w_conv{s}", [P, KT, P], F32) for s in range(2)]
    gain1 = mem.sb("gain1", [P, KT], F32)
    gain_q, gain_k = mem.sb("gain_q", [P, 1], F32), mem.sb("gain_k", [P, 1], F32)
    ident = mem.sb("ident_a", [P, P], F32)
    x_in = [mem.sb(f"x_in{s}", [P, D], F32) for s in range(2)]
    x_norm = mem.sb("x_norm", [P, D], F32)
    square = mem.sb("square", [P, D], F32)
    rms = mem.sb("rms", [P, 1], F32)
    hT = mem.sb("hT", [P, KT, SEQ], F32)
    h_tile = [mem.sb(f"h_tile{s}", [P, KT, P], F32) for s in range(2)]
    qk_norm = mem.sb("qk_norm", [P, 2 * DA], F32)
    qk_square = mem.sb("qk_square", [P, 2 * DA], F32)
    qk_rms = mem.sb("qk_rms", [P, GROUPS], F32)
    with ExitStack() as ctx:
        sem = lambda name: ctx.enter_context(nc.semaphore(name))
        turn_ps = ctx.enter_context(nc.psum_tensor("h_turn_ps", [P, KT, P], F32))
        qk_ps = ctx.enter_context(nc.psum_tensor("qk_ps", [P, 2 * DA], F32))
        v_ps = ctx.enter_context(nc.psum_tensor("v_ps", [P, DA], F32))
        qk_turn_ps = ctx.enter_context(nc.psum_tensor("qk_turn_ps", [P, 2 * HEADS, P], F32))
        x_loaded = [sem(f"x_loaded{s}") for s in range(2)]
        w_loaded, small_loaded = sem("w_loaded"), sem("small_loaded")
        conv_loaded = [sem(f"conv_loaded{s}") for s in range(2)]
        made, gain_scaled, mean_ready = sem("made_a"), sem("gain_scaled"), sem("mean_ready_a")
        qk_step = sem("qk_step")
        conv_ps = (qk_ps[:], turn_ps[:].rearrange("p k t -> p (k t)"))
        summed, root_asked, root_ready = sem("summed"), sem("root_asked"), sem("root_ready")
        norm_ready, turned, h_ready, h_kept = sem("norm_ready"), sem("turned_a"), sem("h_ready"), sem("h_kept")
        qkv_ready, qk_summed = sem("qkv_ready"), sem("qk_summed")
        qk_asked, qk_root, qk_ready, qk_turned = sem("qk_asked"), sem("qk_root"), sem("qk_ready"), sem("qk_turned")
        kept, conv_ready, conv_kept = sem("kept"), sem("conv_ready"), sem("conv_kept")
        block = ctx.enter_context(nc.Block())

        @block.sync
        def _(sp):
            for half in range(2):
                sp.dma_start(gain_q[DH * half:DH * (half + 1), :], q_norm_g).then_inc(small_loaded, 16)
                sp.dma_start(gain_k[DH * half:DH * (half + 1), :], k_norm_g).then_inc(small_loaded, 16)
            sp.dma_start(gain1[:], norm1_g).then_inc(small_loaded, 16)
            with sp.Fori(0, TT // 2) as pair:
                for s in range(2):
                    sp.wait_ge(norm_ready, 2 * pair + s + 1)
                    sp.dma_start(x_in[s][:], x[2 * pair + s]).then_inc(x_loaded[s], 16)
            with sp.Fori(0, CONV_TILES // 2) as pair:
                for s in range(2):
                    i = 2 * pair + s
                    sp.wait_ge(conv_ready, i + 1)
                    sp.dma_start(w_conv[s][:], w_in[:, bass.ds(QKV + P * i, P)].rearrange("(k p) n -> p k n", p=P))\
                      .then_inc(conv_loaded[s], 16)

        @block.gpsimd
        def _(pool):
            pool.memset(ident[:], 0.0).then_inc(made, 1)
            pool.wait_ge(made, 1)
            pool.affine_select(out=ident[:], in_=ident[:], compare_op=ALU.not_equal, fill=1.0, base=0,
                               pattern=[[-1, P]], channel_multiplier=1).then_inc(made, 1)

        @block.scalar
        def _(act):
            act.dma_start(w_qkv[:], w_in[:, 0:QKV].rearrange("(k p) n -> p k n", p=P)).then_inc(w_loaded, 16)

            def prepare(n, s, turn):
                act.wait_ge(x_loaded[s], 16 * (turn + 1))
                act.activation(square[:], x_in[s][:], ACT.Square, accum_out=rms[:]).then_inc(summed, 1)
                act.wait_ge(root_asked, n + 1)
                act.activation(rms[:], rms[:], ACT.Sqrt).then_inc(root_ready, 1)
                act.wait_ge(h_ready, n + 1)
                act.activation(hT[:, :, bass.ds(P * n, P)], h_tile[s][:], ACT.Copy).then_inc(h_kept, 1)

            def finish(n):
                act.wait_ge(qkv_ready, n + 1)
                act.activation(qk_square[:], qk_ps[:], ACT.Square).then_inc(qk_summed, 1)
                act.activation(values[:, n], v_ps[:], ACT.Copy).then_inc(qk_summed, 1)
                act.wait_ge(qk_asked, n + 1)
                act.activation(qk_rms[:], qk_rms[:], ACT.Sqrt).then_inc(qk_root, 1)
                act.wait_ge(qk_turned, n + 1)
                at = bass.ds(P * n, P)
                act.activation(qT[:, :, at], qk_turn_ps[:, 0:HEADS], ACT.Copy, scale=gain_q[:])
                act.activation(kT[:, :, at], qk_turn_ps[:, HEADS:], ACT.Copy, scale=gain_k[:]).then_inc(kept, 1)

            act.sem_inc(kept, 1)
            act.wait_ge(small_loaded, 80)
            act.wait_ge(gain_scaled, 1)
            prepare(0, 0, 0)
            with act.Fori(0, TT // 2 - 1) as pair:
                for s in range(2):
                    prepare(2 * pair + s + 1, 1 - s, pair + s)
                    finish(2 * pair + s)
            prepare(TT - 1, 1, TT // 2 - 1)
            finish(TT - 2)
            finish(TT - 1)
            act.sem_inc(conv_kept, 2)
            with act.Fori(0, CONV_TILES // 2) as pair:
                for s in range(2):
                    act.wait_ge(conv_ready, 2 + 2 * pair + s + 1)
                    act.activation(convT[:, 2 * pair + s], conv_ps[s], ACT.Copy).then_inc(conv_kept, 1)

        @block.vector
        def _(dve):
            SCALE = float(DH) ** -0.5
            dve.wait_ge(small_loaded, 80)
            dve.tensor_scalar(gain_q[:], gain_q[:], SCALE, None, ALU.mult).then_inc(gain_scaled, 1)
            dve.sem_inc(norm_ready, 2)

            def prepare(n, s):
                dve.wait_ge(summed, n + 1)
                dve.tensor_scalar(rms[:], rms[:], 1.0 / D, RMS_EPS, ALU.mult, ALU.add).then_inc(mean_ready, 1)
                dve.wait_ge(mean_ready, n + 1)
                dve.reciprocal(rms[:], rms[:]).then_inc(root_asked, 1)
                dve.wait_ge(root_ready, n + 1)
                dve.tensor_scalar(x_norm[:], x_in[s][:], rms[:], None, ALU.mult).then_inc(norm_ready, 1)
                dve.wait_ge(turned, n + 1)
                dve.tensor_tensor(h_tile[s][:], turn_ps[:], gain1[:].unsqueeze(2).broadcast_to([P, KT, P]),
                                  ALU.mult).then_inc(h_ready, 1)

            def finish(n):
                dve.wait_ge(qk_summed, 2 * n + 2)
                dve.tensor_reduce(qk_rms[:], qk_square[:].rearrange("p (g d) -> p g d", d=DH), AX.X, ALU.add).then_inc(qk_step, 1)
                dve.wait_ge(qk_step, 2 * n + 1)
                dve.tensor_scalar(qk_rms[:], qk_rms[:], 1.0 / DH, RMS_EPS, ALU.mult, ALU.add).then_inc(qk_step, 1)
                dve.wait_ge(qk_step, 2 * n + 2)
                dve.reciprocal(qk_rms[:], qk_rms[:]).then_inc(qk_asked, 1)
                dve.wait_ge(qk_root, n + 1)
                dve.tensor_tensor(qk_norm[:].rearrange("p (g d) -> p g d", d=DH),
                                  qk_ps[:].rearrange("p (g d) -> p g d", d=DH),
                                  qk_rms[:].unsqueeze(2).broadcast_to([P, GROUPS, DH]), ALU.mult).then_inc(qk_ready, 1)

            prepare(0, 0)
            with dve.Fori(0, TT // 2 - 1) as pair:
                for s in range(2):
                    prepare(2 * pair + s + 1, 1 - s)
                    finish(2 * pair + s)
            prepare(TT - 1, 1)
            finish(TT - 2)
            finish(TT - 1)

        @block.tensor
        def _(pe):
            pe.wait_ge(made, 2)

            def turn(n):
                pe.wait_ge(norm_ready, 2 + n + 1)
                for k in range(KT):
                    last = pe.transpose(turn_ps[:, k], x_norm[:, k * P:(k + 1) * P], ident[:])
                last.then_inc(turned, 1)

            def project(n, s):
                pe.wait_ge(h_ready, n + 1)
                for j in range(3):
                    out = v_ps[:] if j == 2 else qk_ps[:, DA * j:DA * (j + 1)]
                    for k in range(KT):
                        last = pe.matmul(out, h_tile[s][:, k], w_qkv[:, k, DA * j:DA * (j + 1)],
                                         start=(k == 0), stop=(k == KT - 1))
                last.then_inc(qkv_ready, 1)

            def turn_qk(n):
                pe.wait_ge(qk_ready, n + 1)
                pe.wait_ge(kept, n + 1)
                for b in range(2 * HEADS):
                    last = pe.transpose(qk_turn_ps[:, b], qk_norm[:, b * P:(b + 1) * P], ident[:])
                last.then_inc(qk_turned, 1)

            turn(0)
            pe.wait_ge(w_loaded, 16)
            with pe.Fori(0, TT // 2 - 1) as pair:
                for s in range(2):
                    pe.wait_ge(h_ready, 2 * pair + s + 1)
                    turn(2 * pair + s + 1)
                    project(2 * pair + s, s)
                    turn_qk(2 * pair + s)
            pe.wait_ge(h_ready, TT - 1)
            turn(TT - 1)
            project(TT - 2, 0)
            turn_qk(TT - 2)
            project(TT - 1, 1)
            turn_qk(TT - 1)
            pe.sem_inc(conv_ready, 2)
            pe.wait_ge(h_kept, TT)
            pe.wait_ge(kept, TT + 1)
            with pe.Fori(0, CONV_TILES // 2) as pair:
                for s in range(2):
                    i = 2 * pair + s
                    pe.wait_ge(conv_loaded[s], 16 * (pair + 1))
                    pe.wait_ge(conv_kept, i + 1)
                    for half in range(2):
                        out = conv_ps[s][:, 512 * half:512 * (half + 1)]
                        for k in range(KT):
                            last = pe.matmul(out, w_conv[s][:, k], hT[:, k, 512 * half:512 * (half + 1)],
                                             start=(k == 0), stop=(k == KT - 1))
                    last.then_inc(conv_ready, 1)


def mix_phase(nc, mem, lam_vectors, subln_g, cf_dw, cf_cols, sc_w, qT, kT, values, convT, mixedT):
    STEPS = TT * HEADS
    U_TILE, C_TILE = HEADS, HEADS + CT
    f = lambda name, shape: mem.sb(name, shape, F32)
    ident, ident_b, mask_b = f("ident_m", [P, P]), mem.sb("ident_b", [P, P], BF16), mem.sb("mask_b", [P, P], BF16)
    lam4, lam_sum, lam_exp, lam = f("lam4", [P, 4, DH]), f("lam_sum", [P, 2]), f("lam_exp", [P, 2]), f("lam", [P, 1])
    lam_product = f("lam_product", [P, 2, DH])
    neg_max, total = f("neg_max", [P, 2, 2]), f("total_m", [P, 2, 2])
    inverse, coef = f("inverse", [P, 2, 2]), f("coef", [P, 2])
    prob = [[f(f"prob{s}{c}", [P, SEQ]) for c in range(2)] for s in range(2)]
    probT = [f(f"probT{s}", [P, TT, P]) for s in range(2)]
    heads_out = f("heads_out", [P, TT, DA])
    heads_square = prob[0][0]
    heads_rms = f("heads_rms", [P, STEPS])
    gain_v = f("gain_v", [P, 1])
    glu = f("glu", [P, CT, CF_TAPS - 1 + SEQ])
    gated = f("gated", [P, CT, SC_TAPS - 1 + SEQ])
    taps_f, taps_s = f("taps_f", [P, CT, CF_TAPS]), f("taps_s", [P, CT, SC_TAPS])
    cols = f("cols", [P, CT, 3])
    same_group = f("same_group", [P, P])
    conv = f("conv", [P, CT, SEQ])
    with ExitStack() as ctx:
        sem = lambda name: ctx.enter_context(nc.semaphore(name))
        s_ps = [ctx.enter_context(nc.psum_tensor(f"s_ps{c}", [P, SEQ], F32)) for c in range(2)]
        pt_ps = ctx.enter_context(nc.psum_tensor("pt_ps", [P, TT, P], F32))
        o_ps = [ctx.enter_context(nc.psum_tensor(f"o_ps{s}", [P, 512], F32)) for s in range(2)]
        loaded, made = sem("loaded_m"), sem("made_m")
        lam_asked, lam_exped, lam_ready = sem("lam_asked"), sem("lam_exped"), sem("lam_ready")
        scores_ready, max_ready, probs_ready = sem("scores_ready"), sem("max_ready"), sem("probs_ready")
        chain, mix_ready, probT_ps_ready = sem("chain_m"), sem("mix_ready"), sem("probT_ps_ready")
        probT_ready, o_ready, o_kept = sem("probT_ready"), sem("o_ready"), sem("o_kept")
        gate_ready, glu_ready, c_ready = sem("gate_ready_m"), sem("glu_ready"), sem("c_ready")
        conv_done, mean_ready, centred, squared = sem("conv_done"), sem("mean_ready"), sem("centred"), sem("squared")
        var_ready, ln_asked, ln_root, ln_ready = sem("var_ready"), sem("ln_asked"), sem("ln_root"), sem("ln_ready")
        heads_squared, heads_asked, heads_root, heads_normed = sem("heads_squared"), sem("heads_asked"), sem("heads_root"), sem("heads_normed")
        heads_turned, heads_kept = sem("heads_turned"), sem("heads_kept")
        block = ctx.enter_context(nc.Block())

        @block.sync
        def _(sp):
            for a, b in ((lam4[:], lam_vectors.unsqueeze(0).broadcast_to([P, 4, DH])), (gain_v[:], subln_g), (taps_f[:], cf_dw), (taps_s[:], sc_w),
                         (cols[:], cf_cols)):
                sp.dma_start(a, b).then_inc(loaded, 16)

        @block.gpsimd
        def _(pool):
            pool.memset(ident[:], 0.0).then_inc(made, 1)
            pool.memset(mask_b[:], 0.0).then_inc(made, 1)
            pool.memset(glu[:, :, 0:CF_TAPS - 1], 0.0).then_inc(made, 1)
            pool.memset(gated[:, :, 0:SC_TAPS - 1], 0.0).then_inc(made, 1)
            pool.memset(same_group[:], 0.0).then_inc(made, 1)
            pool.wait_ge(made, 5)
            pool.affine_select(out=ident[:], in_=ident[:], compare_op=ALU.not_equal, fill=1.0, base=0,
                               pattern=[[-1, P]], channel_multiplier=1).then_inc(made, 1)
            pool.affine_select(out=mask_b[:], in_=mask_b[:], compare_op=ALU.is_ge, fill=MASKED, base=0,
                               pattern=[[-1, P]], channel_multiplier=1).then_inc(made, 1)
            for half in range(P // LN_GROUP):
                at = slice(half * LN_GROUP, (half + 1) * LN_GROUP)
                pool.wait_ge(made, 7 + half)
                pool.memset(same_group[at, at], 1.0 / LN_GROUP).then_inc(made, 1)
            pool.wait_ge(made, 7 + P // LN_GROUP)
            pool.tensor_copy(ident_b[:], ident[:]).then_inc(made, 1)

        MADE = 8 + P // LN_GROUP
        width = lambda step: P * (step // HEADS + 1)

        @block.tensor
        def _(pe):
            pe.wait_ge(made, MADE)

            def scores(step):
                i, h, w = step // HEADS, step % HEADS, width(step)
                for c in range(2):
                    if step:
                        pe.wait_ge(probs_ready, 2 * (step - 1) + c + 1)
                    rows = slice(DH * c, DH * (c + 1))
                    for at in range(0, w, 512):
                        n = min(512, w - at)
                        pe.matmul(s_ps[c][:, at:at + n], qT[rows, h, i * P:(i + 1) * P], kT[rows, h, at:at + n],
                                  start=True, stop=(at + n < w))
                    pe.matmul(s_ps[c][:, w - P:w], ident_b[:], mask_b[:], start=False, stop=True).then_inc(scores_ready, 1)

            def turn(step):
                pe.wait_ge(mix_ready, step + 1)
                if step:
                    pe.wait_ge(probT_ready, step)
                for b in range(step // HEADS + 1):
                    last = pe.transpose(pt_ps[:, b], prob[step % 2][0][:, b * P:(b + 1) * P], ident[:])
                last.then_inc(probT_ps_ready, 1)

            def outputs(step):
                i, h = step // HEADS, step % HEADS
                pe.wait_ge(probT_ready, step + 1)
                if step >= 2:
                    pe.wait_ge(o_kept, step - 1)
                for b in range(i + 1):
                    last = pe.matmul(o_ps[step % 2][:, 0:DV], probT[step % 2][:, b], values[:, b, h * DV:(h + 1) * DV],
                                     start=(b == 0), stop=(b == i))
                last.then_inc(o_ready, 1)

            scores(0)
            for step in range(STEPS):
                if step + 1 < STEPS:
                    scores(step + 1)
                turn(step)
                if step:
                    outputs(step - 1)
            outputs(STEPS - 1)
            pe.wait_ge(conv_done, 1)
            for ct in range(CT):
                for half in range(2):
                    at = slice(512 * half, 512 * (half + 1))
                    last = pe.matmul(s_ps[ct][:, at], same_group[:], conv[:, ct, at], start=True, stop=True)
            last.then_inc(mean_ready, 1)
            pe.wait_ge(squared, 1)
            for ct in range(CT):
                for half in range(2):
                    at = slice(512 * half, 512 * (half + 1))
                    last = pe.matmul(s_ps[ct][:, at], same_group[:], glu[:, ct, at], start=True, stop=True)
            last.then_inc(var_ready, 1)
            pe.wait_ge(heads_normed, 1)
            for h in range(HEADS):
                if h:
                    pe.wait_ge(heads_kept, h)
                for i in range(TT):
                    last = pe.transpose(pt_ps[:, i], heads_out[:, i, h * DV:(h + 1) * DV], ident[:])
                last.then_inc(heads_turned, 1)

        @block.scalar
        def _(act):
            act.wait_ge(lam_asked, 1)
            act.activation(lam_exp[:], lam_sum[:], ACT.Exp).then_inc(lam_exped, 1)
            act.activation(convT[:, CT:2 * CT], convT[:, CT:2 * CT], ACT.Sigmoid).then_inc(gate_ready, 1)

            def probT_copy(step):
                act.wait_ge(probT_ps_ready, step + 1)
                if step >= 2:
                    act.wait_ge(o_ready, step - 1)
                n = step // HEADS + 1
                act.activation(probT[step % 2][:, 0:n], pt_ps[:, 0:n], ACT.Copy).then_inc(probT_ready, 1)

            for step in range(STEPS):
                s, w = step % 2, width(step)
                if step >= 2:
                    act.wait_ge(probT_ps_ready, step - 1)
                for c in range(2):
                    act.wait_ge(max_ready, 2 * step + c + 1)
                    act.activation(prob[s][c][:, 0:w], s_ps[c][:, 0:w], ACT.Exp, bias=neg_max[:, s, c:c + 1],
                                   accum_out=total[:, s, c:c + 1]).then_inc(probs_ready, 1)
                if step:
                    probT_copy(step - 1)
            probT_copy(STEPS - 1)
            act.wait_ge(centred, 1)
            act.activation(glu[:, :, 0:SEQ], conv[:], ACT.Square).then_inc(squared, 1)
            act.wait_ge(o_kept, STEPS)
            for i in range(TT):
                if i >= 2:
                    act.wait_ge(chain, 2 * STEPS + i - 1)
                act.activation(prob[i % 2][0][:, 0:DA], heads_out[:, i], ACT.Square).then_inc(heads_squared, 1)
            act.wait_ge(ln_asked, 1)
            act.activation(gated[:, :, 0:SEQ], gated[:, :, 0:SEQ], ACT.Sqrt).then_inc(ln_root, 1)
            act.wait_ge(heads_asked, 1)
            act.activation(heads_rms[:], heads_rms[:], ACT.Sqrt).then_inc(heads_root, 1)
            for h in range(HEADS):
                act.wait_ge(heads_turned, h + 1)
                act.activation(mixedT[:, h], pt_ps[:], ACT.Copy, scale=gain_v[:]).then_inc(heads_kept, 1)
            act.wait_ge(ln_ready, 1)
            for ct in range(CT):
                last = act.activation(mixedT[:, U_TILE + ct], conv[:, ct], ACT.Silu, bias=cols[:, ct, 2:3],
                                      scale=cols[:, ct, 1:2])
            last.then_inc(heads_kept, 1)

        @block.vector
        def _(dve):
            steps_done = [0]

            def then(ins, s=chain):
                steps_done[0] += 1
                ins.then_inc(s, 1)
                dve.wait_ge(s, steps_done[0])

            lam_chain = lam_ready
            dve.wait_ge(loaded, 16 * 5)
            dve.wait_ge(made, MADE)
            then(dve.tensor_tensor(lam_product[:], lam4[:, 0:4:2], lam4[:, 1:4:2], ALU.mult), lam_chain)
            dve.tensor_reduce(lam_sum[:], lam_product[:], AX.X, ALU.add).then_inc(lam_asked, 1)
            dve.wait_ge(lam_exped, 1)
            then(dve.tensor_tensor(lam[:], lam_exp[:, 1:2], lam_exp[:, 0:1], ALU.subtract), lam_chain)
            then(dve.tensor_scalar(lam[:], lam[:], LAM_INIT, None, ALU.subtract), lam_chain)
            then(dve.tensor_scalar(gain_v[:], gain_v[:], 1.0 - LAM_INIT, None, ALU.mult), lam_chain)
            dve.wait_ge(gate_ready, 1)
            dve.tensor_tensor(gated[:, :, SC_TAPS - 1:], convT[:, 3 * CT:4 * CT], convT[:, 4 * CT:5 * CT], ALU.mult)
            then(dve.tensor_tensor(glu[:, :, CF_TAPS - 1:], convT[:, 0:CT], convT[:, CT:2 * CT], ALU.mult), lam_chain)
            steps_done[0] = 0

            def taps():
                short, long = mixedT[:, C_TILE:C_TILE + CT], conv
                for name, source, weights, count, into in (("s", gated, taps_s, SC_TAPS, short), ("f", glu, taps_f, CF_TAPS, long)):
                    for j in range(count):
                        for ct in range(CT):
                            if j == 0:
                                last = dve.tensor_scalar(into[:, ct], source[:, ct, 0:SEQ], weights[:, ct, 0:1],
                                                         cols[:, ct, 0:1] if name == "f" else 0.0, ALU.mult, ALU.add)
                            else:
                                last = dve.scalar_tensor_tensor(into[:, ct], source[:, ct, j:j + SEQ], weights[:, ct, j:j + 1],
                                                                into[:, ct], ALU.mult, ALU.add)
                        yield last
                    if name == "s":
                        yield dve.tensor_tensor(short, short, convT[:, 2 * CT:3 * CT], ALU.mult)

            tap = taps()
            TAPS = SC_TAPS + 1 + CF_TAPS
            taps_done = 0

            def next_tap():
                nonlocal taps_done
                if taps_done < TAPS:
                    if taps_done:
                        dve.wait_ge(c_ready, taps_done)
                    next(tap).then_inc(c_ready, 1)
                    taps_done += 1

            def keep(step):
                i, h = step // HEADS, step % HEADS
                dve.wait_ge(o_ready, step + 1)
                dve.tensor_scalar(heads_out[:, i, h * DV:(h + 1) * DV], o_ps[step % 2][:, 0:DV],
                                  inverse[:, step % 2, 0:1], None, ALU.mult).then_inc(o_kept, 1)

            def maxima(step):
                for c in range(2):
                    dve.wait_ge(scores_ready, 2 * step + c + 1)
                    dve.tensor_reduce(neg_max[:, step % 2, c:c + 1], s_ps[c][:, 0:width(step)], AX.X, ALU.max,
                                      negate=True).then_inc(max_ready, 1)

            maxima(0)
            for step in range(STEPS):
                s, w = step % 2, width(step)
                next_tap()
                if step >= 2:
                    keep(step - 2)
                    dve.wait_ge(o_kept, step - 1)
                dve.wait_ge(probs_ready, 2 * step + 2)
                then(dve.reciprocal(inverse[:, s], total[:, s]))
                then(dve.tensor_scalar(coef[:, s:s + 1], total[:, s, 0:1], inverse[:, s, 1:2], lam[:], ALU.mult, ALU.mult))
                dve.scalar_tensor_tensor(prob[s][0][:, 0:w], prob[s][1][:, 0:w], coef[:, s:s + 1], prob[s][0][:, 0:w],
                                         ALU.mult, ALU.add).then_inc(mix_ready, 1)
                if step + 1 < STEPS:
                    maxima(step + 1)
            keep(STEPS - 2)
            keep(STEPS - 1)
            while taps_done < TAPS:
                next_tap()
            dve.wait_ge(c_ready, TAPS)
            dve.sem_inc(conv_done, 1)
            dve.wait_ge(mean_ready, 1)
            for ct in range(CT):
                last = dve.tensor_tensor(conv[:, ct], conv[:, ct], s_ps[ct][:], ALU.subtract)
            last.then_inc(centred, 1)
            assert steps_done[0] == 2 * STEPS
            for i in range(TT):
                dve.wait_ge(heads_squared, i + 1)
                dve.tensor_reduce(heads_rms[:, HEADS * i:HEADS * (i + 1)],
                                  prob[i % 2][0][:, 0:DA].rearrange("p (h d) -> p h d", d=DV), AX.X, ALU.add).then_inc(chain, 1)
            steps_done[0] += TT
            dve.wait_ge(chain, steps_done[0])
            then(dve.tensor_scalar(heads_rms[:], heads_rms[:], 1.0 / DV, RMS_EPS, ALU.mult, ALU.add))
            dve.reciprocal(heads_rms[:], heads_rms[:]).then_inc(heads_asked, 1)
            dve.wait_ge(var_ready, 1)
            for ct in range(CT):
                last = dve.tensor_scalar(gated[:, ct, 0:SEQ], s_ps[ct][:], LN_EPS, None, ALU.add)
            then(last)
            dve.reciprocal(gated[:, :, 0:SEQ], gated[:, :, 0:SEQ]).then_inc(ln_asked, 1)
            dve.wait_ge(heads_root, 1)
            dve.tensor_tensor(heads_out[:].rearrange("p i (h d) -> p (i h) d", d=DV),
                              heads_out[:].rearrange("p i (h d) -> p (i h) d", d=DV),
                              heads_rms[:].unsqueeze(2).broadcast_to([P, STEPS, DV]), ALU.mult).then_inc(heads_normed, 1)
            dve.wait_ge(ln_root, 1)
            dve.tensor_tensor(conv[:], conv[:], gated[:, :, 0:SEQ], ALU.mult).then_inc(ln_ready, 1)


def output_phase(nc, mem, tiles_mem, x, norm2_g, w_out, mixedT, x_mid, h2_hi, h2_lo):
    RING = 2
    f = lambda name, shape: mem.sb(name, shape, F32)
    t = lambda name, shape: tiles_mem.sb(name, shape, F32)
    w_raw = [f(f"wo_raw{s}", [P, D]) for s in range(2)]
    w_hi, w_lo = mem.sb("wo_hi", [P, KT, D], F32R), mem.sb("wo_lo", [P, KT, D], F32R)
    m_hi = [m.sb(f"m_hi{s}", [P, KT, P], F32R) for s, m in enumerate((mem, tiles_mem))]
    m_lo = [m.sb(f"m_lo{s}", [P, KT, P], F32R) for s, m in enumerate((mem, tiles_mem))]
    x_in = t("x_in_o", [P, D])
    x_sum = t("x_sum", [P, D])
    x_norm = t("x_norm_o", [P, D])
    h_tile = t("h_tile_o", [P, KT, P])
    gain, ident, rms = f("gain2", [P, KT]), f("ident_o", [P, P]), f("rms_o", [P, 1])
    with ExitStack() as ctx:
        sem = lambda name: ctx.enter_context(nc.semaphore(name))
        out_ps = [ctx.enter_context(nc.psum_tensor(f"mixed_ps{s}", [P, D], F32)) for s in range(2)]
        turn_ps = ctx.enter_context(nc.psum_tensor("turn_o_ps", [P, KT, P], F32))
        w_loaded = [sem(f"wo_loaded{s}") for s in range(2)]
        gain_loaded, x_loaded, made, stored = sem("gain_loaded"), sem("x_loaded_o"), sem("made_o"), sem("x_mid_stored")
        w_hi_ready, w_ready, m_hi_ready, m_ready = sem("wo_hi_ready"), sem("wo_ready"), sem("m_hi_ready"), sem("m_ready")
        mixed_ready, sum_ready, squared, asked = sem("mixed_ready"), sem("sum_ready"), sem("squared_o"), sem("asked_o")
        chain, root, norm_ready, turned = sem("chain_o"), sem("root_o"), sem("norm_ready_o"), sem("turned_o")
        h_ready, hi_ready, lo_ready = sem("h_ready_o"), sem("hi_ready"), sem("lo_ready")
        block = ctx.enter_context(nc.Block())

        @block.sync
        def _(sp):
            sp.dma_start(gain[:], norm2_g).then_inc(gain_loaded, 16)
            for k in range(KT):
                if k >= RING:
                    sp.wait_ge(w_ready, k - 1)
                sp.dma_start(w_raw[k % 2][:], w_out[k * P:(k + 1) * P]).then_inc(w_loaded[k % 2], 16)
            sp.sem_inc(stored, 16)
            with sp.Fori(0, TT) as n:
                sp.wait_ge(sum_ready, 1 + n)
                sp.dma_start(x_in[:], x[n]).then_inc(x_loaded, 16)
                sp.wait_ge(sum_ready, 1 + n + 1)
                sp.dma_start(x_mid[n], x_sum[:]).then_inc(stored, 16)
            sp.wait_ge(stored, 16 * (TT + 1))

        @block.gpsimd
        def _(pool):
            pool.memset(ident[:], 0.0).then_inc(made, 1)
            pool.wait_ge(made, 1)
            pool.affine_select(out=ident[:], in_=ident[:], compare_op=ALU.not_equal, fill=1.0, base=0,
                               pattern=[[-1, P]], channel_multiplier=1).then_inc(made, 1)

        @block.scalar
        def _(act):
            for k in range(KT):
                act.wait_ge(w_loaded[k % 2], 16 * (k // 2 + 1))
                act.activation(w_hi[:, k], w_raw[k % 2][:], ACT.Copy).then_inc(w_hi_ready, 1)
            for s in range(2):
                act.activation(m_hi[s][:], mixedT[:, :, P * s:P * (s + 1)], ACT.Copy).then_inc(m_hi_ready, 1)

            def tile(n, s, more=True):
                if more:
                    act.wait_ge(mixed_ready, n + 1)
                    act.activation(m_hi[s][:], mixedT[:, :, bass.ds(P * (n + 2), P)], ACT.Copy).then_inc(m_hi_ready, 1)
                act.wait_ge(sum_ready, 1 + n + 1)
                act.activation(x_norm[:], x_sum[:], ACT.Square, accum_out=rms[:]).then_inc(squared, 1)
                act.wait_ge(asked, n + 1)
                act.activation(rms[:], rms[:], ACT.Sqrt).then_inc(root, 1)
                act.wait_ge(h_ready, n + 1)
                act.activation(h2_hi[:, :, bass.ds(P * n, P)], h_tile[:], ACT.Copy).then_inc(hi_ready, 1)

            with act.Fori(0, TT // 2 - 1) as pair:
                for s in range(2):
                    tile(2 * pair + s, s)
            for s in range(2):
                tile(TT - 2 + s, s, more=False)

        @block.vector
        def _(dve):
            dve.wait_ge(gain_loaded, 16)
            dve.sem_inc(sum_ready, 1)
            for k in range(KT):
                dve.wait_ge(w_hi_ready, k + 1)
                dve.tensor_tensor(w_lo[:, k], w_raw[k % 2][:], w_hi[:, k].bitcast(F32), ALU.subtract).then_inc(w_ready, 1)

            def split_mixed(n, s):
                dve.wait_ge(m_hi_ready, n + 1)
                dve.tensor_tensor(m_lo[s][:], mixedT[:, :, bass.ds(P * n, P)], m_hi[s][:].bitcast(F32),
                                  ALU.subtract).then_inc(m_ready, 1)

            def tile(n, s, more=True):
                dve.wait_ge(mixed_ready, n + 1)
                dve.wait_ge(x_loaded, 16 * (n + 1))
                dve.wait_ge(stored, 16 * (n + 1))
                dve.tensor_tensor(x_sum[:], x_in[:], out_ps[s][:], ALU.add).then_inc(sum_ready, 1)
                if more:
                    split_mixed(n + 2, s)
                dve.wait_ge(squared, n + 1)
                dve.tensor_scalar(rms[:], rms[:], 1.0 / D, RMS_EPS, ALU.mult, ALU.add).then_inc(chain, 1)
                dve.wait_ge(chain, n + 1)
                dve.reciprocal(rms[:], rms[:]).then_inc(asked, 1)
                dve.wait_ge(root, n + 1)
                dve.tensor_scalar(x_norm[:], x_sum[:], rms[:], None, ALU.mult).then_inc(norm_ready, 1)
                dve.wait_ge(turned, n + 1)
                dve.tensor_tensor(h_tile[:], turn_ps[:], gain[:].unsqueeze(2).broadcast_to([P, KT, P]),
                                  ALU.mult).then_inc(h_ready, 1)
                dve.wait_ge(hi_ready, n + 1)
                at = bass.ds(P * n, P)
                dve.tensor_tensor(h2_lo[:, :, at], h_tile[:], h2_hi[:, :, at].bitcast(F32), ALU.subtract).then_inc(lo_ready, 1)
                dve.wait_ge(lo_ready, n + 1)

            for s in range(2):
                split_mixed(s, s)
            with dve.Fori(0, TT // 2 - 1) as pair:
                for s in range(2):
                    tile(2 * pair + s, s)
            for s in range(2):
                tile(TT - 2 + s, s, more=False)

        @block.tensor
        def _(pe):
            pe.wait_ge(made, 2)

            def project(n, s):
                pe.wait_ge(m_ready, n + 1)
                for k in range(KT):
                    for j, (m, w) in enumerate(((m_hi, w_hi), (m_hi, w_lo), (m_lo, w_hi))):
                        for half in range(2):
                            at = slice(512 * half, 512 * (half + 1))
                            last = pe.matmul(out_ps[s][:, at], m[s][:, k], w[:, k, at], start=(k == 0 and j == 0),
                                             stop=(k == KT - 1 and j == 2))
                last.then_inc(mixed_ready, 1)

            def turn(n):
                pe.wait_ge(norm_ready, n + 1)
                for k in range(KT):
                    last = pe.transpose(turn_ps[:, k], x_norm[:, k * P:(k + 1) * P], ident[:])
                last.then_inc(turned, 1)

            pe.wait_ge(w_ready, KT)
            project(0, 0)
            with pe.Fori(0, TT // 2 - 1) as pair:
                for s in range(2):
                    n = 2 * pair + s
                    project(n + 1, 1 - s)
                    turn(n)
            project(TT - 1, 1)
            turn(TT - 2)
            turn(TT - 1)


def keys_phase(nc, mem, h2_hi, h2_lo, peer_wqt, keys_t, top_s, top_i):
    HC = 2 * PH
    RING = 2
    w_raw = [mem.sb(f"wq_raw{s}", [P, KT, P], F32) for s in range(2)]
    w_hi = [mem.sb(f"wq_hi{s}", [P, KT, P], F32R) for s in range(2)]
    w_lo = [mem.sb(f"wq_lo{s}", [P, KT, P], F32R) for s in range(2)]
    query = [mem.sb(f"query{s}", [P, SEQ], F32) for s in range(2)]
    keys = mem.sb("keys", [P, 2, P], F32)
    sub = [mem.sb(f"sub{s}", [P, TT, P], F32) for s in range(2)]
    best = mem.sb("best", [P, TT, TOPK], F32)
    best_at = mem.sb("best_at", [P, TT, TOPK], U32)
    with ExitStack() as ctx:
        sem = lambda name: ctx.enter_context(nc.semaphore(name))
        q_ps = [ctx.enter_context(nc.psum_tensor(f"q_ps{s}", [P, SEQ], F32)) for s in range(2)]
        sub_ps = [ctx.enter_context(nc.psum_tensor(f"sub_ps{s}", [P, TT, P], F32)) for s in range(2)]
        w_loaded = [sem(f"wq_loaded{s}") for s in range(2)]
        keys_loaded = [sem(f"keys_loaded{s}") for s in range(2)]
        w_hi_ready, w_ready, q_ready, query_ready = sem("wq_hi_ready"), sem("wq_ready"), sem("q_ready"), sem("query_ready")
        products_ready, sub_ready = sem("products_ready"), sem("sub_ready")
        picked, taken, replaced = sem("picked"), sem("taken"), sem("replaced")
        passed = sem("passed")
        block = ctx.enter_context(nc.Block())

        @block.sync
        def _(sp):
            with sp.Fori(0, HC // 2) as pair:
                for s in range(2):
                    i = 2 * pair + s
                    sp.wait_ge(w_ready, RING + i - 1)
                    sp.dma_start(w_raw[s][:], peer_wqt[i]).then_inc(w_loaded[s], 16)
                    sp.wait_ge(products_ready, RING + i - 1)
                    sp.dma_start(keys[:, s], keys_t[i]).then_inc(keys_loaded[s], 16)

        @block.tensor
        def _(pe):
            pe.sem_inc(q_ready, RING)
            pe.sem_inc(products_ready, RING)

            def project(i, s):
                pe.wait_ge(w_ready, RING + i + 1)
                pe.wait_ge(query_ready, RING + i - 1)
                for k in range(KT):
                    for n, (w, h) in enumerate(((w_hi, h2_hi), (w_hi, h2_lo), (w_lo, h2_hi))):
                        for half in range(2):
                            last = pe.matmul(q_ps[s][:, half * 512:(half + 1) * 512], w[s][:, k],
                                             h[:, k, half * 512:(half + 1) * 512],
                                             start=(k == 0 and n == 0), stop=(k == KT - 1 and n == 2))
                last.then_inc(q_ready, 1)

            def match(i, s, turn):
                pe.wait_ge(query_ready, RING + i + 1)
                pe.wait_ge(keys_loaded[s], 16 * (turn + 1))
                pe.wait_ge(sub_ready, RING + i - 1)
                for n in range(TT):
                    last = pe.matmul(sub_ps[s][:, n], query[s][:, n * P:(n + 1) * P], keys[:, s],
                                     start=True, stop=True)
                last.then_inc(products_ready, 1)

            project(0, 0)
            with pe.Fori(0, HC // 2 - 1) as pair:
                for s in range(2):
                    project(2 * pair + s + 1, 1 - s)
                    match(2 * pair + s, s, pair)
            project(HC - 1, 1)
            match(HC - 2, 0, HC // 2 - 1)
            match(HC - 1, 1, HC // 2 - 1)

        @block.scalar
        def _(act):
            act.sem_inc(query_ready, RING)
            act.sem_inc(sub_ready, RING)

            def split(i, s, turn):
                act.wait_ge(w_loaded[s], 16 * (turn + 1))
                act.wait_ge(q_ready, RING + i - 1)
                act.activation(w_hi[s][:], w_raw[s][:], ACT.Copy).then_inc(w_hi_ready, 1)

            def copies(i, s, turn=None):
                act.wait_ge(q_ready, RING + i + 1)
                act.wait_ge(products_ready, RING + i - 1)
                act.activation(query[s][:], q_ps[s][:], ACT.Copy).then_inc(query_ready, 1)
                if turn is not None:
                    split(i + 2, s, turn)
                act.wait_ge(products_ready, RING + i + 1)
                act.wait_ge(taken, i + 1)
                act.activation(sub[s][:], sub_ps[s][:], ACT.Copy).then_inc(sub_ready, 1)

            split(0, 0, 0)
            split(1, 1, 0)
            with act.Fori(0, HC // 2 - 1) as pair:
                for s in range(2):
                    copies(2 * pair + s, s, pair + 1)
            copies(HC - 2, 0)
            copies(HC - 1, 1)

        @block.vector
        def _(dve):
            dve.sem_inc(w_ready, RING)
            dve.sem_inc(taken, RING)

            def split(i, s):
                dve.wait_ge(w_hi_ready, i + 1)
                dve.tensor_tensor(w_lo[s][:], w_raw[s][:], w_hi[s][:].bitcast(F32), ALU.subtract).then_inc(w_ready, 1)

            def pick(i, s):
                STEPS = 4
                dve.wait_ge(sub_ready, RING + i + 1)
                dve.sem_inc(passed, 1)
                for half in range(2):
                    eight = slice(8 * half, 8 * half + 8)
                    for n in range(TT):
                        last = dve.max(best[:, n, eight], sub[s][:, n])
                    last.then_inc(picked, 1)
                    dve.wait_ge(picked, STEPS * i + 2 * half + 1)
                    dve.sem_inc(passed, 1)
                    for n in range(TT):
                        last = dve.max_index(best_at[:, n, eight], best[:, n, eight], sub[s][:, n])
                    if half == 0:
                        last.then_inc(picked, 1)
                        dve.wait_ge(picked, STEPS * i + 2)
                        dve.sem_inc(passed, 1)
                        for n in range(TT):
                            last = dve.match_replace(sub[s][:, n], best[:, n, eight], sub[s][:, n], TAKEN)
                        last.then_inc(replaced, 1)
                        dve.wait_ge(replaced, i + 1)
                        dve.sem_inc(passed, 1)
                    else:
                        last.then_inc(picked, 1)
                        dve.wait_ge(picked, STEPS * i + 4)
                dve.tensor_copy(top_s[:, :, i], best[:])
                dve.tensor_copy(top_i[:, :, i], best_at[:]).then_inc(taken, 1)
                dve.wait_ge(taken, RING + i + 1)

            split(0, 0)
            split(1, 1)
            with dve.Fori(0, HC // 2 - 1) as pair:
                for s in range(2):
                    split(2 * pair + s + 2, s)
                    pick(2 * pair + s, s)
            pick(HC - 2, 0)
            pick(HC - 1, 1)


def gates_phase(nc, mem, top_s, top_i, gates):
    CH = PH * TOPK
    BATCH = 8
    PER_TILE = P // BATCH
    RING = 4
    iota = mem.sb("iota", [P, P], F32)
    iota_i = mem.sb("iota_i", [P, P], I32)
    ident = mem.sb("ident", [P, P], F32)
    index = mem.sb("index", [P, 2, PH, TOPK], F32)
    cand = mem.sb("cand", [P, PH, TOPK * TOPK], F32)
    sel_s = mem.sb("sel_s", [P, PH, TOPK], F32)
    sel_at = mem.sb("sel_at", [P, PH, TOPK], U32)
    sel_ab = mem.sb("sel_ab", [P, 2, CH], U32)
    ab = mem.sb("ab", [P, 2, CH], F32)
    pick_of = mem.sb("pick_of", [P, CH, TOPK], F32)
    chosen = mem.sb("chosen", [P, 3, CH], F32)
    total = mem.sb("total", [P, PH], F32)
    per_choice = [mem.sb(f"per_choice{s}", [P, 3, P], F32) for s in range(2)]
    is_1 = [mem.sb(f"is_1{s}", [P, BATCH, P], BF16) for s in range(RING)]
    hot_1 = [mem.sb(f"hot_1{s}", [P, BATCH, P], F32) for s in range(RING)]
    hot_2 = [mem.sb(f"hot_2{s}", [P, BATCH, P], F32) for s in range(RING)]
    stage = [mem.sb(f"stage{s}", [P, P, GB], F32) for s in range(2)]
    with ExitStack() as ctx:
        sem = lambda name: ctx.enter_context(nc.semaphore(name))
        turn_ps = ctx.enter_context(nc.psum_tensor("turn_ps", [P, 3, P], F32))
        gate_ps = [ctx.enter_context(nc.psum_tensor(f"gate_ps{s}", [P, BATCH, P], F32)) for s in range(2)]
        made, chain = sem("made"), sem("chain")
        passed = sem("passed_g")
        chosen_ready, turned, per_choice_ready = sem("chosen_ready"), sem("turned"), sem("per_choice_ready")
        exp_asked, exp_ready = sem("exp_asked"), sem("exp_ready")
        cand_ready, cand_free = sem("cand_ready"), sem("cand_free")
        is_ready, hot_2_ready = sem("is_ready"), sem("hot_2_ready")
        hot_ready, gate_ready, gate_copied = sem("hot_ready"), sem("gate_ready"), sem("gate_copied")
        stored = [sem(f"gates_stored{s}") for s in range(2)]
        block = ctx.enter_context(nc.Block())

        @block.gpsimd
        def _(pool):
            pool.iota(iota_i[:], pattern=[[1, P]], base=0, channel_multiplier=0).then_inc(made, 1)
            pool.memset(ident[:], 0.0).then_inc(made, 1)
            pool.wait_ge(made, 2)
            pool.tensor_copy(iota[:], iota_i[:]).then_inc(made, 1)
            pool.affine_select(out=ident[:], in_=ident[:], compare_op=ALU.not_equal, fill=1.0, base=0,
                               pattern=[[-1, P]], channel_multiplier=1).then_inc(made, 1)
            pool.wait_ge(made, 4)
            pool.sem_inc(hot_ready, RING)

            def sums(n):
                pool.wait_ge(cand_free, n + 1)
                pair = top_s[:, n].rearrange("p (h c) k -> p h c k", c=2)
                for h in range(PH):
                    last = pool.tensor_tensor(cand[:, h].rearrange("p (a b) -> p a b", a=TOPK),
                                              pair[:, h, 0].unsqueeze(2).broadcast_to([P, TOPK, TOPK]),
                                              pair[:, h, 1].unsqueeze(1).broadcast_to([P, TOPK, TOPK]), ALU.add)
                last.then_inc(cand_ready, 1)

            def weigh(n, m, b, s):
                q = PER_TILE * n + b
                pool.wait_ge(is_ready, q + 1)
                pool.wait_ge(gate_ready, q + 1)
                pool.tensor_tensor(hot_1[s][:], is_1[s][:],
                                   per_choice[m][:, 2, bass.ds(BATCH * b, BATCH)].unsqueeze(2).broadcast_to([P, BATCH, P]),
                                   ALU.mult).then_inc(hot_ready, 1)

            def weigh_tile(n, m):
                with pool.Fori(0, PER_TILE // RING) as turn:
                    for s in range(RING):
                        weigh(n, m, RING * turn + s, s)

            sums(0)
            with pool.Fori(0, TT // 2 - 1) as half:
                for m in range(2):
                    sums(2 * half + m + 1)
                    weigh_tile(2 * half + m, m)
            sums(TT - 1)
            weigh_tile(TT - 2, 0)
            weigh_tile(TT - 1, 1)

        @block.vector
        def _(dve):
            CHAIN = 18
            dve.wait_ge(made, 4)

            def select(n):
                steps = [0]

                def then(ins):
                    steps[0] += 1
                    ins.then_inc(chain, 1)
                    dve.wait_ge(chain, CHAIN * n + steps[0])
                    dve.sem_inc(passed, 1)

                then(dve.tensor_copy(index[:].rearrange("p c h k -> p h c k"),
                                     top_i[:, n].rearrange("p (h c) k -> p h c k", c=2)))
                dve.wait_ge(cand_ready, n + 1)
                dve.sem_inc(passed, 1)
                for half in range(2):
                    eight = slice(8 * half, 8 * half + 8)
                    for h in range(PH):
                        last = dve.max(sel_s[:, h, eight], cand[:, h])
                    then(last)
                    for h in range(PH):
                        last = dve.max_index(sel_at[:, h, eight], sel_s[:, h, eight], cand[:, h])
                    then(last)
                    if half == 0:
                        for h in range(PH):
                            last = dve.match_replace(cand[:, h], sel_s[:, h, eight], cand[:, h], TAKEN)
                        then(last)
                dve.sem_inc(cand_free, 1)
                flat = sel_at[:].rearrange("p h k -> p (h k)")
                dve.tensor_scalar(sel_ab[:, 0], flat, 4, None, ALU.logical_shift_right)
                then(dve.tensor_scalar(sel_ab[:, 1], flat, TOPK - 1, None, ALU.bitwise_and))
                then(dve.tensor_copy(ab[:], sel_ab[:]))
                dve.wait_ge(turned, n + 1)
                for side in range(2):
                    rank = ab[:, side].unsqueeze(2).broadcast_to([P, CH, TOPK])
                    ranks = iota[:, 0:TOPK].unsqueeze(1).broadcast_to([P, CH, TOPK])
                    then(dve.tensor_tensor(pick_of[:], rank, ranks, ALU.is_equal))
                    hk = pick_of[:].rearrange("p (h k) j -> p h k j", h=PH)
                    for h in range(PH):
                        last = dve.tensor_tensor(hk[:, h], hk[:, h],
                                                 index[:, side, h].unsqueeze(1).broadcast_to([P, TOPK, TOPK]),
                                                 ALU.mult)
                    then(last)
                    then(dve.tensor_reduce(chosen[:, side], pick_of[:], AX.X, ALU.add))
                gate = chosen[:, 2].rearrange("p (h k) -> p h k", h=PH)
                dve.tensor_tensor(gate, sel_s[:], sel_s[:, :, 0:1].broadcast_to([P, PH, TOPK]),
                                  ALU.subtract).then_inc(exp_asked, 1)
                dve.wait_ge(exp_ready, n + 1)
                then(dve.tensor_reduce(total[:], gate, AX.X, ALU.add))
                then(dve.reciprocal(total[:], total[:]))
                dve.tensor_tensor(gate, gate, total[:].unsqueeze(2).broadcast_to([P, PH, TOPK]),
                                  ALU.mult).then_inc(chosen_ready, 1)
                assert steps[0] <= CHAIN
                if steps[0] < CHAIN:
                    dve.sem_inc(chain, CHAIN - steps[0])

            def one_hots(n, m, b, s):
                q = PER_TILE * n + b
                dve.wait_ge(gate_ready, q + 1)
                dve.wait_ge(hot_ready, q + 1)
                keys = iota[:].unsqueeze(1).broadcast_to([P, BATCH, P])
                key = lambda side: per_choice[m][:, side, bass.ds(BATCH * b, BATCH)].unsqueeze(2).broadcast_to([P, BATCH, P])
                dve.tensor_tensor(is_1[s][:], keys, key(0), ALU.is_equal).then_inc(is_ready, 1)
                dve.tensor_tensor(hot_2[s][:], keys, key(1), ALU.is_equal).then_inc(hot_2_ready, 1)

            def one_hots_tile(n, m):
                dve.wait_ge(per_choice_ready, 1 + n + 1)
                dve.sem_inc(passed, 1)
                with dve.Fori(0, PER_TILE // RING) as turn:
                    for s in range(RING):
                        one_hots(n, m, RING * turn + s, s)

            dve.sem_inc(cand_free, 1)
            select(0)
            with dve.Fori(0, TT // 2 - 1) as half:
                for m in range(2):
                    select(2 * half + m + 1)
                    one_hots_tile(2 * half + m, m)
            select(TT - 1)
            one_hots_tile(TT - 2, 0)
            one_hots_tile(TT - 1, 1)

        @block.tensor
        def _(pe):
            pe.wait_ge(made, 4)
            pe.sem_inc(turned, 1)
            pe.sem_inc(gate_ready, RING)

            def turn(n):
                pe.wait_ge(chosen_ready, n + 1)
                pe.wait_ge(per_choice_ready, n + 1)
                for k in range(3):
                    last = pe.transpose(turn_ps[:, k], chosen[:, k], ident[:])
                last.then_inc(turned, 1)

            def products(n):
                with pe.Fori(0, PER_TILE // RING) as round_:
                    for s in range(RING):
                        q = PER_TILE * n + RING * round_ + s
                        pe.wait_ge(hot_2_ready, q + 1)
                        pe.wait_ge(hot_ready, RING + q + 1)
                        pe.wait_ge(gate_copied, 2 + q - 1)
                        for t in range(BATCH):
                            last = pe.matmul(gate_ps[s % 2][:, t], hot_2[s][:, t], hot_1[s][:, t], start=True, stop=True)
                        last.then_inc(gate_ready, 1)

            turn(0)
            with pe.Fori(0, TT - 1) as n:
                turn(n + 1)
                products(n)
            products(TT - 1)

        @block.scalar
        def _(act):
            act.sem_inc(gate_copied, 2)
            gate = chosen[:, 2]

            def softmax_and_turn(n, m):
                act.wait_ge(exp_asked, n + 1)
                act.activation(gate, gate, ACT.Exp).then_inc(exp_ready, 1)
                act.wait_ge(turned, n + 2)
                act.activation(per_choice[m][:], turn_ps[:], ACT.Copy).then_inc(per_choice_ready, 1)

            def copies(n):
                for part in range(2):
                    act.wait_ge(stored[part], 16 * (n + 1))
                    with act.Fori(0, GB // BATCH // 2) as pair:
                        for s in range(2):
                            b = 2 * pair + s
                            q = PER_TILE * n + (GB // BATCH) * part + b
                            act.wait_ge(gate_ready, RING + q + 1)
                            act.activation(stage[part][:, :, bass.ds(BATCH * b, BATCH)].rearrange("p k t -> p t k"),
                                           gate_ps[s][:], ACT.Copy).then_inc(gate_copied, 1)

            act.sem_inc(per_choice_ready, 1)
            softmax_and_turn(0, 0)
            with act.Fori(0, TT // 2 - 1) as half:
                for m in range(2):
                    softmax_and_turn(2 * half + m + 1, 1 - m)
                    copies(2 * half + m)
            softmax_and_turn(TT - 1, 1)
            copies(TT - 2)
            copies(TT - 1)

        @block.sync
        def _(sp):
            for s in range(2):
                sp.sem_inc(stored[s], 16)
            with sp.Fori(0, TT) as n:
                for s in range(2):
                    sp.wait_ge(gate_copied, 2 + PER_TILE * n + (GB // BATCH) * (s + 1))
                    sp.dma_start(gates[2 * n + s], stage[s][:]).then_inc(stored[s], 16)
            for s in range(2):
                sp.wait_ge(stored[s], 16 * (TT + 1))


def dense_phase(nc, mem, h2_hi, h2_lo, peer_ut, peer_v, gates, x_mid, out):
    E = 4
    GROUPS = N_KEYS // E
    HALVES = SEQ // 512
    BANKS = 4
    RING = 2
    OUTS = TT * (D // 512)

    u_raw = mem.sb("u_raw", [P, 2, KT, P], F32)
    u_hi = [mem.sb(f"u_hi{s}", [P, KT, P], F32R) for s in range(2)]
    u_lo = [mem.sb(f"u_lo{s}", [P, KT, P], F32R) for s in range(2)]
    v_raw = mem.sb("v_raw", [P, 2, D], F32)
    v_hi = mem.sb("v_hi", [P, E, D], F32R)
    v_lo = mem.sb("v_lo", [P, E, D], F32R)
    gate = mem.sb("gate", [P, 2, SEQ], F32)
    weight = mem.sb("weight", [P, 2, SEQ], F32)
    w_hi = mem.sb("w_hi", [P, E, SEQ], F32R)
    w_lo = mem.sb("w_lo", [P, E, SEQ], F32R)
    acc = mem.sb("acc", [P, TT, D], F32)

    with ExitStack() as ctx:
        sem = lambda name: ctx.enter_context(nc.semaphore(name))
        z_ps = [ctx.enter_context(nc.psum_tensor(f"z_ps{s}", [P, SEQ], F32)) for s in range(2)]
        out_ps = [ctx.enter_context(nc.psum_tensor(f"out_ps{b}", [P, 512], F32)) for b in range(BANKS)]
        u_loaded = [sem(f"u_loaded{s}") for s in range(2)]
        v_loaded = [sem(f"v_loaded{s}") for s in range(2)]
        gate_loaded = [sem(f"gate_loaded{s}") for s in range(2)]
        acc_loaded = sem("acc_loaded")
        u_hi_ready, u_ready = sem("u_hi_ready"), sem("u_ready")
        v_hi_ready, v_ready = sem("v_hi_ready"), sem("v_ready")
        z_ready = sem("z_ready")
        gelu_ready, weight_ready = sem("gelu_ready"), sem("weight_ready")
        w_hi_ready, w_ready = sem("w_hi_ready"), sem("w_ready")
        out_ready, out_free, out_stored = sem("out_ready"), sem("out_free"), sem("out_stored")
        block = ctx.enter_context(nc.Block())

        @block.sync
        def _(sp):
            sp.dma_start(acc[:], x_mid.rearrange("n p d -> p n d")).then_inc(acc_loaded, 16)
            with sp.Fori(0, N_KEYS // 2) as pair:
                for s in range(2):
                    e = 2 * pair + s
                    sp.wait_ge(u_ready, RING + e - 1)
                    sp.dma_start(u_raw[:, s], peer_ut[e]).then_inc(u_loaded[s], 16)
                    sp.wait_ge(weight_ready, RING + e - 1)
                    sp.dma_start(gate[:, s].rearrange("p (b t) -> p b t", t=GB),
                                 gates[:, :, e].rearrange("b p t -> p b t")).then_inc(gate_loaded[s], 16)
                    sp.wait_ge(v_ready, RING + e - 1)
                    sp.dma_start(v_raw[:, s], peer_v[e]).then_inc(v_loaded[s], 16)
            for n in range(TT):
                sp.wait_ge(out_free, BANKS + OUTS * (GROUPS - 1) + 2 * (n + 1))
                sp.dma_start(out[n * P:(n + 1) * P], acc[:, n]).then_inc(out_stored, 16)
            sp.wait_ge(out_stored, 16 * TT)

        @block.scalar
        def _(act):
            act.sem_inc(gelu_ready, RING)

            def split_u(e, s, turn):
                act.wait_ge(u_loaded[s], 16 * (turn + 1))
                act.wait_ge(z_ready, RING + e - 1)
                act.activation(u_hi[s][:], u_raw[:, s], ACT.Copy).then_inc(u_hi_ready, 1)

            def step(g, j, more=True):
                e, s = E * g + j, j % 2
                turn = (E // 2) * g + j // 2
                if more:
                    split_u(e + 1, 1 - s, (E // 2) * g + (j + 1) // 2)
                act.wait_ge(z_ready, RING + e + 1)
                act.wait_ge(w_ready, RING + e - 1)
                act.activation(weight[:, s], z_ps[s][:], ACT.Gelu).then_inc(gelu_ready, 1)
                act.wait_ge(v_loaded[s], 16 * (turn + 1))
                act.wait_ge(out_ready, OUTS * (g + 1))
                act.activation(v_hi[:, j], v_raw[:, s], ACT.Copy).then_inc(v_hi_ready, 1)
                act.wait_ge(weight_ready, RING + e + 1)
                act.activation(w_hi[:, j], weight[:, s], ACT.Copy).then_inc(w_hi_ready, 1)

            split_u(0, 0, 0)
            step(0, 0)
            with act.Fori(0, GROUPS - 1) as g:
                for j in range(1, E):
                    step(g, j)
                step(g + 1, 0)
            for j in range(1, E):
                step(GROUPS - 1, j, more=j < E - 1)

        @block.vector
        def _(dve):
            dve.sem_inc(out_free, BANKS)
            for ready in (u_ready, v_ready, weight_ready, w_ready):
                dve.sem_inc(ready, RING)
            dve.wait_ge(acc_loaded, 16)

            def split_u(e, s):
                dve.wait_ge(u_hi_ready, e + 1)
                dve.tensor_tensor(u_lo[s][:], u_raw[:, s], u_hi[s][:].bitcast(F32), ALU.subtract).then_inc(u_ready, 1)

            def step(g, j, more=True, add_group=None):
                e, s = E * g + j, j % 2
                turn = (E // 2) * g + j // 2
                if more:
                    split_u(e + 1, 1 - s)
                dve.wait_ge(gelu_ready, RING + e + 1)
                dve.wait_ge(gate_loaded[s], 16 * (turn + 1))
                dve.tensor_tensor(weight[:, s], weight[:, s], gate[:, s], ALU.mult).then_inc(weight_ready, 1)
                if add_group is not None:
                    add_outputs(add_group)
                dve.wait_ge(v_hi_ready, e + 1)
                dve.tensor_tensor(v_lo[:, j], v_raw[:, s], v_hi[:, j].bitcast(F32), ALU.subtract).then_inc(v_ready, 1)
                dve.wait_ge(w_hi_ready, e + 1)
                dve.tensor_tensor(w_lo[:, j], weight[:, s], w_hi[:, j].bitcast(F32), ALU.subtract).then_inc(w_ready, 1)

            def add_outputs(g):
                for o in range(OUTS):
                    dve.wait_ge(out_ready, OUTS * (g + 1) + o + 1)
                    part = acc[:, o // 2, (o % 2) * 512:(o % 2 + 1) * 512]
                    dve.tensor_tensor(part, part, out_ps[o % BANKS][:], ALU.add).then_inc(out_free, 1)

            split_u(0, 0)
            step(0, 0)
            with dve.Fori(0, GROUPS - 1) as g:
                for j in range(1, E):
                    step(g, j)
                step(g + 1, 0, add_group=g)
            for j in range(1, E):
                step(GROUPS - 1, j, more=j < E - 1)
            add_outputs(GROUPS - 1)

        @block.tensor
        def _(pe):
            pe.sem_inc(z_ready, RING)
            pe.sem_inc(out_ready, OUTS)

            def project_u(e, s):
                pe.wait_ge(u_ready, RING + e + 1)
                pe.wait_ge(gelu_ready, RING + e - 1)
                for k in range(KT):
                    for n, (u, h) in enumerate(((u_hi, h2_hi), (u_hi, h2_lo), (u_lo, h2_hi))):
                        for half in range(HALVES):
                            last = pe.matmul(z_ps[s][:, half * 512:(half + 1) * 512], u[s][:, k],
                                             h[:, k, half * 512:(half + 1) * 512],
                                             start=(k == 0 and n == 0), stop=(k == KT - 1 and n == 2))
                last.then_inc(z_ready, 1)

            def project_v(g):
                pe.wait_ge(w_ready, RING + E * (g + 1))
                pe.wait_ge(v_ready, RING + E * (g + 1))
                for o in range(OUTS):
                    n, half = o // 2, o % 2
                    pe.wait_ge(out_free, OUTS * g + o + 1)
                    for j in range(E):
                        for m, (w, v) in enumerate(((w_hi, v_hi), (w_hi, v_lo), (w_lo, v_hi))):
                            last = pe.matmul(out_ps[o % BANKS][:], w[:, j, n * P:(n + 1) * P],
                                             v[:, j, half * 512:(half + 1) * 512],
                                             start=(j == 0 and m == 0), stop=(j == E - 1 and m == 2))
                    last.then_inc(out_ready, 1)

            project_u(0, 0)
            with pe.Fori(0, GROUPS - 1) as g:
                for j in range(1, E + 1):
                    project_u(E * g + j, j % 2)
                project_v(g)
            for j in range(1, E):
                project_u(E * (GROUPS - 1) + j, j % 2)
            project_v(GROUPS - 1)
def build(nc, a, out):
    start, end = 8320, nc.sbuf_usable_end
    KB = 1024
    x_mid = nc.dram_tensor("x_mid", (TT, P, D), F32, kind="Internal").ap()
    gates = nc.dram_tensor("gates", (SEQ // GB, P, N_KEYS, GB), F32, kind="Internal").ap()
    x = a["x"].rearrange("b (n p) d -> (b n) p d", p=P)

    kept = Memory(nc, start, start + 88 * KB)
    qT = kept.sb("qT", [P, HEADS, SEQ], F32)
    kT = kept.sb("kT", [P, HEADS, SEQ], F32)
    values = kept.sb("values", [P, TT, DA], F32)
    convT = kept.sb("convT", [P, 5 * CT, SEQ], F32)
    project_phase(nc, Memory(nc, kept.at, end), x, a["norm1_g"], a["w_in"], a["q_norm_g"], a["k_norm_g"],
                  qT, kT, values, convT)

    mixed = Memory(nc, kept.at, end)
    mixedT = mixed.sb("mixedT", [P, KT, SEQ], F32)
    mix_phase(nc, mixed, a["lam_vectors"], a["subln_g"], a["cf_dw"], a["cf_cols"], a["sc_w"],
              qT, kT, values, convT, mixedT)

    h2 = Memory(nc, start, start + 64 * KB)
    h2_hi = h2.sb("h2_hi", [P, KT, SEQ], F32R)
    h2_lo = h2.sb("h2_lo", [P, KT, SEQ], F32R)
    output_phase(nc, Memory(nc, kept.at + 32 * KB, end), Memory(nc, h2.at, kept.at), x, a["norm2_g"], a["w_out"], mixedT, x_mid, h2_hi, h2_lo)

    tops = Memory(nc, h2.at, end)
    top_s = tops.sb("top_s", [P, TT, 2 * PH, TOPK], F32)
    top_i = tops.sb("top_i", [P, TT, 2 * PH, TOPK], F32)
    keys_phase(nc, Memory(nc, tops.at, end), h2_hi, h2_lo, a["peer_wqt"], a["keys_t"], top_s, top_i)
    gates_phase(nc, Memory(nc, tops.at, end), top_s, top_i, gates)
    dense_phase(nc, Memory(nc, h2.at, end), h2_hi, h2_lo, a["peer_ut"], a["peer_v"], gates, x_mid, out)


def kernel(x, norm1_g, w_in, q_norm_g, k_norm_g, lam_q1, lam_k1, lam_q2, lam_k2, subln_g,
           cf_dw, cf_dw_b, cf_ln_g, cf_ln_b, sc_w, w_out, norm2_g,
           peer_wq, peer_keys, peer_u, peer_v):
    import concourse.bacc as bacc
    from concourse.bass_utils import run_bass_kernel_spmd

    def by_partition(v):
        return v.reshape(-1, P).T

    arrays = {
        "x": x,
        "norm1_g": by_partition(norm1_g[0]),
        "w_in": w_in[0],
        "q_norm_g": q_norm_g[0].reshape(DH, 1),
        "k_norm_g": k_norm_g[0].reshape(DH, 1),
        "lam_vectors": np.stack([lam_q1[0], lam_k1[0], lam_q2[0], lam_k2[0]]),
        "subln_g": subln_g[0].reshape(DV, 1),
        "cf_dw": cf_dw[0].reshape(CF_TAPS, CT, P).transpose(2, 1, 0),
        "cf_cols": np.stack([by_partition(v[0]) for v in (cf_dw_b, cf_ln_g, cf_ln_b)], axis=-1),
        "sc_w": sc_w[0].reshape(SC_TAPS, CT, P).transpose(2, 1, 0),
        "w_out": w_out[0],
        "norm2_g": by_partition(norm2_g[0]),
        "peer_wqt": peer_wq[0].reshape(KT, P, 2 * PH, P).transpose(2, 1, 0, 3),
        "keys_t": peer_keys[0].reshape(2 * PH, N_KEYS, P).transpose(0, 2, 1),
        "peer_ut": peer_u[0].reshape(N_KEYS, N_KEYS, KT, P).transpose(0, 3, 2, 1),
        "peer_v": peer_v[0].reshape(N_KEYS, N_KEYS, D),
    }
    arrays = {name: np.ascontiguousarray(v) for name, v in arrays.items()}
    nc = bacc.Bacc("TRN2", target_bir_lowering=False, num_devices=1, dynamic_dma_scratch_size=8192)
    args = {name: nc.dram_tensor(f"in_{name}", v.shape, mybir.dt.from_np(v.dtype), kind="ExternalInput").ap()
            for name, v in arrays.items()}
    out = nc.dram_tensor("out", (1, SEQ, D), F32, kind="ExternalOutput").ap()
    build(nc, args, out.rearrange("b s d -> (b s) d"))
    result = run_bass_kernel_spmd(nc, [{f"in_{name}": v for name, v in arrays.items()}], core_ids=[0])
    return result.results[0]["out"]
```

```python
from collections import namedtuple
from contextlib import ExitStack

import numpy as np

import concourse.bass as bass
from concourse import mybir
from concourse.alu_op_type import AluOpType as ALU

ACT = mybir.ActivationFunctionType
AX = mybir.AxisListType
F32, F32R, BF16 = mybir.dt.float32, mybir.dt.float32r, mybir.dt.bfloat16
I32, U32, U16 = mybir.dt.int32, mybir.dt.uint32, mybir.dt.uint16

P = 128
SEQ = 1024
D = 1024
TT = SEQ // P
KT = D // P
HEADS = 4
DH = 64
DV = 2 * DH
DA = HEADS * DV
CONV = 256
CT = CONV // P
CF_TAPS = 31
SC_TAPS = 3
LN_GROUP = 64
N_KEYS = 128
PH = 8
TOPK = 16
RMS_EPS = 1e-6
LN_EPS = 1e-5
LAM_INIT = 0.8 - 0.6 * 1.0
MASKED = -1e30
TAKEN = -3.0e38
E = 4
GROUPS = N_KEYS // E
GB = 64
DMA_SCRATCH = 1024
SBUF_START = DMA_SCRATCH + 128


class Memory:

    def __init__(self, nc, start, end):
        self.nc, self.at, self.end = nc, start, end

    def sb(self, name, shape, dtype):
        size = int(np.prod(shape[1:])) * (2 if dtype in (BF16, U16) else 4)
        tensor = self.nc.alloc_sbuf_tensor_at(name, shape, dtype, offset=self.at)
        self.at += -(-size // 32) * 32
        assert self.at <= self.end, (name, self.at, self.end)
        return tensor


def project_phase(nc, mem, x, norm1_g, w_in, q_norm_g, k_norm_g, qT, kT, values, convT):
    QKV = 3 * DA
    GROUPS = 2 * DA // DH
    CONV_TILES = convT.shape[1]
    w_qkv = mem.sb("w_qkv", [P, KT, QKV], F32)
    w_conv = [mem.sb(f"w_conv{s}", [P, KT, P], F32) for s in range(2)]
    gain1 = mem.sb("gain1", [P, KT], F32)
    gain_q, gain_k = mem.sb("gain_q", [P, 1], F32), mem.sb("gain_k", [P, 1], F32)
    ident = mem.sb("ident_a", [P, P], F32)
    x_in = [mem.sb(f"x_in{s}", [P, D], F32) for s in range(2)]
    x_norm = mem.sb("x_norm", [P, D], F32)
    square = mem.sb("square", [P, D], F32)
    rms = mem.sb("rms", [P, 1], F32)
    hT = mem.sb("hT", [P, KT, SEQ], F32)
    h_tile = [mem.sb(f"h_tile{s}", [P, KT, P], F32) for s in range(2)]
    qk_norm = mem.sb("qk_norm", [P, 2 * DA], F32)
    qk_square = mem.sb("qk_square", [P, 2 * DA], F32)
    qk_rms = mem.sb("qk_rms", [P, GROUPS], F32)
    with ExitStack() as ctx:
        sem = lambda name: ctx.enter_context(nc.semaphore(name))
        turn_ps = ctx.enter_context(nc.psum_tensor("h_turn_ps", [P, KT, P], F32))
        qk_ps = ctx.enter_context(nc.psum_tensor("qk_ps", [P, 2 * DA], F32))
        v_ps = ctx.enter_context(nc.psum_tensor("v_ps", [P, DA], F32))
        qk_turn_ps = ctx.enter_context(nc.psum_tensor("qk_turn_ps", [P, 2 * HEADS, P], F32))
        x_loaded = [sem(f"x_loaded{s}") for s in range(2)]
        w_loaded, small_loaded = sem("w_loaded"), sem("small_loaded")
        conv_loaded = [sem(f"conv_loaded{s}") for s in range(2)]
        made, gain_scaled, mean_ready = sem("made_a"), sem("gain_scaled"), sem("mean_ready_a")
        qk_step = sem("qk_step")
        conv_ps = (qk_ps[:], turn_ps[:].rearrange("p k t -> p (k t)"))
        summed, root_asked, root_ready = sem("summed"), sem("root_asked"), sem("root_ready")
        norm_ready, turned, h_ready, h_kept = sem("norm_ready"), sem("turned_a"), sem("h_ready"), sem("h_kept")
        qkv_ready, qk_summed = sem("qkv_ready"), sem("qk_summed")
        qk_asked, qk_root, qk_ready, qk_turned = sem("qk_asked"), sem("qk_root"), sem("qk_ready"), sem("qk_turned")
        kept, conv_ready, conv_kept = sem("kept"), sem("conv_ready"), sem("conv_kept")
        block = ctx.enter_context(nc.Block())

        @block.sync
        def _(sp):
            for half in range(2):
                sp.dma_start(gain_q[DH * half:DH * (half + 1), :], q_norm_g).then_inc(small_loaded, 16)
                sp.dma_start(gain_k[DH * half:DH * (half + 1), :], k_norm_g).then_inc(small_loaded, 16)
            sp.dma_start(gain1[:], norm1_g).then_inc(small_loaded, 16)
            with sp.Fori(0, TT // 2) as pair:
                for s in range(2):
                    sp.wait_ge(norm_ready, 2 * pair + s + 1)
                    sp.dma_start(x_in[s][:], x[2 * pair + s]).then_inc(x_loaded[s], 16)
            with sp.Fori(0, CONV_TILES // 2) as pair:
                for s in range(2):
                    i = 2 * pair + s
                    sp.wait_ge(conv_ready, i + 1)
                    sp.dma_start(w_conv[s][:], w_in[:, bass.ds(QKV + P * i, P)].rearrange("(k p) n -> p k n", p=P))\
                      .then_inc(conv_loaded[s], 16)

        @block.gpsimd
        def _(pool):
            pool.memset(ident[:], 0.0).then_inc(made, 1)
            pool.wait_ge(made, 1)
            pool.affine_select(out=ident[:], in_=ident[:], compare_op=ALU.not_equal, fill=1.0, base=0,
                               pattern=[[-1, P]], channel_multiplier=1).then_inc(made, 1)

        @block.scalar
        def _(act):
            act.dma_start(w_qkv[:], w_in[:, 0:QKV].rearrange("(k p) n -> p k n", p=P)).then_inc(w_loaded, 16)

            def prepare(n, s, turn):
                act.wait_ge(x_loaded[s], 16 * (turn + 1))
                act.activation(square[:], x_in[s][:], ACT.Square, accum_out=rms[:]).then_inc(summed, 1)
                act.wait_ge(root_asked, n + 1)
                act.activation(rms[:], rms[:], ACT.Sqrt).then_inc(root_ready, 1)
                act.wait_ge(h_ready, n + 1)
                act.activation(hT[:, :, bass.ds(P * n, P)], h_tile[s][:], ACT.Copy).then_inc(h_kept, 1)

            def finish(n):
                act.wait_ge(qkv_ready, n + 1)
                act.activation(qk_square[:], qk_ps[:], ACT.Square).then_inc(qk_summed, 1)
                act.activation(values[:, n], v_ps[:], ACT.Copy).then_inc(qk_summed, 1)
                act.wait_ge(qk_asked, n + 1)
                act.activation(qk_rms[:], qk_rms[:], ACT.Sqrt).then_inc(qk_root, 1)
                act.wait_ge(qk_turned, n + 1)
                at = bass.ds(P * n, P)
                act.activation(qT[:, :, at], qk_turn_ps[:, 0:HEADS], ACT.Copy, scale=gain_q[:])
                act.activation(kT[:, :, at], qk_turn_ps[:, HEADS:], ACT.Copy, scale=gain_k[:]).then_inc(kept, 1)

            act.sem_inc(kept, 1)
            act.wait_ge(small_loaded, 80)
            act.wait_ge(gain_scaled, 1)
            prepare(0, 0, 0)
            with act.Fori(0, TT // 2 - 1) as pair:
                for s in range(2):
                    prepare(2 * pair + s + 1, 1 - s, pair + s)
                    finish(2 * pair + s)
            prepare(TT - 1, 1, TT // 2 - 1)
            finish(TT - 2)
            finish(TT - 1)
            act.sem_inc(conv_kept, 2)
            with act.Fori(0, CONV_TILES // 2) as pair:
                for s in range(2):
                    act.wait_ge(conv_ready, 2 + 2 * pair + s + 1)
                    act.activation(convT[:, 2 * pair + s], conv_ps[s], ACT.Copy).then_inc(conv_kept, 1)

        @block.vector
        def _(dve):
            SCALE = float(DH) ** -0.5
            dve.wait_ge(small_loaded, 80)
            dve.tensor_scalar(gain_q[:], gain_q[:], SCALE, None, ALU.mult).then_inc(gain_scaled, 1)
            dve.sem_inc(norm_ready, 2)

            def prepare(n, s):
                dve.wait_ge(summed, n + 1)
                dve.tensor_scalar(rms[:], rms[:], 1.0 / D, RMS_EPS, ALU.mult, ALU.add).then_inc(mean_ready, 1)
                dve.wait_ge(mean_ready, n + 1)
                dve.reciprocal(rms[:], rms[:]).then_inc(root_asked, 1)
                dve.wait_ge(root_ready, n + 1)
                dve.tensor_scalar(x_norm[:], x_in[s][:], rms[:], None, ALU.mult).then_inc(norm_ready, 1)
                dve.wait_ge(turned, n + 1)
                dve.tensor_tensor(h_tile[s][:], turn_ps[:], gain1[:].unsqueeze(2).broadcast_to([P, KT, P]),
                                  ALU.mult).then_inc(h_ready, 1)

            def finish(n):
                dve.wait_ge(qk_summed, 2 * n + 2)
                dve.tensor_reduce(qk_rms[:], qk_square[:].rearrange("p (g d) -> p g d", d=DH), AX.X, ALU.add).then_inc(qk_step, 1)
                dve.wait_ge(qk_step, 2 * n + 1)
                dve.tensor_scalar(qk_rms[:], qk_rms[:], 1.0 / DH, RMS_EPS, ALU.mult, ALU.add).then_inc(qk_step, 1)
                dve.wait_ge(qk_step, 2 * n + 2)
                dve.reciprocal(qk_rms[:], qk_rms[:]).then_inc(qk_asked, 1)
                dve.wait_ge(qk_root, n + 1)
                dve.tensor_tensor(qk_norm[:].rearrange("p (g d) -> p g d", d=DH),
                                  qk_ps[:].rearrange("p (g d) -> p g d", d=DH),
                                  qk_rms[:].unsqueeze(2).broadcast_to([P, GROUPS, DH]), ALU.mult).then_inc(qk_ready, 1)

            prepare(0, 0)
            with dve.Fori(0, TT // 2 - 1) as pair:
                for s in range(2):
                    prepare(2 * pair + s + 1, 1 - s)
                    finish(2 * pair + s)
            prepare(TT - 1, 1)
            finish(TT - 2)
            finish(TT - 1)

        @block.tensor
        def _(pe):
            pe.wait_ge(made, 2)

            def turn(n):
                pe.wait_ge(norm_ready, 2 + n + 1)
                for k in range(KT):
                    last = pe.transpose(turn_ps[:, k], x_norm[:, k * P:(k + 1) * P], ident[:])
                last.then_inc(turned, 1)

            def project(n, s):
                pe.wait_ge(h_ready, n + 1)
                for j in range(3):
                    out = v_ps[:] if j == 2 else qk_ps[:, DA * j:DA * (j + 1)]
                    for k in range(KT):
                        last = pe.matmul(out, h_tile[s][:, k], w_qkv[:, k, DA * j:DA * (j + 1)],
                                         start=(k == 0), stop=(k == KT - 1))
                last.then_inc(qkv_ready, 1)

            def turn_qk(n):
                pe.wait_ge(qk_ready, n + 1)
                pe.wait_ge(kept, n + 1)
                for b in range(2 * HEADS):
                    last = pe.transpose(qk_turn_ps[:, b], qk_norm[:, b * P:(b + 1) * P], ident[:])
                last.then_inc(qk_turned, 1)

            turn(0)
            pe.wait_ge(w_loaded, 16)
            with pe.Fori(0, TT // 2 - 1) as pair:
                for s in range(2):
                    pe.wait_ge(h_ready, 2 * pair + s + 1)
                    turn(2 * pair + s + 1)
                    project(2 * pair + s, s)
                    turn_qk(2 * pair + s)
            pe.wait_ge(h_ready, TT - 1)
            turn(TT - 1)
            project(TT - 2, 0)
            turn_qk(TT - 2)
            project(TT - 1, 1)
            turn_qk(TT - 1)
            pe.sem_inc(conv_ready, 2)
            pe.wait_ge(h_kept, TT)
            pe.wait_ge(kept, TT + 1)
            with pe.Fori(0, CONV_TILES // 2) as pair:
                for s in range(2):
                    i = 2 * pair + s
                    pe.wait_ge(conv_loaded[s], 16 * (pair + 1))
                    pe.wait_ge(conv_kept, i + 1)
                    for half in range(2):
                        out = conv_ps[s][:, 512 * half:512 * (half + 1)]
                        for k in range(KT):
                            last = pe.matmul(out, w_conv[s][:, k], hT[:, k, 512 * half:512 * (half + 1)],
                                             start=(k == 0), stop=(k == KT - 1))
                    last.then_inc(conv_ready, 1)


def mix_phase(nc, mem, lam_vectors, subln_g, cf_dw, cf_cols, sc_w, qT, kT, values, convT, mixedT):
    STEPS = TT * HEADS
    U_TILE, C_TILE = HEADS, HEADS + CT
    f = lambda name, shape: mem.sb(name, shape, F32)
    ident, ident_b, mask_b = f("ident_m", [P, P]), mem.sb("ident_b", [P, P], BF16), mem.sb("mask_b", [P, P], BF16)
    lam4, lam_sum, lam_exp, lam = f("lam4", [P, 4, DH]), f("lam_sum", [P, 2]), f("lam_exp", [P, 2]), f("lam", [P, 1])
    lam_product = f("lam_product", [P, 2, DH])
    neg_max, total = f("neg_max", [P, 2, 2]), f("total_m", [P, 2, 2])
    inverse, coef = f("inverse", [P, 2, 2]), f("coef", [P, 2])
    prob = [[f(f"prob{s}{c}", [P, SEQ]) for c in range(2)] for s in range(2)]
    probT = [f(f"probT{s}", [P, TT, P]) for s in range(2)]
    heads_out = f("heads_out", [P, TT, DA])
    heads_square = prob[0][0]
    heads_rms = f("heads_rms", [P, STEPS])
    gain_v = f("gain_v", [P, 1])
    glu = f("glu", [P, CT, CF_TAPS - 1 + SEQ])
    gated = f("gated", [P, CT, SC_TAPS - 1 + SEQ])
    taps_f, taps_s = f("taps_f", [P, CT, CF_TAPS]), f("taps_s", [P, CT, SC_TAPS])
    cols = f("cols", [P, CT, 3])
    same_group = f("same_group", [P, P])
    conv = f("conv", [P, CT, SEQ])
    with ExitStack() as ctx:
        sem = lambda name: ctx.enter_context(nc.semaphore(name))
        s_ps = [ctx.enter_context(nc.psum_tensor(f"s_ps{c}", [P, SEQ], F32)) for c in range(2)]
        pt_ps = ctx.enter_context(nc.psum_tensor("pt_ps", [P, TT, P], F32))
        o_ps = [ctx.enter_context(nc.psum_tensor(f"o_ps{s}", [P, 512], F32)) for s in range(2)]
        loaded, made = sem("loaded_m"), sem("made_m")
        lam_asked, lam_exped, lam_ready = sem("lam_asked"), sem("lam_exped"), sem("lam_ready")
        scores_ready, max_ready, probs_ready = sem("scores_ready"), sem("max_ready"), sem("probs_ready")
        chain, mix_ready, probT_ps_ready = sem("chain_m"), sem("mix_ready"), sem("probT_ps_ready")
        probT_ready, o_ready, o_kept = sem("probT_ready"), sem("o_ready"), sem("o_kept")
        gate_ready, glu_ready, c_ready = sem("gate_ready_m"), sem("glu_ready"), sem("c_ready")
        conv_done, mean_ready, centred, squared = sem("conv_done"), sem("mean_ready"), sem("centred"), sem("squared")
        var_ready, ln_asked, ln_root, ln_ready = sem("var_ready"), sem("ln_asked"), sem("ln_root"), sem("ln_ready")
        heads_squared, heads_asked, heads_root, heads_normed = sem("heads_squared"), sem("heads_asked"), sem("heads_root"), sem("heads_normed")
        heads_turned, heads_kept = sem("heads_turned"), sem("heads_kept")
        block = ctx.enter_context(nc.Block())

        @block.sync
        def _(sp):
            for a, b in ((lam4[:], lam_vectors.unsqueeze(0).broadcast_to([P, 4, DH])), (gain_v[:], subln_g), (taps_f[:], cf_dw), (taps_s[:], sc_w),
                         (cols[:], cf_cols)):
                sp.dma_start(a, b).then_inc(loaded, 16)

        @block.gpsimd
        def _(pool):
            pool.memset(ident[:], 0.0).then_inc(made, 1)
            pool.memset(mask_b[:], 0.0).then_inc(made, 1)
            pool.memset(glu[:, :, 0:CF_TAPS - 1], 0.0).then_inc(made, 1)
            pool.memset(gated[:, :, 0:SC_TAPS - 1], 0.0).then_inc(made, 1)
            pool.memset(same_group[:], 0.0).then_inc(made, 1)
            pool.wait_ge(made, 5)
            pool.affine_select(out=ident[:], in_=ident[:], compare_op=ALU.not_equal, fill=1.0, base=0,
                               pattern=[[-1, P]], channel_multiplier=1).then_inc(made, 1)
            pool.affine_select(out=mask_b[:], in_=mask_b[:], compare_op=ALU.is_ge, fill=MASKED, base=0,
                               pattern=[[-1, P]], channel_multiplier=1).then_inc(made, 1)
            for half in range(P // LN_GROUP):
                at = slice(half * LN_GROUP, (half + 1) * LN_GROUP)
                pool.wait_ge(made, 7 + half)
                pool.memset(same_group[at, at], 1.0 / LN_GROUP).then_inc(made, 1)
            pool.wait_ge(made, 7 + P // LN_GROUP)
            pool.tensor_copy(ident_b[:], ident[:]).then_inc(made, 1)

        MADE = 8 + P // LN_GROUP
        width = lambda step: P * (step // HEADS + 1)

        @block.tensor
        def _(pe):
            pe.wait_ge(made, MADE)

            def scores(step):
                i, h, w = step // HEADS, step % HEADS, width(step)
                for c in range(2):
                    if step:
                        pe.wait_ge(probs_ready, 2 * (step - 1) + c + 1)
                    rows = slice(DH * c, DH * (c + 1))
                    for at in range(0, w, 512):
                        n = min(512, w - at)
                        pe.matmul(s_ps[c][:, at:at + n], qT[rows, h, i * P:(i + 1) * P], kT[rows, h, at:at + n],
                                  start=True, stop=(at + n < w))
                    pe.matmul(s_ps[c][:, w - P:w], ident_b[:], mask_b[:], start=False, stop=True).then_inc(scores_ready, 1)

            def turn(step):
                pe.wait_ge(mix_ready, step + 1)
                if step:
                    pe.wait_ge(probT_ready, step)
                for b in range(step // HEADS + 1):
                    last = pe.transpose(pt_ps[:, b], prob[step % 2][0][:, b * P:(b + 1) * P], ident[:])
                last.then_inc(probT_ps_ready, 1)

            def outputs(step):
                i, h = step // HEADS, step % HEADS
                pe.wait_ge(probT_ready, step + 1)
                if step >= 2:
                    pe.wait_ge(o_kept, step - 1)
                for b in range(i + 1):
                    last = pe.matmul(o_ps[step % 2][:, 0:DV], probT[step % 2][:, b], values[:, b, h * DV:(h + 1) * DV],
                                     start=(b == 0), stop=(b == i))
                last.then_inc(o_ready, 1)

            scores(0)
            for step in range(STEPS):
                if step + 1 < STEPS:
                    scores(step + 1)
                turn(step)
                if step:
                    outputs(step - 1)
            outputs(STEPS - 1)
            pe.wait_ge(conv_done, 1)
            for ct in range(CT):
                for half in range(2):
                    at = slice(512 * half, 512 * (half + 1))
                    last = pe.matmul(s_ps[ct][:, at], same_group[:], conv[:, ct, at], start=True, stop=True)
            last.then_inc(mean_ready, 1)
            pe.wait_ge(squared, 1)
            for ct in range(CT):
                for half in range(2):
                    at = slice(512 * half, 512 * (half + 1))
                    last = pe.matmul(s_ps[ct][:, at], same_group[:], glu[:, ct, at], start=True, stop=True)
            last.then_inc(var_ready, 1)
            pe.wait_ge(heads_normed, 1)
            for h in range(HEADS):
                if h:
                    pe.wait_ge(heads_kept, h)
                for i in range(TT):
                    last = pe.transpose(pt_ps[:, i], heads_out[:, i, h * DV:(h + 1) * DV], ident[:])
                last.then_inc(heads_turned, 1)

        @block.scalar
        def _(act):
            act.wait_ge(lam_asked, 1)
            act.activation(lam_exp[:], lam_sum[:], ACT.Exp).then_inc(lam_exped, 1)
            act.activation(convT[:, CT:2 * CT], convT[:, CT:2 * CT], ACT.Sigmoid).then_inc(gate_ready, 1)

            def probT_copy(step):
                act.wait_ge(probT_ps_ready, step + 1)
                if step >= 2:
                    act.wait_ge(o_ready, step - 1)
                n = step // HEADS + 1
                act.activation(probT[step % 2][:, 0:n], pt_ps[:, 0:n], ACT.Copy).then_inc(probT_ready, 1)

            for step in range(STEPS):
                s, w = step % 2, width(step)
                if step >= 2:
                    act.wait_ge(probT_ps_ready, step - 1)
                for c in range(2):
                    act.wait_ge(max_ready, 2 * step + c + 1)
                    act.activation(prob[s][c][:, 0:w], s_ps[c][:, 0:w], ACT.Exp, bias=neg_max[:, s, c:c + 1],
                                   accum_out=total[:, s, c:c + 1]).then_inc(probs_ready, 1)
                if step:
                    probT_copy(step - 1)
            probT_copy(STEPS - 1)
            act.wait_ge(centred, 1)
            act.activation(glu[:, :, 0:SEQ], conv[:], ACT.Square).then_inc(squared, 1)
            act.wait_ge(o_kept, STEPS)
            for i in range(TT):
                if i >= 2:
                    act.wait_ge(chain, 2 * STEPS + i - 1)
                act.activation(prob[i % 2][0][:, 0:DA], heads_out[:, i], ACT.Square).then_inc(heads_squared, 1)
            act.wait_ge(ln_asked, 1)
            act.activation(gated[:, :, 0:SEQ], gated[:, :, 0:SEQ], ACT.Sqrt).then_inc(ln_root, 1)
            act.wait_ge(heads_asked, 1)
            act.activation(heads_rms[:], heads_rms[:], ACT.Sqrt).then_inc(heads_root, 1)
            for h in range(HEADS):
                act.wait_ge(heads_turned, h + 1)
                act.activation(mixedT[:, h], pt_ps[:], ACT.Copy, scale=gain_v[:]).then_inc(heads_kept, 1)
            act.wait_ge(ln_ready, 1)
            for ct in range(CT):
                last = act.activation(mixedT[:, U_TILE + ct], conv[:, ct], ACT.Silu, bias=cols[:, ct, 2:3],
                                      scale=cols[:, ct, 1:2])
            last.then_inc(heads_kept, 1)

        @block.vector
        def _(dve):
            steps_done = [0]

            def then(ins, s=chain):
                steps_done[0] += 1
                ins.then_inc(s, 1)
                dve.wait_ge(s, steps_done[0])

            lam_chain = lam_ready
            dve.wait_ge(loaded, 16 * 5)
            dve.wait_ge(made, MADE)
            then(dve.tensor_tensor(lam_product[:], lam4[:, 0:4:2], lam4[:, 1:4:2], ALU.mult), lam_chain)
            dve.tensor_reduce(lam_sum[:], lam_product[:], AX.X, ALU.add).then_inc(lam_asked, 1)
            dve.wait_ge(lam_exped, 1)
            then(dve.tensor_tensor(lam[:], lam_exp[:, 1:2], lam_exp[:, 0:1], ALU.subtract), lam_chain)
            then(dve.tensor_scalar(lam[:], lam[:], LAM_INIT, None, ALU.subtract), lam_chain)
            then(dve.tensor_scalar(gain_v[:], gain_v[:], 1.0 - LAM_INIT, None, ALU.mult), lam_chain)
            dve.wait_ge(gate_ready, 1)
            dve.tensor_tensor(gated[:, :, SC_TAPS - 1:], convT[:, 3 * CT:4 * CT], convT[:, 4 * CT:5 * CT], ALU.mult)
            then(dve.tensor_tensor(glu[:, :, CF_TAPS - 1:], convT[:, 0:CT], convT[:, CT:2 * CT], ALU.mult), lam_chain)
            steps_done[0] = 0

            def taps():
                short, long = mixedT[:, C_TILE:C_TILE + CT], conv
                for name, source, weights, count, into in (("s", gated, taps_s, SC_TAPS, short), ("f", glu, taps_f, CF_TAPS, long)):
                    for j in range(count):
                        for ct in range(CT):
                            if j == 0:
                                last = dve.tensor_scalar(into[:, ct], source[:, ct, 0:SEQ], weights[:, ct, 0:1],
                                                         cols[:, ct, 0:1] if name == "f" else 0.0, ALU.mult, ALU.add)
                            else:
                                last = dve.scalar_tensor_tensor(into[:, ct], source[:, ct, j:j + SEQ], weights[:, ct, j:j + 1],
                                                                into[:, ct], ALU.mult, ALU.add)
                        yield last
                    if name == "s":
                        yield dve.tensor_tensor(short, short, convT[:, 2 * CT:3 * CT], ALU.mult)

            tap = taps()
            TAPS = SC_TAPS + 1 + CF_TAPS
            taps_done = 0

            def next_tap():
                nonlocal taps_done
                if taps_done < TAPS:
                    if taps_done:
                        dve.wait_ge(c_ready, taps_done)
                    next(tap).then_inc(c_ready, 1)
                    taps_done += 1

            def keep(step):
                i, h = step // HEADS, step % HEADS
                dve.wait_ge(o_ready, step + 1)
                dve.tensor_scalar(heads_out[:, i, h * DV:(h + 1) * DV], o_ps[step % 2][:, 0:DV],
                                  inverse[:, step % 2, 0:1], None, ALU.mult).then_inc(o_kept, 1)

            def maxima(step):
                for c in range(2):
                    dve.wait_ge(scores_ready, 2 * step + c + 1)
                    dve.tensor_reduce(neg_max[:, step % 2, c:c + 1], s_ps[c][:, 0:width(step)], AX.X, ALU.max,
                                      negate=True).then_inc(max_ready, 1)

            maxima(0)
            for step in range(STEPS):
                s, w = step % 2, width(step)
                next_tap()
                if step >= 2:
                    keep(step - 2)
                    dve.wait_ge(o_kept, step - 1)
                dve.wait_ge(probs_ready, 2 * step + 2)
                then(dve.reciprocal(inverse[:, s], total[:, s]))
                then(dve.tensor_scalar(coef[:, s:s + 1], total[:, s, 0:1], inverse[:, s, 1:2], lam[:], ALU.mult, ALU.mult))
                dve.scalar_tensor_tensor(prob[s][0][:, 0:w], prob[s][1][:, 0:w], coef[:, s:s + 1], prob[s][0][:, 0:w],
                                         ALU.mult, ALU.add).then_inc(mix_ready, 1)
                if step + 1 < STEPS:
                    maxima(step + 1)
            keep(STEPS - 2)
            keep(STEPS - 1)
            while taps_done < TAPS:
                next_tap()
            dve.wait_ge(c_ready, TAPS)
            dve.sem_inc(conv_done, 1)
            dve.wait_ge(mean_ready, 1)
            for ct in range(CT):
                last = dve.tensor_tensor(conv[:, ct], conv[:, ct], s_ps[ct][:], ALU.subtract)
            last.then_inc(centred, 1)
            assert steps_done[0] == 2 * STEPS
            for i in range(TT):
                dve.wait_ge(heads_squared, i + 1)
                dve.tensor_reduce(heads_rms[:, HEADS * i:HEADS * (i + 1)],
                                  prob[i % 2][0][:, 0:DA].rearrange("p (h d) -> p h d", d=DV), AX.X, ALU.add).then_inc(chain, 1)
            steps_done[0] += TT
            dve.wait_ge(chain, steps_done[0])
            then(dve.tensor_scalar(heads_rms[:], heads_rms[:], 1.0 / DV, RMS_EPS, ALU.mult, ALU.add))
            dve.reciprocal(heads_rms[:], heads_rms[:]).then_inc(heads_asked, 1)
            dve.wait_ge(var_ready, 1)
            for ct in range(CT):
                last = dve.tensor_scalar(gated[:, ct, 0:SEQ], s_ps[ct][:], LN_EPS, None, ALU.add)
            then(last)
            dve.reciprocal(gated[:, :, 0:SEQ], gated[:, :, 0:SEQ]).then_inc(ln_asked, 1)
            dve.wait_ge(heads_root, 1)
            dve.tensor_tensor(heads_out[:].rearrange("p i (h d) -> p (i h) d", d=DV),
                              heads_out[:].rearrange("p i (h d) -> p (i h) d", d=DV),
                              heads_rms[:].unsqueeze(2).broadcast_to([P, STEPS, DV]), ALU.mult).then_inc(heads_normed, 1)
            dve.wait_ge(ln_root, 1)
            dve.tensor_tensor(conv[:], conv[:], gated[:, :, 0:SEQ], ALU.mult).then_inc(ln_ready, 1)


def output_phase(nc, mem, tiles_mem, x, norm2_g, w_out, mixedT, x_mid, h2_hi, h2_lo):
    RING = 2
    f = lambda name, shape: mem.sb(name, shape, F32)
    t = lambda name, shape: tiles_mem.sb(name, shape, F32)
    w_raw = [f(f"wo_raw{s}", [P, D]) for s in range(2)]
    w_hi, w_lo = mem.sb("wo_hi", [P, KT, D], F32R), mem.sb("wo_lo", [P, KT, D], F32R)
    m_hi = [m.sb(f"m_hi{s}", [P, KT, P], F32R) for s, m in enumerate((mem, tiles_mem))]
    m_lo = [m.sb(f"m_lo{s}", [P, KT, P], F32R) for s, m in enumerate((mem, tiles_mem))]
    x_in = t("x_in_o", [P, D])
    x_sum = t("x_sum", [P, D])
    x_norm = t("x_norm_o", [P, D])
    h_tile = t("h_tile_o", [P, KT, P])
    gain, ident, rms = f("gain2", [P, KT]), f("ident_o", [P, P]), f("rms_o", [P, 1])
    with ExitStack() as ctx:
        sem = lambda name: ctx.enter_context(nc.semaphore(name))
        out_ps = [ctx.enter_context(nc.psum_tensor(f"mixed_ps{s}", [P, D], F32)) for s in range(2)]
        turn_ps = ctx.enter_context(nc.psum_tensor("turn_o_ps", [P, KT, P], F32))
        w_loaded = [sem(f"wo_loaded{s}") for s in range(2)]
        gain_loaded, x_loaded, made, stored = sem("gain_loaded"), sem("x_loaded_o"), sem("made_o"), sem("x_mid_stored")
        w_hi_ready, w_ready, m_hi_ready, m_ready = sem("wo_hi_ready"), sem("wo_ready"), sem("m_hi_ready"), sem("m_ready")
        mixed_ready, sum_ready, squared, asked = sem("mixed_ready"), sem("sum_ready"), sem("squared_o"), sem("asked_o")
        chain, root, norm_ready, turned = sem("chain_o"), sem("root_o"), sem("norm_ready_o"), sem("turned_o")
        h_ready, hi_ready, lo_ready = sem("h_ready_o"), sem("hi_ready"), sem("lo_ready")
        block = ctx.enter_context(nc.Block())

        @block.sync
        def _(sp):
            sp.dma_start(gain[:], norm2_g).then_inc(gain_loaded, 16)
            for k in range(KT):
                if k >= RING:
                    sp.wait_ge(w_ready, k - 1)
                sp.dma_start(w_raw[k % 2][:], w_out[k * P:(k + 1) * P]).then_inc(w_loaded[k % 2], 16)
            sp.sem_inc(stored, 16)
            with sp.Fori(0, TT) as n:
                sp.wait_ge(sum_ready, 1 + n)
                sp.dma_start(x_in[:], x[n]).then_inc(x_loaded, 16)
                sp.wait_ge(sum_ready, 1 + n + 1)
                sp.dma_start(x_mid[n], x_sum[:]).then_inc(stored, 16)
            sp.wait_ge(stored, 16 * (TT + 1))

        @block.gpsimd
        def _(pool):
            pool.memset(ident[:], 0.0).then_inc(made, 1)
            pool.wait_ge(made, 1)
            pool.affine_select(out=ident[:], in_=ident[:], compare_op=ALU.not_equal, fill=1.0, base=0,
                               pattern=[[-1, P]], channel_multiplier=1).then_inc(made, 1)

        @block.scalar
        def _(act):
            for k in range(KT):
                act.wait_ge(w_loaded[k % 2], 16 * (k // 2 + 1))
                act.activation(w_hi[:, k], w_raw[k % 2][:], ACT.Copy).then_inc(w_hi_ready, 1)
            for s in range(2):
                act.activation(m_hi[s][:], mixedT[:, :, P * s:P * (s + 1)], ACT.Copy).then_inc(m_hi_ready, 1)

            def tile(n, s, more=True):
                if more:
                    act.wait_ge(mixed_ready, n + 1)
                    act.activation(m_hi[s][:], mixedT[:, :, bass.ds(P * (n + 2), P)], ACT.Copy).then_inc(m_hi_ready, 1)
                act.wait_ge(sum_ready, 1 + n + 1)
                act.activation(x_norm[:], x_sum[:], ACT.Square, accum_out=rms[:]).then_inc(squared, 1)
                act.wait_ge(asked, n + 1)
                act.activation(rms[:], rms[:], ACT.Sqrt).then_inc(root, 1)
                act.wait_ge(h_ready, n + 1)
                act.activation(h2_hi[:, :, bass.ds(P * n, P)], h_tile[:], ACT.Copy).then_inc(hi_ready, 1)

            with act.Fori(0, TT // 2 - 1) as pair:
                for s in range(2):
                    tile(2 * pair + s, s)
            for s in range(2):
                tile(TT - 2 + s, s, more=False)

        @block.vector
        def _(dve):
            dve.wait_ge(gain_loaded, 16)
            dve.sem_inc(sum_ready, 1)
            for k in range(KT):
                dve.wait_ge(w_hi_ready, k + 1)
                dve.tensor_tensor(w_lo[:, k], w_raw[k % 2][:], w_hi[:, k].bitcast(F32), ALU.subtract).then_inc(w_ready, 1)

            def split_mixed(n, s):
                dve.wait_ge(m_hi_ready, n + 1)
                dve.tensor_tensor(m_lo[s][:], mixedT[:, :, bass.ds(P * n, P)], m_hi[s][:].bitcast(F32),
                                  ALU.subtract).then_inc(m_ready, 1)

            def tile(n, s, more=True):
                dve.wait_ge(mixed_ready, n + 1)
                dve.wait_ge(x_loaded, 16 * (n + 1))
                dve.wait_ge(stored, 16 * (n + 1))
                dve.tensor_tensor(x_sum[:], x_in[:], out_ps[s][:], ALU.add).then_inc(sum_ready, 1)
                if more:
                    split_mixed(n + 2, s)
                dve.wait_ge(squared, n + 1)
                dve.tensor_scalar(rms[:], rms[:], 1.0 / D, RMS_EPS, ALU.mult, ALU.add).then_inc(chain, 1)
                dve.wait_ge(chain, n + 1)
                dve.reciprocal(rms[:], rms[:]).then_inc(asked, 1)
                dve.wait_ge(root, n + 1)
                dve.tensor_scalar(x_norm[:], x_sum[:], rms[:], None, ALU.mult).then_inc(norm_ready, 1)
                dve.wait_ge(turned, n + 1)
                dve.tensor_tensor(h_tile[:], turn_ps[:], gain[:].unsqueeze(2).broadcast_to([P, KT, P]),
                                  ALU.mult).then_inc(h_ready, 1)
                dve.wait_ge(hi_ready, n + 1)
                at = bass.ds(P * n, P)
                dve.tensor_tensor(h2_lo[:, :, at], h_tile[:], h2_hi[:, :, at].bitcast(F32), ALU.subtract).then_inc(lo_ready, 1)
                dve.wait_ge(lo_ready, n + 1)

            for s in range(2):
                split_mixed(s, s)
            with dve.Fori(0, TT // 2 - 1) as pair:
                for s in range(2):
                    tile(2 * pair + s, s)
            for s in range(2):
                tile(TT - 2 + s, s, more=False)

        @block.tensor
        def _(pe):
            pe.wait_ge(made, 2)

            def project(n, s):
                pe.wait_ge(m_ready, n + 1)
                for k in range(KT):
                    for j, (m, w) in enumerate(((m_hi, w_hi), (m_hi, w_lo), (m_lo, w_hi))):
                        for half in range(2):
                            at = slice(512 * half, 512 * (half + 1))
                            last = pe.matmul(out_ps[s][:, at], m[s][:, k], w[:, k, at], start=(k == 0 and j == 0),
                                             stop=(k == KT - 1 and j == 2))
                last.then_inc(mixed_ready, 1)

            def turn(n):
                pe.wait_ge(norm_ready, n + 1)
                for k in range(KT):
                    last = pe.transpose(turn_ps[:, k], x_norm[:, k * P:(k + 1) * P], ident[:])
                last.then_inc(turned, 1)

            pe.wait_ge(w_ready, KT)
            project(0, 0)
            with pe.Fori(0, TT // 2 - 1) as pair:
                for s in range(2):
                    n = 2 * pair + s
                    project(n + 1, 1 - s)
                    turn(n)
            project(TT - 1, 1)
            turn(TT - 2)
            turn(TT - 1)


def keys_phase(nc, mem, h2_hi, h2_lo, peer_wqt, keys_t, top_s, top_i):
    HC = 2 * PH
    RING = 2
    w_raw = [mem.sb(f"wq_raw{s}", [P, KT, P], F32) for s in range(2)]
    w_hi = [mem.sb(f"wq_hi{s}", [P, KT, P], F32R) for s in range(2)]
    w_lo = [mem.sb(f"wq_lo{s}", [P, KT, P], F32R) for s in range(2)]
    query = [mem.sb(f"query{s}", [P, SEQ], F32) for s in range(2)]
    keys = mem.sb("keys", [P, 2, P], F32)
    sub = [mem.sb(f"sub{s}", [P, TT, P], F32) for s in range(2)]
    best = mem.sb("best", [P, TT, TOPK], F32)
    best_at = mem.sb("best_at", [P, TT, TOPK], U32)
    with ExitStack() as ctx:
        sem = lambda name: ctx.enter_context(nc.semaphore(name))
        q_ps = [ctx.enter_context(nc.psum_tensor(f"q_ps{s}", [P, SEQ], F32)) for s in range(2)]
        sub_ps = [ctx.enter_context(nc.psum_tensor(f"sub_ps{s}", [P, TT, P], F32)) for s in range(2)]
        w_loaded = [sem(f"wq_loaded{s}") for s in range(2)]
        keys_loaded = [sem(f"keys_loaded{s}") for s in range(2)]
        w_hi_ready, w_ready, q_ready, query_ready = sem("wq_hi_ready"), sem("wq_ready"), sem("q_ready"), sem("query_ready")
        products_ready, sub_ready = sem("products_ready"), sem("sub_ready")
        picked, taken, replaced = sem("picked"), sem("taken"), sem("replaced")
        passed = sem("passed")
        block = ctx.enter_context(nc.Block())

        @block.sync
        def _(sp):
            with sp.Fori(0, HC // 2) as pair:
                for s in range(2):
                    i = 2 * pair + s
                    sp.wait_ge(w_ready, RING + i - 1)
                    sp.dma_start(w_raw[s][:], peer_wqt[i]).then_inc(w_loaded[s], 16)
                    sp.wait_ge(products_ready, RING + i - 1)
                    sp.dma_start(keys[:, s], keys_t[i]).then_inc(keys_loaded[s], 16)

        @block.tensor
        def _(pe):
            pe.sem_inc(q_ready, RING)
            pe.sem_inc(products_ready, RING)

            def project(i, s):
                pe.wait_ge(w_ready, RING + i + 1)
                pe.wait_ge(query_ready, RING + i - 1)
                for k in range(KT):
                    for n, (w, h) in enumerate(((w_hi, h2_hi), (w_hi, h2_lo), (w_lo, h2_hi))):
                        for half in range(2):
                            last = pe.matmul(q_ps[s][:, half * 512:(half + 1) * 512], w[s][:, k],
                                             h[:, k, half * 512:(half + 1) * 512],
                                             start=(k == 0 and n == 0), stop=(k == KT - 1 and n == 2))
                last.then_inc(q_ready, 1)

            def match(i, s, turn):
                pe.wait_ge(query_ready, RING + i + 1)
                pe.wait_ge(keys_loaded[s], 16 * (turn + 1))
                pe.wait_ge(sub_ready, RING + i - 1)
                for n in range(TT):
                    last = pe.matmul(sub_ps[s][:, n], query[s][:, n * P:(n + 1) * P], keys[:, s],
                                     start=True, stop=True)
                last.then_inc(products_ready, 1)

            project(0, 0)
            with pe.Fori(0, HC // 2 - 1) as pair:
                for s in range(2):
                    project(2 * pair + s + 1, 1 - s)
                    match(2 * pair + s, s, pair)
            project(HC - 1, 1)
            match(HC - 2, 0, HC // 2 - 1)
            match(HC - 1, 1, HC // 2 - 1)

        @block.scalar
        def _(act):
            act.sem_inc(query_ready, RING)
            act.sem_inc(sub_ready, RING)

            def split(i, s, turn):
                act.wait_ge(w_loaded[s], 16 * (turn + 1))
                act.wait_ge(q_ready, RING + i - 1)
                act.activation(w_hi[s][:], w_raw[s][:], ACT.Copy).then_inc(w_hi_ready, 1)

            def copies(i, s, turn=None):
                act.wait_ge(q_ready, RING + i + 1)
                act.wait_ge(products_ready, RING + i - 1)
                act.activation(query[s][:], q_ps[s][:], ACT.Copy).then_inc(query_ready, 1)
                if turn is not None:
                    split(i + 2, s, turn)
                act.wait_ge(products_ready, RING + i + 1)
                act.wait_ge(taken, i + 1)
                act.activation(sub[s][:], sub_ps[s][:], ACT.Copy).then_inc(sub_ready, 1)

            split(0, 0, 0)
            split(1, 1, 0)
            with act.Fori(0, HC // 2 - 1) as pair:
                for s in range(2):
                    copies(2 * pair + s, s, pair + 1)
            copies(HC - 2, 0)
            copies(HC - 1, 1)

        @block.vector
        def _(dve):
            dve.sem_inc(w_ready, RING)
            dve.sem_inc(taken, RING)

            def split(i, s):
                dve.wait_ge(w_hi_ready, i + 1)
                dve.tensor_tensor(w_lo[s][:], w_raw[s][:], w_hi[s][:].bitcast(F32), ALU.subtract).then_inc(w_ready, 1)

            def pick(i, s):
                STEPS = 4
                dve.wait_ge(sub_ready, RING + i + 1)
                dve.sem_inc(passed, 1)
                for half in range(2):
                    eight = slice(8 * half, 8 * half + 8)
                    for n in range(TT):
                        last = dve.max(best[:, n, eight], sub[s][:, n])
                    last.then_inc(picked, 1)
                    dve.wait_ge(picked, STEPS * i + 2 * half + 1)
                    dve.sem_inc(passed, 1)
                    for n in range(TT):
                        last = dve.max_index(best_at[:, n, eight], best[:, n, eight], sub[s][:, n])
                    if half == 0:
                        last.then_inc(picked, 1)
                        dve.wait_ge(picked, STEPS * i + 2)
                        dve.sem_inc(passed, 1)
                        for n in range(TT):
                            last = dve.match_replace(sub[s][:, n], best[:, n, eight], sub[s][:, n], TAKEN)
                        last.then_inc(replaced, 1)
                        dve.wait_ge(replaced, i + 1)
                        dve.sem_inc(passed, 1)
                    else:
                        last.then_inc(picked, 1)
                        dve.wait_ge(picked, STEPS * i + 4)
                dve.tensor_copy(top_s[:, :, i], best[:])
                dve.tensor_copy(top_i[:, :, i], best_at[:]).then_inc(taken, 1)
                dve.wait_ge(taken, RING + i + 1)

            split(0, 0)
            split(1, 1)
            with dve.Fori(0, HC // 2 - 1) as pair:
                for s in range(2):
                    split(2 * pair + s + 2, s)
                    pick(2 * pair + s, s)
            pick(HC - 2, 0)
            pick(HC - 1, 1)


def gates_phase(nc, mem, top_s, top_i, gates, h2_hi, h2_lo, peer_ut, early_gelu):
    PER_ROUND = GROUPS // TT
    CH = PH * TOPK
    BATCH = 8
    PER_TILE = P // BATCH
    RING = 4
    iota = mem.sb("iota", [P, P], F32)
    ident = mem.sb("ident", [P, P], F32)
    index = mem.sb("index", [P, 2, PH, TOPK], BF16)
    cand = mem.sb("cand", [P, PH, TOPK * TOPK], F32)
    sel_s = mem.sb("sel_s", [P, PH, TOPK], F32)
    sel_at = mem.sb("sel_at", [P, PH, TOPK], U32)
    sel_ab = mem.sb("sel_ab", [P, 2, CH], U32)
    ab = sel_ab[:].bitcast(F32)
    pick_of = mem.sb("pick_of", [P, CH, TOPK], BF16)
    chosen = mem.sb("chosen", [P, 3, CH], F32)
    total = mem.sb("total", [P, PH], F32)
    per_choice = mem.sb("per_choice", [P, 3, P], F32)
    is_1 = [mem.sb(f"is_1{s}", [P, BATCH, P], BF16) for s in range(2)]
    hot_1 = [mem.sb(f"hot_1{s}", [P, BATCH, P], F32) for s in range(RING)]
    hot_2 = [mem.sb(f"hot_2{s}", [P, BATCH, P], F32) for s in range(RING)]
    stage = [mem.sb(f"stage{s}", [P, P, GB], F32) for s in range(2)]
    e_raw = [mem.sb(f"e_raw{s}", [P, KT, P], F32) for s in range(2)]
    e_hi = [mem.sb(f"e_hi{s}", [P, KT, P], F32R) for s in range(2)]
    e_lo = [mem.sb(f"e_lo{s}", [P, KT, P], F32R) for s in range(2)]
    e_gelu = mem.sb("e_gelu", [P, SEQ], F32)
    iota_i = e_gelu[:, 0:P].bitcast(I32)
    with ExitStack() as ctx:
        sem = lambda name: ctx.enter_context(nc.semaphore(name))
        e_ps = ctx.enter_context(nc.psum_tensor("e_ps", [P, SEQ], F32))
        e_hi_ready, e_lo_ready, e_ready = sem("e_hi_ready"), sem("e_lo_ready"), sem("e_ready")
        e_gelu_ready, e_stored = sem("e_gelu_ready"), sem("e_stored")
        e_loaded = [sem(f"e_loaded{s}") for s in range(2)]
        turn_ps = ctx.enter_context(nc.psum_tensor("turn_ps", [P, 3, P], F32))
        gate_ps = [ctx.enter_context(nc.psum_tensor(f"gate_ps{s}", [P, BATCH, P], F32)) for s in range(2)]
        made, chain, summed = sem("made"), sem("chain"), sem("summed")
        passed = sem("passed_g")
        chosen_ready, turned, per_choice_ready = sem("chosen_ready"), sem("turned"), sem("per_choice_ready")
        exp_asked, exp_ready = sem("exp_asked"), sem("exp_ready")
        cand_ready, cand_free = sem("cand_ready"), sem("cand_free")
        is_ready, hot_2_ready = sem("is_ready"), sem("hot_2_ready")
        hot_ready, gate_ready, gate_copied = sem("hot_ready"), sem("gate_ready"), sem("gate_copied")
        stored = [sem(f"gates_stored{s}") for s in range(2)]
        block = ctx.enter_context(nc.Block())

        @block.gpsimd
        def _(pool):
            pool.iota(iota_i, pattern=[[1, P]], base=0, channel_multiplier=0).then_inc(made, 1)
            pool.memset(ident[:], 0.0).then_inc(made, 1)
            pool.wait_ge(made, 2)
            pool.tensor_copy(iota[:], iota_i).then_inc(made, 1)
            pool.affine_select(out=ident[:], in_=ident[:], compare_op=ALU.not_equal, fill=1.0, base=0,
                               pattern=[[-1, P]], channel_multiplier=1).then_inc(made, 1)
            pool.wait_ge(made, 4)
            pool.sem_inc(hot_ready, RING)

            def sums(n):
                pool.wait_ge(cand_free, n + 1)
                pair = top_s[:, n].rearrange("p (h c) k -> p h c k", c=2)
                for h in range(PH):
                    last = pool.tensor_tensor(cand[:, h].rearrange("p (a b) -> p a b", a=TOPK),
                                              pair[:, h, 0].unsqueeze(2).broadcast_to([P, TOPK, TOPK]),
                                              pair[:, h, 1].unsqueeze(1).broadcast_to([P, TOPK, TOPK]), ALU.add)
                last.then_inc(cand_ready, 1)

            def weigh(n, b, s):
                q = PER_TILE * n + b
                pool.wait_ge(is_ready, q + 1)
                pool.wait_ge(gate_ready, q + 1)
                pool.tensor_tensor(hot_1[s][:], is_1[s % 2][:],
                                   per_choice[:, 2, bass.ds(BATCH * b, BATCH)].unsqueeze(2).broadcast_to([P, BATCH, P]),
                                   ALU.mult).then_inc(hot_ready, 1)

            def weigh_tile(n):
                with pool.Fori(0, PER_TILE // RING) as turn:
                    for s in range(RING):
                        weigh(n, RING * turn + s, s)

            def split(m, s):
                pool.wait_ge(e_hi_ready, m + 1)
                pool.tensor_tensor(e_lo[s][:], e_raw[s][:], e_hi[s][:].bitcast(F32), ALU.subtract).then_inc(e_lo_ready, 1)

            def splits(r):
                for c in range(1, PER_ROUND):
                    split(PER_ROUND * r + c, c % 2)

            pool.sem_inc(e_lo_ready, 2)
            split(0, 0)
            sums(0)
            splits(0)
            sums(1)
            split(PER_ROUND, 0)
            with pool.Fori(1, TT - 1) as r:
                splits(r)
                sums(r + 1)
                split(PER_ROUND * (r + 1), 0)
                weigh_tile(r - 1)
            splits(TT - 1)
            weigh_tile(TT - 2)
            weigh_tile(TT - 1)

        @block.vector
        def _(dve):
            CHAIN = 14
            gate = chosen[:, 2].rearrange("p (h k) -> p h k", h=PH)
            dve.wait_ge(made, 4)

            def choose(n):
                steps = [0]

                def then(ins):
                    steps[0] += 1
                    ins.then_inc(chain, 1)
                    dve.wait_ge(chain, CHAIN * n + steps[0])
                    dve.sem_inc(passed, 1)

                then(dve.tensor_copy(index[:].rearrange("p c h k -> p h c k"),
                                     top_i[:, n].rearrange("p (h c) k -> p h c k", c=2)))
                dve.wait_ge(cand_ready, n + 1)
                dve.sem_inc(passed, 1)
                for half in range(2):
                    eight = slice(8 * half, 8 * half + 8)
                    for h in range(PH):
                        last = dve.max(sel_s[:, h, eight], cand[:, h])
                    then(last)
                    for h in range(PH):
                        last = dve.max_index(sel_at[:, h, eight], sel_s[:, h, eight], cand[:, h])
                    then(last)
                    if half == 0:
                        for h in range(PH):
                            last = dve.match_replace(cand[:, h], sel_s[:, h, eight], cand[:, h], TAKEN)
                        then(last)
                dve.sem_inc(cand_free, 1)
                flat = sel_at[:].rearrange("p h k -> p (h k)")
                dve.tensor_scalar(sel_ab[:, 0], flat, 4, None, ALU.logical_shift_right)
                then(dve.tensor_scalar(sel_ab[:, 1], flat, TOPK - 1, None, ALU.bitwise_and))
                then(dve.tensor_copy(ab, sel_ab[:]))
                dve.wait_ge(turned, n + 1)
                for side in range(2):
                    rank = ab[:, side].unsqueeze(2).broadcast_to([P, CH, TOPK])
                    ranks = iota[:, 0:TOPK].unsqueeze(1).broadcast_to([P, CH, TOPK])
                    then(dve.tensor_tensor(pick_of[:], rank, ranks, ALU.is_equal))
                    hk = pick_of[:].rearrange("p (h k) j -> p h k j", h=PH)
                    for h in range(PH):
                        last = dve.tensor_tensor(hk[:, h], hk[:, h],
                                                 index[:, side, h].unsqueeze(1).broadcast_to([P, TOPK, TOPK]),
                                                 ALU.mult)
                    then(last)
                    then(dve.tensor_reduce(chosen[:, side], pick_of[:], AX.X, ALU.add))
                dve.tensor_tensor(gate, sel_s[:], sel_s[:, :, 0:1].broadcast_to([P, PH, TOPK]),
                                  ALU.subtract).then_inc(exp_asked, 1)
                assert steps[0] == CHAIN, steps

            def normalise(n):
                dve.wait_ge(exp_ready, n + 1)
                dve.tensor_reduce(total[:], gate, AX.X, ALU.add).then_inc(summed, 1)
                dve.wait_ge(summed, 2 * n + 1)
                dve.reciprocal(total[:], total[:]).then_inc(summed, 1)
                dve.wait_ge(summed, 2 * n + 2)
                dve.tensor_tensor(gate, gate, total[:].unsqueeze(2).broadcast_to([P, PH, TOPK]),
                                  ALU.mult).then_inc(chosen_ready, 1)

            def one_hots(n, b, s):
                q = PER_TILE * n + b
                dve.wait_ge(gate_ready, q + 1)
                dve.wait_ge(hot_ready, RING + q - 1)
                keys = iota[:].unsqueeze(1).broadcast_to([P, BATCH, P])
                key = lambda side: per_choice[:, side, bass.ds(BATCH * b, BATCH)].unsqueeze(2).broadcast_to([P, BATCH, P])
                dve.tensor_tensor(is_1[s % 2][:], keys, key(0), ALU.is_equal).then_inc(is_ready, 1)
                dve.tensor_tensor(hot_2[s][:], keys, key(1), ALU.is_equal).then_inc(hot_2_ready, 1)

            def one_hots_tile(n):
                dve.wait_ge(per_choice_ready, 1 + n + 1)
                dve.sem_inc(passed, 1)
                with dve.Fori(0, PER_TILE // RING) as turn:
                    for s in range(RING):
                        one_hots(n, RING * turn + s, s)

            dve.sem_inc(cand_free, 1)
            choose(0)
            normalise(0)
            with dve.Fori(1, TT) as r:
                choose(r)
                one_hots_tile(r - 1)
                normalise(r)
            one_hots_tile(TT - 1)

        @block.tensor
        def _(pe):
            pe.wait_ge(made, 4)
            pe.sem_inc(turned, 1)
            pe.sem_inc(gate_ready, RING)

            def turn(n):
                pe.wait_ge(chosen_ready, n + 1)
                pe.wait_ge(per_choice_ready, n + 1)
                for k in range(3):
                    last = pe.transpose(turn_ps[:, k], chosen[:, k], ident[:])
                last.then_inc(turned, 1)

            def products(n):
                with pe.Fori(0, PER_TILE // RING) as round_:
                    for s in range(RING):
                        q = PER_TILE * n + RING * round_ + s
                        pe.wait_ge(hot_2_ready, q + 1)
                        pe.wait_ge(hot_ready, RING + q + 1)
                        pe.wait_ge(gate_copied, 2 + q - 1)
                        for t in range(BATCH):
                            last = pe.matmul(gate_ps[s % 2][:, t], hot_2[s][:, t], hot_1[s][:, t], start=True, stop=True)
                        last.then_inc(gate_ready, 1)

            def project(r):
                for c in range(PER_ROUND):
                    m, s = PER_ROUND * r + c, c % 2
                    pe.wait_ge(e_lo_ready, 2 + m + 1)
                    for half in range(2):
                        at = slice(512 * half, 512 * (half + 1))
                        pe.wait_ge(e_gelu_ready, 2 * m + half + 1)
                        for k in range(KT):
                            for j, (u, h) in enumerate(((e_hi, h2_hi), (e_hi, h2_lo), (e_lo, h2_hi))):
                                last = pe.matmul(e_ps[:, at], u[s][:, k], h[:, k, at], start=(k == 0 and j == 0),
                                                 stop=(k == KT - 1 and j == 2))
                        last.then_inc(e_ready, 1)

            pe.sem_inc(e_ready, 4)
            project(0)
            turn(0)
            with pe.Fori(1, TT) as r:
                project(r)
                products(r - 1)
                turn(r)
            products(TT - 1)

        @block.scalar
        def _(act):
            act.sem_inc(gate_copied, 2)
            gate = chosen[:, 2]

            def split(m, s, turn):
                act.wait_ge(e_loaded[s], 16 * (turn + 1))
                act.wait_ge(e_ready, 2 * m + 2)
                act.activation(e_hi[s][:], e_raw[s][:], ACT.Copy).then_inc(e_hi_ready, 1)

            def gelu(m):
                act.wait_ge(e_stored, 16 * (m + 1))
                for half in range(2):
                    at = slice(512 * half, 512 * (half + 1))
                    act.wait_ge(e_ready, 4 + 2 * m + half + 1)
                    act.activation(e_gelu[:, at], e_ps[:, at], ACT.Gelu).then_inc(e_gelu_ready, 1)
                act.wait_ge(e_gelu_ready, 2 + 2 * (m + 1))
                act.dma_start(early_gelu[m], e_gelu[:]).then_inc(e_stored, 16)

            def early(r, more=True):
                for c in range(PER_ROUND):
                    m = PER_ROUND * r + c
                    if more or c < PER_ROUND - 1:
                        split(m + 1, (c + 1) % 2, PER_ROUND // 2 * r + (c + 1) // 2)
                    gelu(m)

            def exp(n):
                act.wait_ge(exp_asked, n + 1)
                act.activation(gate, gate, ACT.Exp).then_inc(exp_ready, 1)

            def turned_choices(n):
                act.wait_ge(turned, n + 2)
                act.activation(per_choice[:], turn_ps[:], ACT.Copy).then_inc(per_choice_ready, 1)

            def copies(n):
                for part in range(2):
                    act.wait_ge(stored[part], 16 * (n + 1))
                    with act.Fori(0, GB // BATCH // 2) as pair:
                        for s in range(2):
                            b = 2 * pair + s
                            q = PER_TILE * n + (GB // BATCH) * part + b
                            act.wait_ge(gate_ready, RING + q + 1)
                            act.activation(stage[part][:, :, bass.ds(BATCH * b, BATCH)].rearrange("p k t -> p t k"),
                                           gate_ps[s][:], ACT.Copy).then_inc(gate_copied, 1)

            act.sem_inc(per_choice_ready, 1)
            act.sem_inc(e_gelu_ready, 2)
            act.sem_inc(e_stored, 16)
            split(0, 0, 0)
            early(0)
            exp(0)
            turned_choices(0)
            with act.Fori(1, TT - 1) as r:
                early(r)
                exp(r)
                copies(r - 1)
                turned_choices(r)
            early(TT - 1, more=False)
            exp(TT - 1)
            copies(TT - 2)
            turned_choices(TT - 1)
            copies(TT - 1)
            act.wait_ge(e_stored, 16 * (GROUPS + 1))

        @block.sync
        def _(sp):
            for s in range(2):
                sp.sem_inc(stored[s], 16)

            def load(m, s):
                sp.wait_ge(e_lo_ready, m + 1)
                sp.dma_start(e_raw[s][:], peer_ut[E * m + E - 1]).then_inc(e_loaded[s], 16)

            def store(n):
                for s in range(2):
                    sp.wait_ge(gate_copied, 2 + PER_TILE * n + (GB // BATCH) * (s + 1))
                    sp.dma_start(gates[2 * n + s], stage[s][:]).then_inc(stored[s], 16)

            AHEAD = 2
            for m in range(PER_ROUND + AHEAD):
                load(m, m % 2)
            with sp.Fori(1, TT - 1) as r:
                for c in range(AHEAD, PER_ROUND + AHEAD):
                    load(PER_ROUND * r + c, c % 2)
                store(r - 1)
            for c in range(AHEAD, PER_ROUND):
                load(PER_ROUND * (TT - 1) + c, c % 2)
            store(TT - 2)
            store(TT - 1)
            for s in range(2):
                sp.wait_ge(stored[s], 16 * (TT + 1))


def dense_phase(nc, mem, h2_hi, h2_lo, peer_ut, peer_v, gates, early_gelu, x_mid, out):
    HALVES = SEQ // 512
    BANKS = 4
    RING = 2
    OUTS = TT * (D // 512)

    Tile = namedtuple("Tile", "j early c slot next_turn")

    def group(pair, half):
        def tile(p):
            j = (0, 1, 3, 2)[p]
            if j == 3:
                return Tile(j, True, None, None, None)
            c = (E - 1) * half + j
            return Tile(j, False, 2 * (E - 1) * pair + c, c % 2, (E - 1) * pair + (c + 1) // 2)
        return tile

    u_raw = mem.sb("u_raw", [P, 2, KT, P], F32)
    u_hi = [mem.sb(f"u_hi{s}", [P, KT, P], F32R) for s in range(2)]
    u_lo = [mem.sb(f"u_lo{s}", [P, KT, P], F32R) for s in range(2)]
    v_raw = mem.sb("v_raw", [P, 2, D], F32)
    v_hi = mem.sb("v_hi", [P, E, D], F32R)
    v_lo = mem.sb("v_lo", [P, E, D], F32R)
    early = mem.sb("early", [P, SEQ], F32)
    gate = mem.sb("gate", [P, 2, SEQ], F32)
    weight = mem.sb("weight", [P, 2, SEQ], F32)
    w_hi = mem.sb("w_hi", [P, E, SEQ], F32R)
    w_lo = mem.sb("w_lo", [P, E, SEQ], F32R)
    acc = mem.sb("acc", [P, TT, D], F32)

    with ExitStack() as ctx:
        sem = lambda name: ctx.enter_context(nc.semaphore(name))
        z_ps = [ctx.enter_context(nc.psum_tensor(f"z_ps{s}", [P, SEQ], F32)) for s in range(2)]
        out_ps = [ctx.enter_context(nc.psum_tensor(f"out_ps{b}", [P, 512], F32)) for b in range(BANKS)]
        u_loaded = [sem(f"u_loaded{s}") for s in range(2)]
        v_loaded = [sem(f"v_loaded{s}") for s in range(2)]
        gate_loaded = [sem(f"gate_loaded{s}") for s in range(2)]
        acc_loaded, early_loaded = sem("acc_loaded"), sem("early_loaded")
        u_hi_ready, u_ready = sem("u_hi_ready"), sem("u_ready")
        v_hi_ready, v_ready = sem("v_hi_ready"), sem("v_ready")
        z_ready = sem("z_ready")
        gelu_ready, weight_ready = sem("gelu_ready"), sem("weight_ready")
        w_hi_ready, w_ready = sem("w_hi_ready"), sem("w_ready")
        out_ready, out_free, out_stored = sem("out_ready"), sem("out_free"), sem("out_stored")
        block = ctx.enter_context(nc.Block())

        @block.sync
        def _(sp):
            def load_u(g, p, kind):
                tile = kind(p)
                if tile.early:
                    sp.wait_ge(w_ready, RING + E * g - 1)
                    sp.dma_start(early[:], early_gelu[g]).then_inc(early_loaded, 16)
                else:
                    sp.wait_ge(u_ready, RING + tile.c - 1)
                    sp.dma_start(u_raw[:, tile.slot], peer_ut[E * g + tile.j]).then_inc(u_loaded[tile.slot], 16)

            def load_rest(g, p, kind):
                tile, q, s = kind(p), E * g + p, p % 2
                e = E * g + tile.j
                sp.wait_ge(weight_ready, RING + q - 1)
                sp.dma_start(gate[:, s].rearrange("p (b t) -> p b t", t=GB),
                             gates[:, :, e].rearrange("b p t -> p b t")).then_inc(gate_loaded[s], 16)
                sp.wait_ge(v_ready, RING + q - 1)
                sp.dma_start(v_raw[:, s], peer_v[e]).then_inc(v_loaded[s], 16)

            def load_group(g, pair, half, last=False):
                for p in range(E):
                    if p < E - 2:
                        load_u(g, p + 2, group(pair, half))
                    elif not last:
                        load_u(g + 1, p - 2, group(pair + half, 1 - half))
                    load_rest(g, p, group(pair, half))

            load_u(0, 0, group(0, 0))
            load_u(0, 1, group(0, 0))
            with sp.Fori(0, GROUPS // 2 - 1) as pair:
                for half in range(2):
                    load_group(2 * pair + half, pair, half)
            load_group(GROUPS - 2, GROUPS // 2 - 1, 0)
            load_group(GROUPS - 1, GROUPS // 2 - 1, 1, last=True)
            for n in range(TT):
                sp.wait_ge(out_free, BANKS + OUTS * (GROUPS - 1) + 2 * (n + 1))
                sp.dma_start(out[n * P:(n + 1) * P], acc[:, n]).then_inc(out_stored, 16)
            sp.wait_ge(out_stored, 16 * TT)

        @block.scalar
        def _(act):
            act.sem_inc(gelu_ready, RING)


            def split_u(c, slot, turn):
                act.wait_ge(u_loaded[slot], 16 * (turn + 1))
                act.wait_ge(z_ready, RING + c - 1)
                act.activation(u_hi[slot][:], u_raw[:, slot], ACT.Copy).then_inc(u_hi_ready, 1)

            def step(g, p, kind, more=True):
                tile, q, s = kind(p), E * g + p, p % 2
                turn = (E // 2) * g + p // 2
                if tile.early:
                    gelu = early[:]
                else:
                    gelu = weight[:, tile.slot]
                    if more:
                        split_u(tile.c + 1, 1 - tile.slot, tile.next_turn)
                    act.wait_ge(z_ready, RING + tile.c + 1)
                    act.wait_ge(w_ready, RING + q - 1)
                    act.activation(gelu, z_ps[tile.slot][:], ACT.Gelu).then_inc(gelu_ready, 1)
                act.wait_ge(v_loaded[s], 16 * (turn + 1))
                act.wait_ge(out_ready, OUTS * (g + 1))
                act.activation(v_hi[:, tile.j], v_raw[:, s], ACT.Copy).then_inc(v_hi_ready, 1)
                act.wait_ge(weight_ready, RING + q + 1)
                act.activation(w_hi[:, tile.j], gelu, ACT.Copy).then_inc(w_hi_ready, 1)

            split_u(0, 0, 0)
            def rest_of_group(g, pair, half):
                for p in range(1, E):
                    step(g, p, group(pair, half))
                step(g + 1, 0, group(pair + half, 1 - half))

            step(0, 0, group(0, 0))
            act.dma_start(acc[:], x_mid.rearrange("n p d -> p n d")).then_inc(acc_loaded, 16)
            with act.Fori(0, GROUPS // 2 - 1) as pair:
                for half in range(2):
                    rest_of_group(2 * pair + half, pair, half)
            rest_of_group(GROUPS - 2, GROUPS // 2 - 1, 0)
            for p in range(1, E):
                step(GROUPS - 1, p, group(GROUPS // 2 - 1, 1), more=p < E - 1)

        @block.vector
        def _(dve):
            dve.sem_inc(out_free, BANKS)
            for ready in (u_ready, v_ready, weight_ready, w_ready):
                dve.sem_inc(ready, RING)

            def split_u(c, slot):
                dve.wait_ge(u_hi_ready, c + 1)
                dve.tensor_tensor(u_lo[slot][:], u_raw[:, slot], u_hi[slot][:].bitcast(F32), ALU.subtract).then_inc(u_ready, 1)

            def step(g, p, kind, more=True, add_group=None):
                tile, q, s = kind(p), E * g + p, p % 2
                turn = (E // 2) * g + p // 2
                if tile.early:
                    weights = early[:]
                    dve.wait_ge(early_loaded, 16 * (g + 1))
                else:
                    weights = weight[:, tile.slot]
                    if more:
                        split_u(tile.c + 1, 1 - tile.slot)
                    dve.wait_ge(gelu_ready, RING + tile.c + 1)
                dve.wait_ge(gate_loaded[s], 16 * (turn + 1))
                dve.tensor_tensor(weights, weights, gate[:, s], ALU.mult).then_inc(weight_ready, 1)
                if add_group is not None:
                    add_outputs(add_group)
                dve.wait_ge(v_hi_ready, q + 1)
                dve.tensor_tensor(v_lo[:, tile.j], v_raw[:, s], v_hi[:, tile.j].bitcast(F32), ALU.subtract).then_inc(v_ready, 1)
                dve.wait_ge(w_hi_ready, q + 1)
                dve.tensor_tensor(w_lo[:, tile.j], weights, w_hi[:, tile.j].bitcast(F32), ALU.subtract).then_inc(w_ready, 1)

            def add_outputs(g):
                for o in range(OUTS):
                    dve.wait_ge(out_ready, OUTS * (g + 1) + o + 1)
                    part = acc[:, o // 2, (o % 2) * 512:(o % 2 + 1) * 512]
                    dve.tensor_tensor(part, part, out_ps[o % BANKS][:], ALU.add).then_inc(out_free, 1)

            split_u(0, 0)
            def rest_of_group(g, pair, half):
                for p in range(1, E):
                    step(g, p, group(pair, half))
                step(g + 1, 0, group(pair + half, 1 - half), add_group=g)

            step(0, 0, group(0, 0))
            dve.wait_ge(acc_loaded, 16)
            with dve.Fori(0, GROUPS // 2 - 1) as pair:
                for half in range(2):
                    rest_of_group(2 * pair + half, pair, half)
            rest_of_group(GROUPS - 2, GROUPS // 2 - 1, 0)
            for p in range(1, E):
                step(GROUPS - 1, p, group(GROUPS // 2 - 1, 1), more=p < E - 1)
            add_outputs(GROUPS - 1)

        @block.tensor
        def _(pe):
            pe.sem_inc(z_ready, RING)
            pe.sem_inc(out_ready, OUTS)

            def project_u(tile):
                s = tile.slot
                pe.wait_ge(u_ready, RING + tile.c + 1)
                pe.wait_ge(gelu_ready, RING + tile.c - 1)
                for k in range(KT):
                    for n, (u, h) in enumerate(((u_hi, h2_hi), (u_hi, h2_lo), (u_lo, h2_hi))):
                        for half in range(HALVES):
                            last = pe.matmul(z_ps[s][:, half * 512:(half + 1) * 512], u[s][:, k],
                                             h[:, k, half * 512:(half + 1) * 512],
                                             start=(k == 0 and n == 0), stop=(k == KT - 1 and n == 2))
                last.then_inc(z_ready, 1)

            def project_v(g):
                pe.wait_ge(w_ready, RING + E * (g + 1))
                pe.wait_ge(v_ready, RING + E * (g + 1))
                for o in range(OUTS):
                    n, half = o // 2, o % 2
                    pe.wait_ge(out_free, OUTS * g + o + 1)
                    for j in range(E):
                        for m, (w, v) in enumerate(((w_hi, v_hi), (w_hi, v_lo), (w_lo, v_hi))):
                            last = pe.matmul(out_ps[o % BANKS][:], w[:, j, n * P:(n + 1) * P],
                                             v[:, j, half * 512:(half + 1) * 512],
                                             start=(j == 0 and m == 0), stop=(j == E - 1 and m == 2))
                    last.then_inc(out_ready, 1)

            def rest_of_group(g, pair, half):
                for p in (1, 3):
                    project_u(group(pair, half)(p))
                project_u(group(pair + half, 1 - half)(0))
                project_v(g)

            project_u(group(0, 0)(0))
            with pe.Fori(0, GROUPS // 2 - 1) as pair:
                for half in range(2):
                    rest_of_group(2 * pair + half, pair, half)
            rest_of_group(GROUPS - 2, GROUPS // 2 - 1, 0)
            for p in (1, 3):
                project_u(group(GROUPS // 2 - 1, 1)(p))
            project_v(GROUPS - 1)
def build(nc, a, out):
    start, end = SBUF_START, nc.sbuf_usable_end
    KB = 1024
    x_mid = nc.dram_tensor("x_mid", (TT, P, D), F32, kind="Internal").ap()
    gates = nc.dram_tensor("gates", (SEQ // GB, P, N_KEYS, GB), F32, kind="Internal").ap()
    early_gelu = nc.dram_tensor("early_gelu", (GROUPS, P, SEQ), F32, kind="Internal").ap()
    x = a["x"].rearrange("b (n p) d -> (b n) p d", p=P)

    kept = Memory(nc, start, start + 88 * KB)
    qT = kept.sb("qT", [P, HEADS, SEQ], F32)
    kT = kept.sb("kT", [P, HEADS, SEQ], F32)
    values = kept.sb("values", [P, TT, DA], F32)
    convT = kept.sb("convT", [P, 5 * CT, SEQ], F32)
    project_phase(nc, Memory(nc, kept.at, end), x, a["norm1_g"], a["w_in"], a["q_norm_g"], a["k_norm_g"],
                  qT, kT, values, convT)

    mixed = Memory(nc, kept.at, end)
    mixedT = mixed.sb("mixedT", [P, KT, SEQ], F32)
    mix_phase(nc, mixed, a["lam_vectors"], a["subln_g"], a["cf_dw"], a["cf_cols"], a["sc_w"],
              qT, kT, values, convT, mixedT)

    h2 = Memory(nc, start, start + 64 * KB)
    h2_hi = h2.sb("h2_hi", [P, KT, SEQ], F32R)
    h2_lo = h2.sb("h2_lo", [P, KT, SEQ], F32R)
    output_phase(nc, Memory(nc, kept.at + 32 * KB, end), Memory(nc, h2.at, kept.at), x, a["norm2_g"], a["w_out"], mixedT, x_mid, h2_hi, h2_lo)

    tops = Memory(nc, h2.at, end)
    top_s = tops.sb("top_s", [P, TT, 2 * PH, TOPK], F32)
    top_i = tops.sb("top_i", [P, TT, 2 * PH, TOPK], BF16)
    keys_phase(nc, Memory(nc, tops.at, end), h2_hi, h2_lo, a["peer_wqt"], a["keys_t"], top_s, top_i)
    gates_phase(nc, Memory(nc, tops.at, end), top_s, top_i, gates, h2_hi, h2_lo, a["peer_ut"], early_gelu)
    dense_phase(nc, Memory(nc, h2.at, end), h2_hi, h2_lo, a["peer_ut"], a["peer_v"], gates, early_gelu, x_mid, out)


def kernel(x, norm1_g, w_in, q_norm_g, k_norm_g, lam_q1, lam_k1, lam_q2, lam_k2, subln_g,
           cf_dw, cf_dw_b, cf_ln_g, cf_ln_b, sc_w, w_out, norm2_g,
           peer_wq, peer_keys, peer_u, peer_v):
    import concourse.bacc as bacc
    from concourse.bass_utils import run_bass_kernel_spmd

    def by_partition(v):
        return v.reshape(-1, P).T

    arrays = {
        "x": x,
        "norm1_g": by_partition(norm1_g[0]),
        "w_in": w_in[0],
        "q_norm_g": q_norm_g[0].reshape(DH, 1),
        "k_norm_g": k_norm_g[0].reshape(DH, 1),
        "lam_vectors": np.stack([lam_q1[0], lam_k1[0], lam_q2[0], lam_k2[0]]),
        "subln_g": subln_g[0].reshape(DV, 1),
        "cf_dw": cf_dw[0].reshape(CF_TAPS, CT, P).transpose(2, 1, 0),
        "cf_cols": np.stack([by_partition(v[0]) for v in (cf_dw_b, cf_ln_g, cf_ln_b)], axis=-1),
        "sc_w": sc_w[0].reshape(SC_TAPS, CT, P).transpose(2, 1, 0),
        "w_out": w_out[0],
        "norm2_g": by_partition(norm2_g[0]),
        "peer_wqt": peer_wq[0].reshape(KT, P, 2 * PH, P).transpose(2, 1, 0, 3),
        "keys_t": peer_keys[0].reshape(2 * PH, N_KEYS, P).transpose(0, 2, 1),
        "peer_ut": peer_u[0].reshape(N_KEYS, N_KEYS, KT, P).transpose(0, 3, 2, 1),
        "peer_v": peer_v[0].reshape(N_KEYS, N_KEYS, D),
    }
    arrays = {name: np.ascontiguousarray(v) for name, v in arrays.items()}
    nc = bacc.Bacc("TRN2", target_bir_lowering=False, num_devices=1, dynamic_dma_scratch_size=DMA_SCRATCH)
    args = {name: nc.dram_tensor(f"in_{name}", v.shape, mybir.dt.from_np(v.dtype), kind="ExternalInput").ap()
            for name, v in arrays.items()}
    out = nc.dram_tensor("out", (1, SEQ, D), F32, kind="ExternalOutput").ap()
    build(nc, args, out.rearrange("b s d -> (b s) d"))
    result = run_bass_kernel_spmd(nc, [{f"in_{name}": v for name, v in arrays.items()}], core_ids=[0])
    return result.results[0]["out"]
```

```python
from collections import namedtuple
from contextlib import ExitStack

import numpy as np

import concourse.bass as bass
from concourse import mybir
from concourse.alu_op_type import AluOpType as ALU

ACT = mybir.ActivationFunctionType
AX = mybir.AxisListType
F32, F32R, BF16 = mybir.dt.float32, mybir.dt.float32r, mybir.dt.bfloat16
I32, U32, U16 = mybir.dt.int32, mybir.dt.uint32, mybir.dt.uint16

P = 128
SEQ = 1024
D = 1024
TT = SEQ // P
KT = D // P
HEADS = 4
DH = 64
DV = 2 * DH
DA = HEADS * DV
CONV = 256
CT = CONV // P
CF_TAPS = 31
SC_TAPS = 3
LN_GROUP = 64
N_KEYS = 128
PH = 8
TOPK = 16
RMS_EPS = 1e-6
LN_EPS = 1e-5
LAM_INIT = 0.8 - 0.6 * 1.0
MASKED = -1e30
TAKEN = -3.0e38
E = 4
GROUPS = N_KEYS // E
GB = 64
DMA_SCRATCH = 1024
SBUF_START = DMA_SCRATCH + 128


class Memory:

    def __init__(self, nc, start, end):
        self.nc, self.at, self.end = nc, start, end

    def sb(self, name, shape, dtype):
        size = int(np.prod(shape[1:])) * (2 if dtype in (BF16, U16) else 4)
        tensor = self.nc.alloc_sbuf_tensor_at(name, shape, dtype, offset=self.at)
        self.at += -(-size // 32) * 32
        assert self.at <= self.end, (name, self.at, self.end)
        return tensor


def project_phase(nc, mem, w_mem, x, norm1_g, w_in, q_norm_g, k_norm_g, cf_dw, cf_cols,
                  qT, kT, values, convT, glu, conv, taps_f, cols):
    QKV = 3 * DA
    GROUPS = 2 * DA // DH
    CONV_TILES = convT.shape[1]
    w_qkv = w_mem.sb("w_qkv", [P, KT, QKV], F32)
    w_conv = [mem.sb(f"w_conv{s}", [P, KT, P], F32) for s in range(2)]
    gain1 = mem.sb("gain1", [P, KT], F32)
    gain_q, gain_k = mem.sb("gain_q", [P, 1], F32), mem.sb("gain_k", [P, 1], F32)
    ident = mem.sb("ident_a", [P, P], F32)
    x_in = [mem.sb(f"x_in{s}", [P, D], F32) for s in range(2)]
    x_norm = mem.sb("x_norm", [P, D], F32)
    square = mem.sb("square", [P, D], F32)
    rms = mem.sb("rms", [P, 1], F32)
    hT = mem.sb("hT", [P, KT, SEQ], F32)
    h_tile = [mem.sb(f"h_tile{s}", [P, KT, P], F32) for s in range(2)]
    qk_norm = mem.sb("qk_norm", [P, 2 * DA], F32)
    qk_square = mem.sb("qk_square", [P, 2 * DA], F32)
    qk_rms = mem.sb("qk_rms", [P, GROUPS], F32)
    with ExitStack() as ctx:
        sem = lambda name: ctx.enter_context(nc.semaphore(name))
        turn_ps = ctx.enter_context(nc.psum_tensor("h_turn_ps", [P, KT, P], F32))
        qk_ps = [ctx.enter_context(nc.psum_tensor(f"qk_ps{s}", [P, 2 * DA], F32)) for s in range(2)]
        v_ps = ctx.enter_context(nc.psum_tensor("v_ps", [P, DA], F32))
        qk_turn_ps = turn_ps
        x_loaded = [sem(f"x_loaded{s}") for s in range(2)]
        w_loaded = [sem(f"w_loaded{j}") for j in range(3)]
        small_loaded = sem("small_loaded")
        conv_loaded = [sem(f"conv_loaded{s}") for s in range(2)]
        made, gain_scaled, mean_ready = sem("made_a"), sem("gain_scaled"), sem("mean_ready_a")
        qk_step = sem("qk_step")
        conv_ps = qk_ps
        summed, root_asked, root_ready = sem("summed"), sem("root_asked"), sem("root_ready")
        norm_ready, turned, h_ready, h_kept = sem("norm_ready"), sem("turned_a"), sem("h_ready"), sem("h_kept")
        qkv_ready, qk_summed = sem("qkv_ready"), sem("qk_summed")
        qk_asked, qk_root, qk_ready, qk_turned = sem("qk_asked"), sem("qk_root"), sem("qk_ready"), sem("qk_turned")
        kept, conv_ready, conv_kept = sem("kept"), sem("conv_ready"), sem("conv_kept")
        pads_ready, glu_ready, tap_done = sem("pads_ready"), sem("glu_ready"), sem("tap_done")
        block = ctx.enter_context(nc.Block())

        @block.sync
        def _(sp):
            for half in range(2):
                sp.dma_start(gain_q[DH * half:DH * (half + 1), :], q_norm_g).then_inc(small_loaded, 16)
                sp.dma_start(gain_k[DH * half:DH * (half + 1), :], k_norm_g).then_inc(small_loaded, 16)
            for into, source in ((gain1, norm1_g), (taps_f, cf_dw), (cols, cf_cols)):
                sp.dma_start(into[:], source).then_inc(small_loaded, 16)
            with sp.Fori(0, TT // 2) as pair:
                for s in range(2):
                    sp.wait_ge(norm_ready, 2 * pair + s + 1)
                    sp.dma_start(x_in[s][:], x[2 * pair + s]).then_inc(x_loaded[s], 16)
            with sp.Fori(0, CONV_TILES // 2) as pair:
                for s in range(2):
                    i = 2 * pair + s
                    sp.wait_ge(conv_ready, i + 1)
                    sp.dma_start(w_conv[s][:], w_in[:, bass.ds(QKV + P * i, P)].rearrange("(k p) n -> p k n", p=P))\
                      .then_inc(conv_loaded[s], 16)

        @block.gpsimd
        def _(pool):
            pool.memset(ident[:], 0.0).then_inc(made, 1)
            pool.wait_ge(made, 1)
            pool.affine_select(out=ident[:], in_=ident[:], compare_op=ALU.not_equal, fill=1.0, base=0,
                               pattern=[[-1, P]], channel_multiplier=1).then_inc(made, 1)
            pool.wait_ge(qkv_ready, TT)
            pool.memset(glu[:, :, 0:CF_TAPS - 1], 0.0).then_inc(pads_ready, 1)

        @block.scalar
        def _(act):
            act.wait_ge(x_loaded[0], 16)
            for j in range(3):
                at = slice(DA * j, DA * (j + 1))
                act.dma_start(w_qkv[:, :, at], w_in[:, at].rearrange("(k p) n -> p k n", p=P)).then_inc(w_loaded[j], 16)

            def norm(n, s, turn):
                act.wait_ge(x_loaded[s], 16 * (turn + 1))
                act.activation(square[:], x_in[s][:], ACT.Square, accum_out=rms[:]).then_inc(summed, 1)
                act.wait_ge(root_asked, n + 1)
                act.activation(rms[:], rms[:], ACT.Sqrt).then_inc(root_ready, 1)

            def keep(n, s):
                act.wait_ge(h_ready, n + 1)
                act.activation(hT[:, :, bass.ds(P * n, P)], h_tile[s][:], ACT.Copy).then_inc(h_kept, 1)

            def finish(n, s):
                act.wait_ge(qkv_ready, n + 1)
                act.activation(qk_square[:], qk_ps[s][:], ACT.Square).then_inc(qk_summed, 1)
                act.activation(values[:, n], v_ps[:], ACT.Copy).then_inc(qk_summed, 1)
                act.wait_ge(qk_asked, n + 1)
                act.activation(qk_rms[:], qk_rms[:], ACT.Sqrt).then_inc(qk_root, 1)

            def keep_qk(n):
                act.wait_ge(qk_turned, n + 1)
                at = bass.ds(P * n, P)
                act.activation(qT[:, :, at], qk_turn_ps[:, 0:HEADS], ACT.Copy, scale=gain_q[:])
                act.activation(kT[:, :, at], qk_turn_ps[:, HEADS:], ACT.Copy, scale=gain_k[:]).then_inc(kept, 1)

            def tile(n, s, turn, more=True):
                finish(n - 1, 1 - s)
                keep(n + 1, 1 - s)
                keep_qk(n - 1)
                if more:
                    norm(n + 2, s, turn + 1)

            act.sem_inc(kept, 1)
            act.wait_ge(small_loaded, 16 * 7)
            act.wait_ge(gain_scaled, 1)
            norm(0, 0, 0)
            keep(0, 0)
            norm(1, 1, 0)
            keep(1, 1)
            norm(2, 0, 1)
            with act.Fori(0, TT // 2 - 2) as pair:
                for s in (1, 0):
                    tile(2 * pair + 2 - s, s, pair + 1 - s)
            tile(TT - 3, 1, TT // 2 - 2)
            tile(TT - 2, 0, TT // 2 - 1, more=False)
            for n in (TT - 2, TT - 1):
                finish(n, n % 2)
                keep_qk(n)
            act.sem_inc(conv_kept, 2)

            def keep_columns(pair, what=ACT.Copy):
                for s in range(2):
                    act.wait_ge(conv_ready, 2 + 2 * pair + s + 1)
                    act.activation(convT[:, 2 * pair + s], conv_ps[s][:], what).then_inc(conv_kept, 1)

            keep_columns(0)
            keep_columns(1, ACT.Sigmoid)
            with act.Fori(2, CONV_TILES // 2) as pair:
                keep_columns(pair)

        @block.vector
        def _(dve):
            SCALE = float(DH) ** -0.5
            dve.wait_ge(small_loaded, 16 * 7)
            dve.tensor_scalar(gain_q[:], gain_q[:], SCALE, None, ALU.mult).then_inc(gain_scaled, 1)
            dve.sem_inc(norm_ready, 2)

            def norm(n, s):
                dve.wait_ge(summed, n + 1)
                dve.tensor_scalar(rms[:], rms[:], 1.0 / D, RMS_EPS, ALU.mult, ALU.add).then_inc(mean_ready, 1)
                dve.wait_ge(mean_ready, n + 1)
                dve.reciprocal(rms[:], rms[:]).then_inc(root_asked, 1)
                dve.wait_ge(root_ready, n + 1)
                dve.tensor_scalar(x_norm[:], x_in[s][:], rms[:], None, ALU.mult).then_inc(norm_ready, 1)

            def scale(n, s):
                dve.wait_ge(turned, n + 1)
                dve.tensor_tensor(h_tile[s][:], turn_ps[:], gain1[:].unsqueeze(2).broadcast_to([P, KT, P]),
                                  ALU.mult).then_inc(h_ready, 1)

            def finish(n, s):
                dve.wait_ge(qk_summed, 2 * n + 2)
                dve.tensor_reduce(qk_rms[:], qk_square[:].rearrange("p (g d) -> p g d", d=DH), AX.X, ALU.add).then_inc(qk_step, 1)
                dve.wait_ge(qk_step, 2 * n + 1)
                dve.tensor_scalar(qk_rms[:], qk_rms[:], 1.0 / DH, RMS_EPS, ALU.mult, ALU.add).then_inc(qk_step, 1)
                dve.wait_ge(qk_step, 2 * n + 2)
                dve.reciprocal(qk_rms[:], qk_rms[:]).then_inc(qk_asked, 1)
                dve.wait_ge(qk_root, n + 1)
                dve.tensor_tensor(qk_norm[:].rearrange("p (g d) -> p g d", d=DH),
                                  qk_ps[s][:].rearrange("p (g d) -> p g d", d=DH),
                                  qk_rms[:].unsqueeze(2).broadcast_to([P, GROUPS, DH]), ALU.mult).then_inc(qk_ready, 1)

            def tile(n, s, more=True):
                scale(n + 1, 1 - s)
                finish(n - 1, 1 - s)
                if more:
                    norm(n + 2, s)

            norm(0, 0)
            scale(0, 0)
            norm(1, 1)
            scale(1, 1)
            norm(2, 0)
            with dve.Fori(0, TT // 2 - 2) as pair:
                for s in (1, 0):
                    tile(2 * pair + 2 - s, s)
            tile(TT - 3, 1)
            tile(TT - 2, 0, more=False)
            finish(TT - 2, 0)
            finish(TT - 1, 1)
            dve.wait_ge(pads_ready, 1)
            dve.wait_ge(conv_kept, 2 + 2 * CT)
            dve.tensor_tensor(glu[:, :, CF_TAPS - 1:], convT[:, 0:CT], convT[:, CT:2 * CT], ALU.mult).then_inc(glu_ready, 1)
            dve.wait_ge(glu_ready, 1)
            for j in range(CF_TAPS):
                if j:
                    dve.wait_ge(tap_done, CT * j)
                for ct in range(CT):
                    if j == 0:
                        dve.tensor_scalar(conv[:, ct], glu[:, ct, 0:SEQ], taps_f[:, ct, 0:1], cols[:, ct, 0:1],
                                          ALU.mult, ALU.add).then_inc(tap_done, 1)
                    else:
                        dve.scalar_tensor_tensor(conv[:, ct], glu[:, ct, j:j + SEQ], taps_f[:, ct, j:j + 1], conv[:, ct],
                                                 ALU.mult, ALU.add).then_inc(tap_done, 1)

        @block.tensor
        def _(pe):
            pe.wait_ge(made, 2)

            def turn(n):
                pe.wait_ge(norm_ready, 2 + n + 1)
                for k in range(KT):
                    last = pe.transpose(turn_ps[:, k], x_norm[:, k * P:(k + 1) * P], ident[:])
                last.then_inc(turned, 1)

            def turn_qk(n):
                pe.wait_ge(qk_ready, n + 1)
                for b in range(2 * HEADS):
                    last = pe.transpose(qk_turn_ps[:, b], qk_norm[:, b * P:(b + 1) * P], ident[:])
                last.then_inc(qk_turned, 1)

            def project(n, s, before=True):
                for j in range(3):
                    out = v_ps[:] if j == 2 else qk_ps[s][:, DA * j:DA * (j + 1)]
                    pe.wait_ge(w_loaded[j], 16)
                    for k in range(KT):
                        last = pe.matmul(out, h_tile[s][:, k], w_qkv[:, k, DA * j:DA * (j + 1)],
                                         start=(k == 0), stop=(k == KT - 1))
                    if j == 0 and before:
                        turn_qk(n - 1)
                last.then_inc(qkv_ready, 1)

            def tile(n, s):
                pe.wait_ge(kept, n)
                turn(n + 1)
                pe.wait_ge(h_ready, n + 2)
                project(n, s)

            turn(0)
            pe.wait_ge(h_ready, 1)
            turn(1)
            pe.wait_ge(h_ready, 2)
            project(0, 0, before=False)
            with pe.Fori(0, TT // 2 - 2) as pair:
                for s in (1, 0):
                    tile(2 * pair + 2 - s, s)
            tile(TT - 3, 1)
            tile(TT - 2, 0)
            pe.wait_ge(kept, TT - 1)
            project(TT - 1, 1)
            pe.wait_ge(kept, TT)
            turn_qk(TT - 1)
            pe.sem_inc(conv_ready, 2)
            pe.wait_ge(h_kept, TT)
            pe.wait_ge(kept, TT + 1)
            with pe.Fori(0, CONV_TILES // 2) as pair:
                for s in range(2):
                    i = 2 * pair + s
                    pe.wait_ge(conv_loaded[s], 16 * (pair + 1))
                    pe.wait_ge(conv_kept, i + 1)
                    for half in range(2):
                        out = conv_ps[s][:, 512 * half:512 * (half + 1)]
                        for k in range(KT):
                            last = pe.matmul(out, w_conv[s][:, k], hT[:, k, 512 * half:512 * (half + 1)],
                                             start=(k == 0), stop=(k == KT - 1))
                    last.then_inc(conv_ready, 1)


def mix_phase(nc, mem, lam_vectors, subln_g, sc_w, qT, kT, values, convT, glu, conv, cols, mixedT):
    STEPS = TT * HEADS
    U_TILE, C_TILE = HEADS, HEADS + CT
    f = lambda name, shape: mem.sb(name, shape, F32)
    ident, ident_b, mask_b = f("ident_m", [P, P]), mem.sb("ident_b", [P, P], BF16), mem.sb("mask_b", [P, P], BF16)
    lam4, lam_sum, lam_exp, lam = f("lam4", [P, 4, DH]), f("lam_sum", [P, 2]), f("lam_exp", [P, 2]), f("lam", [P, 1])
    lam_product = f("lam_product", [P, 2, DH])
    neg_max, total = f("neg_max", [P, 2, 2]), f("total_m", [P, 2, 2])
    inverse, coef = f("inverse", [P, 2, 2]), f("coef", [P, 2])
    prob = [[f(f"prob{s}{c}", [P, SEQ]) for c in range(2)] for s in range(2)]
    probT = [f(f"probT{s}", [P, TT, P]) for s in range(2)]
    heads_out = f("heads_out", [P, TT, DA])
    heads_square = f("heads_square", [P, DV])
    heads_rms = f("heads_rms", [P, STEPS])
    gain_v = f("gain_v", [P, 1])
    gated = f("gated", [P, CT, SC_TAPS - 1 + SEQ])
    taps_s = f("taps_s", [P, CT, SC_TAPS])
    same_group = f("same_group", [P, P])
    squares = glu[:, :, 0:SEQ]
    with ExitStack() as ctx:
        sem = lambda name: ctx.enter_context(nc.semaphore(name))
        s_ps = [ctx.enter_context(nc.psum_tensor(f"s_ps{c}", [P, SEQ], F32)) for c in range(2)]
        pt_ps = ctx.enter_context(nc.psum_tensor("pt_ps", [P, TT, P], F32))
        o_ps = [ctx.enter_context(nc.psum_tensor(f"o_ps{s}", [P, 512], F32)) for s in range(2)]
        loaded, made = sem("loaded_m"), sem("made_m")
        lam_asked, lam_exped, lam_ready = sem("lam_asked"), sem("lam_exped"), sem("lam_ready")
        scores_ready, max_ready, probs_ready = sem("scores_ready"), sem("max_ready"), sem("probs_ready")
        chain, mix_ready, probT_ps_ready = sem("chain_m"), sem("mix_ready"), sem("probT_ps_ready")
        probT_ready, o_ready, o_kept = sem("probT_ready"), sem("o_ready"), sem("o_kept")
        c_ready, var_taken = sem("c_ready"), sem("var_taken")
        mean_ready, centred, squared = sem("mean_ready"), sem("centred"), sem("squared")
        var_ready, ln_asked, ln_root, ln_ready = sem("var_ready"), sem("ln_asked"), sem("ln_root"), sem("ln_ready")
        heads_squared, heads_asked, heads_root, heads_normed = sem("heads_squared"), sem("heads_asked"), sem("heads_root"), sem("heads_normed")
        heads_turned, heads_kept = sem("heads_turned"), sem("heads_kept")
        block = ctx.enter_context(nc.Block())

        @block.sync
        def _(sp):
            for a, b in ((lam4[:], lam_vectors.unsqueeze(0).broadcast_to([P, 4, DH])), (gain_v[:], subln_g), (taps_s[:], sc_w)):
                sp.dma_start(a, b).then_inc(loaded, 16)

        @block.gpsimd
        def _(pool):
            pool.memset(ident[:], 0.0).then_inc(made, 1)
            pool.memset(mask_b[:], 0.0).then_inc(made, 1)
            pool.memset(gated[:, :, 0:SC_TAPS - 1], 0.0).then_inc(made, 1)
            pool.memset(same_group[:], 0.0).then_inc(made, 1)
            pool.wait_ge(made, 4)
            pool.affine_select(out=ident[:], in_=ident[:], compare_op=ALU.not_equal, fill=1.0, base=0,
                               pattern=[[-1, P]], channel_multiplier=1).then_inc(made, 1)
            pool.affine_select(out=mask_b[:], in_=mask_b[:], compare_op=ALU.is_ge, fill=MASKED, base=0,
                               pattern=[[-1, P]], channel_multiplier=1).then_inc(made, 1)
            for half in range(P // LN_GROUP):
                at = slice(half * LN_GROUP, (half + 1) * LN_GROUP)
                pool.wait_ge(made, 6 + half)
                pool.memset(same_group[at, at], 1.0 / LN_GROUP).then_inc(made, 1)
            pool.wait_ge(made, 6 + P // LN_GROUP)
            pool.tensor_copy(ident_b[:], ident[:]).then_inc(made, 1)

        MADE = 7 + P // LN_GROUP
        width = lambda step: P * (step // HEADS + 1)

        @block.tensor
        def _(pe):
            pe.wait_ge(made, MADE)

            def scores(step):
                i, h, w = step // HEADS, step % HEADS, width(step)
                for c in range(2):
                    if step:
                        pe.wait_ge(probs_ready, 2 * (step - 1) + c + 1)
                    rows = slice(DH * c, DH * (c + 1))
                    for at in range(0, w, 512):
                        n = min(512, w - at)
                        pe.matmul(s_ps[c][:, at:at + n], qT[rows, h, i * P:(i + 1) * P], kT[rows, h, at:at + n],
                                  start=True, stop=(at + n < w))
                    pe.matmul(s_ps[c][:, w - P:w], ident_b[:], mask_b[:], start=False, stop=True).then_inc(scores_ready, 1)

            def turn(step):
                pe.wait_ge(mix_ready, step + 1)
                if step:
                    pe.wait_ge(probT_ready, step)
                for b in range(step // HEADS + 1):
                    last = pe.transpose(pt_ps[:, b], prob[step % 2][0][:, b * P:(b + 1) * P], ident[:])
                last.then_inc(probT_ps_ready, 1)

            def outputs(step):
                i, h = step // HEADS, step % HEADS
                pe.wait_ge(probT_ready, step + 1)
                if step >= 2:
                    pe.wait_ge(o_kept, step - 1)
                for b in range(i + 1):
                    last = pe.matmul(o_ps[step % 2][:, 0:DV], probT[step % 2][:, b], values[:, b, h * DV:(h + 1) * DV],
                                     start=(b == 0), stop=(b == i))
                last.then_inc(o_ready, 1)

            def group_mean(source, ready):
                for ct in range(CT):
                    for half in range(2):
                        at = slice(512 * half, 512 * (half + 1))
                        last = pe.matmul(s_ps[ct][:, at], same_group[:], source[:, ct, at], start=True, stop=True)
                last.then_inc(ready, 1)

            group_mean(conv, mean_ready)
            pe.wait_ge(squared, 1)
            group_mean(squares, var_ready)
            pe.wait_ge(var_taken, 1)
            scores(0)
            for step in range(STEPS):
                if step + 1 < STEPS:
                    scores(step + 1)
                turn(step)
                if step:
                    outputs(step - 1)
            outputs(STEPS - 1)
            for h in range(HEADS):
                pe.wait_ge(heads_normed, h + 1)
                if h:
                    pe.wait_ge(heads_kept, h)
                for i in range(TT):
                    last = pe.transpose(pt_ps[:, i], heads_out[:, i, h * DV:(h + 1) * DV], ident[:])
                last.then_inc(heads_turned, 1)

        @block.scalar
        def _(act):
            act.wait_ge(lam_asked, 1)
            act.activation(lam_exp[:], lam_sum[:], ACT.Exp).then_inc(lam_exped, 1)
            act.wait_ge(centred, 1)
            act.activation(squares, conv[:], ACT.Square).then_inc(squared, 1)

            def probT_copy(step):
                act.wait_ge(probT_ps_ready, step + 1)
                if step >= 2:
                    act.wait_ge(o_ready, step - 1)
                n = step // HEADS + 1
                act.activation(probT[step % 2][:, 0:n], pt_ps[:, 0:n], ACT.Copy).then_inc(probT_ready, 1)

            def head_square(step):
                i, h = step // HEADS, step % HEADS
                act.wait_ge(o_kept, step + 1)
                if step:
                    act.wait_ge(heads_squared, step)
                act.activation(heads_square[:], heads_out[:, i, h * DV:(h + 1) * DV], ACT.Square,
                               accum_out=heads_rms[:, step:step + 1]).then_inc(heads_squared, 1)

            for step in range(STEPS):
                s, w = step % 2, width(step)
                if step >= 2:
                    act.wait_ge(probT_ps_ready, step - 1)
                for c in range(2):
                    act.wait_ge(max_ready, 2 * step + c + 1)
                    act.activation(prob[s][c][:, 0:w], s_ps[c][:, 0:w], ACT.Exp, bias=neg_max[:, s, c:c + 1],
                                   accum_out=total[:, s, c:c + 1]).then_inc(probs_ready, 1)
                if step:
                    probT_copy(step - 1)
                if step >= 4:
                    head_square(step - 4)
                if step == 2:
                    act.wait_ge(ln_asked, 1)
                    act.activation(squares, squares, ACT.Sqrt).then_inc(ln_root, 1)
                if step == 5:
                    act.wait_ge(ln_ready, 1)
                    for ct in range(CT):
                        act.activation(mixedT[:, U_TILE + ct], conv[:, ct], ACT.Silu, bias=cols[:, ct, 2:3],
                                       scale=cols[:, ct, 1:2])
            probT_copy(STEPS - 1)
            for step in range(STEPS - 4, STEPS):
                head_square(step)
            act.wait_ge(heads_asked, 1)
            act.activation(heads_rms[:], heads_rms[:], ACT.Sqrt).then_inc(heads_root, 1)
            for h in range(HEADS):
                act.wait_ge(heads_turned, h + 1)
                act.activation(mixedT[:, h], pt_ps[:], ACT.Copy, scale=gain_v[:]).then_inc(heads_kept, 1)

        @block.vector
        def _(dve):
            steps_done = [0]

            def then(ins, s=chain):
                steps_done[0] += 1
                ins.then_inc(s, 1)
                dve.wait_ge(s, steps_done[0])

            lam_chain = lam_ready
            dve.wait_ge(loaded, 16 * 3)
            dve.wait_ge(made, MADE)
            dve.wait_ge(mean_ready, 1)
            for ct in range(CT):
                last = dve.tensor_tensor(conv[:, ct], conv[:, ct], s_ps[ct][:], ALU.subtract)
            last.then_inc(centred, 1)
            then(dve.tensor_tensor(lam_product[:], lam4[:, 0:4:2], lam4[:, 1:4:2], ALU.mult), lam_chain)
            dve.tensor_reduce(lam_sum[:], lam_product[:], AX.X, ALU.add).then_inc(lam_asked, 1)
            dve.wait_ge(lam_exped, 1)
            then(dve.tensor_tensor(lam[:], lam_exp[:, 1:2], lam_exp[:, 0:1], ALU.subtract), lam_chain)
            then(dve.tensor_scalar(lam[:], lam[:], LAM_INIT, None, ALU.subtract), lam_chain)
            then(dve.tensor_scalar(gain_v[:], gain_v[:], 1.0 - LAM_INIT, None, ALU.mult), lam_chain)
            then(dve.tensor_tensor(gated[:, :, SC_TAPS - 1:], convT[:, 3 * CT:4 * CT], convT[:, 4 * CT:5 * CT], ALU.mult), lam_chain)
            dve.wait_ge(var_ready, 1)
            for ct in range(CT):
                last = dve.tensor_scalar(squares[:, ct], s_ps[ct][:], LN_EPS, None, ALU.add)
            last.then_inc(var_taken, 1)
            steps_done[0] = 0

            def taps():
                short = mixedT[:, C_TILE:C_TILE + CT]
                for j in range(SC_TAPS):
                    for ct in range(CT):
                        if j == 0:
                            last = dve.tensor_scalar(short[:, ct], gated[:, ct, 0:SEQ], taps_s[:, ct, 0:1], None, ALU.mult)
                        else:
                            last = dve.scalar_tensor_tensor(short[:, ct], gated[:, ct, j:j + SEQ], taps_s[:, ct, j:j + 1],
                                                            short[:, ct], ALU.mult, ALU.add)
                    yield last
                yield dve.tensor_tensor(short, short, convT[:, 2 * CT:3 * CT], ALU.mult)

            tap = taps()
            TAPS = SC_TAPS + 1
            taps_done = 0

            def next_tap():
                nonlocal taps_done
                if taps_done < TAPS:
                    if taps_done:
                        dve.wait_ge(c_ready, taps_done)
                    next(tap).then_inc(c_ready, 1)
                    taps_done += 1

            def keep(step):
                i, h = step // HEADS, step % HEADS
                dve.wait_ge(o_ready, step + 1)
                dve.tensor_scalar(heads_out[:, i, h * DV:(h + 1) * DV], o_ps[step % 2][:, 0:DV],
                                  inverse[:, step % 2, 0:1], None, ALU.mult).then_inc(o_kept, 1)

            def maxima(step):
                for c in range(2):
                    dve.wait_ge(scores_ready, 2 * step + c + 1)
                    dve.tensor_reduce(neg_max[:, step % 2, c:c + 1], s_ps[c][:, 0:width(step)], AX.X, ALU.max,
                                      negate=True).then_inc(max_ready, 1)

            maxima(0)
            for step in range(STEPS):
                s, w = step % 2, width(step)
                if step >= 6:
                    next_tap()
                if step == 1:
                    dve.wait_ge(var_taken, 1)
                    dve.reciprocal(squares, squares).then_inc(ln_asked, 1)
                if step == 4:
                    dve.wait_ge(ln_root, 1)
                    dve.tensor_tensor(conv[:], conv[:], squares, ALU.mult).then_inc(ln_ready, 1)
                if step >= 2:
                    keep(step - 2)
                    dve.wait_ge(o_kept, step - 1)
                dve.wait_ge(probs_ready, 2 * step + 2)
                then(dve.reciprocal(inverse[:, s], total[:, s]))
                then(dve.tensor_scalar(coef[:, s:s + 1], total[:, s, 0:1], inverse[:, s, 1:2], lam[:], ALU.mult, ALU.mult))
                dve.scalar_tensor_tensor(prob[s][0][:, 0:w], prob[s][1][:, 0:w], coef[:, s:s + 1], prob[s][0][:, 0:w],
                                         ALU.mult, ALU.add).then_inc(mix_ready, 1)
                if step + 1 < STEPS:
                    maxima(step + 1)
            keep(STEPS - 2)
            keep(STEPS - 1)
            assert taps_done == TAPS and steps_done[0] == 2 * STEPS
            dve.wait_ge(heads_squared, STEPS)
            then(dve.tensor_scalar(heads_rms[:], heads_rms[:], 1.0 / DV, RMS_EPS, ALU.mult, ALU.add))
            dve.reciprocal(heads_rms[:], heads_rms[:]).then_inc(heads_asked, 1)
            dve.wait_ge(heads_root, 1)
            for h in range(HEADS):
                at = heads_out[:, :, h * DV:(h + 1) * DV]
                dve.tensor_tensor(at, at, heads_rms[:, h:STEPS:HEADS].unsqueeze(2).broadcast_to([P, TT, DV]),
                                  ALU.mult).then_inc(heads_normed, 1)


def output_phase(nc, mem, tiles_mem, x, norm2_g, w_out, mixedT, x_mid, h2_hi, h2_lo):
    RING = 2
    f = lambda name, shape: mem.sb(name, shape, F32)
    t = lambda name, shape: tiles_mem.sb(name, shape, F32)
    W_RING = 6
    w_raw = [f(f"wo_raw{s}", [P, D]) for s in range(W_RING)]
    w_hi, w_lo = mem.sb("wo_hi", [P, KT, D], F32R), mem.sb("wo_lo", [P, KT, D], F32R)
    m_hi = [m.sb(f"m_hi{s}", [P, KT, P], F32R) for s, m in enumerate((mem, tiles_mem))]
    m_lo = [m.sb(f"m_lo{s}", [P, KT, P], F32R) for s, m in enumerate((mem, tiles_mem))]
    x_in = t("x_in_o", [P, D])
    x_sum = t("x_sum", [P, D])
    x_norm = t("x_norm_o", [P, D])
    h_tile = t("h_tile_o", [P, KT, P])
    gain, ident, rms = f("gain2", [P, KT]), f("ident_o", [P, P]), f("rms_o", [P, 1])
    with ExitStack() as ctx:
        sem = lambda name: ctx.enter_context(nc.semaphore(name))
        out_ps = [ctx.enter_context(nc.psum_tensor(f"mixed_ps{s}", [P, D], F32)) for s in range(2)]
        turn_ps = ctx.enter_context(nc.psum_tensor("turn_o_ps", [P, KT, P], F32))
        w_loaded = [sem(f"wo_loaded{s}") for s in range(W_RING)]
        gain_loaded, x_loaded, made, stored = sem("gain_loaded"), sem("x_loaded_o"), sem("made_o"), sem("x_mid_stored")
        w_hi_ready, w_ready, m_hi_ready, m_ready = sem("wo_hi_ready"), sem("wo_ready"), sem("m_hi_ready"), sem("m_ready")
        mixed_ready, sum_ready, squared, asked = sem("mixed_ready"), sem("sum_ready"), sem("squared_o"), sem("asked_o")
        chain, root, norm_ready, turned = sem("chain_o"), sem("root_o"), sem("norm_ready_o"), sem("turned_o")
        h_ready, hi_ready, lo_ready = sem("h_ready_o"), sem("hi_ready"), sem("lo_ready")
        block = ctx.enter_context(nc.Block())

        @block.sync
        def _(sp):
            sp.dma_start(gain[:], norm2_g).then_inc(gain_loaded, 16)
            for k in range(KT):
                if k >= W_RING:
                    sp.wait_ge(w_ready, k - W_RING + 1)
                sp.dma_start(w_raw[k % W_RING][:], w_out[k * P:(k + 1) * P]).then_inc(w_loaded[k % W_RING], 16)
            sp.sem_inc(stored, 16)
            with sp.Fori(0, TT) as n:
                sp.wait_ge(sum_ready, 1 + n)
                sp.dma_start(x_in[:], x[n]).then_inc(x_loaded, 16)
                sp.wait_ge(sum_ready, 1 + n + 1)
                sp.dma_start(x_mid[n], x_sum[:]).then_inc(stored, 16)
            sp.wait_ge(stored, 16 * (TT + 1))

        @block.gpsimd
        def _(pool):
            pool.memset(ident[:], 0.0).then_inc(made, 1)
            pool.wait_ge(made, 1)
            pool.affine_select(out=ident[:], in_=ident[:], compare_op=ALU.not_equal, fill=1.0, base=0,
                               pattern=[[-1, P]], channel_multiplier=1).then_inc(made, 1)

        @block.scalar
        def _(act):
            for s in range(2):
                act.activation(m_hi[s][:], mixedT[:, :, P * s:P * (s + 1)], ACT.Copy).then_inc(m_hi_ready, 1)
            for k in range(KT):
                act.wait_ge(w_loaded[k % W_RING], 16 * (k // W_RING + 1))
                act.activation(w_hi[:, k], w_raw[k % W_RING][:], ACT.Copy).then_inc(w_hi_ready, 1)

            def tile(n, s, more=True):
                if more:
                    act.wait_ge(mixed_ready, n + 1)
                    act.activation(m_hi[s][:], mixedT[:, :, bass.ds(P * (n + 2), P)], ACT.Copy).then_inc(m_hi_ready, 1)
                act.wait_ge(sum_ready, 1 + n + 1)
                act.activation(x_norm[:], x_sum[:], ACT.Square, accum_out=rms[:]).then_inc(squared, 1)
                act.wait_ge(asked, n + 1)
                act.activation(rms[:], rms[:], ACT.Sqrt).then_inc(root, 1)
                act.wait_ge(h_ready, n + 1)
                act.activation(h2_hi[:, :, bass.ds(P * n, P)], h_tile[:], ACT.Copy).then_inc(hi_ready, 1)

            with act.Fori(0, TT // 2 - 1) as pair:
                for s in range(2):
                    tile(2 * pair + s, s)
            for s in range(2):
                tile(TT - 2 + s, s, more=False)

        @block.vector
        def _(dve):
            dve.wait_ge(gain_loaded, 16)
            dve.sem_inc(sum_ready, 1)

            def split_mixed(n, s):
                dve.wait_ge(m_hi_ready, n + 1)
                dve.tensor_tensor(m_lo[s][:], mixedT[:, :, bass.ds(P * n, P)], m_hi[s][:].bitcast(F32),
                                  ALU.subtract).then_inc(m_ready, 1)

            def tile(n, s, more=True):
                dve.wait_ge(mixed_ready, n + 1)
                dve.wait_ge(x_loaded, 16 * (n + 1))
                dve.wait_ge(stored, 16 * (n + 1))
                dve.tensor_tensor(x_sum[:], x_in[:], out_ps[s][:], ALU.add).then_inc(sum_ready, 1)
                if more:
                    split_mixed(n + 2, s)
                dve.wait_ge(squared, n + 1)
                dve.tensor_scalar(rms[:], rms[:], 1.0 / D, RMS_EPS, ALU.mult, ALU.add).then_inc(chain, 1)
                dve.wait_ge(chain, n + 1)
                dve.reciprocal(rms[:], rms[:]).then_inc(asked, 1)
                dve.wait_ge(root, n + 1)
                dve.tensor_scalar(x_norm[:], x_sum[:], rms[:], None, ALU.mult).then_inc(norm_ready, 1)
                dve.wait_ge(turned, n + 1)
                dve.tensor_tensor(h_tile[:], turn_ps[:], gain[:].unsqueeze(2).broadcast_to([P, KT, P]),
                                  ALU.mult).then_inc(h_ready, 1)
                dve.wait_ge(hi_ready, n + 1)
                at = bass.ds(P * n, P)
                dve.tensor_tensor(h2_lo[:, :, at], h_tile[:], h2_hi[:, :, at].bitcast(F32), ALU.subtract).then_inc(lo_ready, 1)
                dve.wait_ge(lo_ready, n + 1)

            for s in range(2):
                split_mixed(s, s)
            for k in range(KT):
                dve.wait_ge(w_hi_ready, k + 1)
                dve.tensor_tensor(w_lo[:, k], w_raw[k % W_RING][:], w_hi[:, k].bitcast(F32), ALU.subtract).then_inc(w_ready, 1)
            with dve.Fori(0, TT // 2 - 1) as pair:
                for s in range(2):
                    tile(2 * pair + s, s)
            for s in range(2):
                tile(TT - 2 + s, s, more=False)

        @block.tensor
        def _(pe):
            pe.wait_ge(made, 2)

            def project(n, s, first=False):
                pe.wait_ge(m_ready, n + 1)
                for k in range(KT):
                    if first:
                        pe.wait_ge(w_ready, k + 1)
                    for j, (m, w) in enumerate(((m_hi, w_hi), (m_hi, w_lo), (m_lo, w_hi))):
                        for half in range(2):
                            at = slice(512 * half, 512 * (half + 1))
                            last = pe.matmul(out_ps[s][:, at], m[s][:, k], w[:, k, at], start=(k == 0 and j == 0),
                                             stop=(k == KT - 1 and j == 2))
                last.then_inc(mixed_ready, 1)

            def turn(n):
                pe.wait_ge(norm_ready, n + 1)
                for k in range(KT):
                    last = pe.transpose(turn_ps[:, k], x_norm[:, k * P:(k + 1) * P], ident[:])
                last.then_inc(turned, 1)

            project(0, 0, first=True)
            with pe.Fori(0, TT // 2 - 1) as pair:
                for s in range(2):
                    n = 2 * pair + s
                    project(n + 1, 1 - s)
                    turn(n)
            project(TT - 1, 1)
            turn(TT - 2)
            turn(TT - 1)


def keys_phase(nc, mem, h2_hi, h2_lo, peer_wqt, keys_t, top_s, top_i):
    HC = 2 * PH
    RING = 2
    w_raw = [mem.sb(f"wq_raw{s}", [P, KT, P], F32) for s in range(2)]
    w_hi = [mem.sb(f"wq_hi{s}", [P, KT, P], F32R) for s in range(2)]
    w_lo = [mem.sb(f"wq_lo{s}", [P, KT, P], F32R) for s in range(2)]
    query = [mem.sb(f"query{s}", [P, SEQ], F32) for s in range(2)]
    keys = mem.sb("keys", [P, 2, P], F32)
    sub = [mem.sb(f"sub{s}", [P, TT, P], F32) for s in range(2)]
    best = mem.sb("best", [P, TT, TOPK], F32)
    best_at = mem.sb("best_at", [P, TT, TOPK], U32)
    with ExitStack() as ctx:
        sem = lambda name: ctx.enter_context(nc.semaphore(name))
        q_ps = [ctx.enter_context(nc.psum_tensor(f"q_ps{s}", [P, SEQ], F32)) for s in range(2)]
        sub_ps = [ctx.enter_context(nc.psum_tensor(f"sub_ps{s}", [P, TT, P], F32)) for s in range(2)]
        w_loaded = [sem(f"wq_loaded{s}") for s in range(2)]
        keys_loaded = [sem(f"keys_loaded{s}") for s in range(2)]
        w_hi_ready, w_ready, q_ready, query_ready = sem("wq_hi_ready"), sem("wq_ready"), sem("q_ready"), sem("query_ready")
        products_ready, sub_ready = sem("products_ready"), sem("sub_ready")
        picked, taken, replaced = sem("picked"), sem("taken"), sem("replaced")
        passed = sem("passed")
        block = ctx.enter_context(nc.Block())

        @block.sync
        def _(sp):
            with sp.Fori(0, HC // 2) as pair:
                for s in range(2):
                    i = 2 * pair + s
                    sp.wait_ge(w_ready, RING + i - 1)
                    sp.dma_start(w_raw[s][:], peer_wqt[i]).then_inc(w_loaded[s], 16)
                    sp.wait_ge(products_ready, RING + i - 1)
                    sp.dma_start(keys[:, s], keys_t[i]).then_inc(keys_loaded[s], 16)

        @block.tensor
        def _(pe):
            pe.sem_inc(q_ready, RING)
            pe.sem_inc(products_ready, RING)

            def project(i, s):
                pe.wait_ge(w_ready, RING + i + 1)
                pe.wait_ge(query_ready, RING + i - 1)
                for k in range(KT):
                    for n, (w, h) in enumerate(((w_hi, h2_hi), (w_hi, h2_lo), (w_lo, h2_hi))):
                        for half in range(2):
                            last = pe.matmul(q_ps[s][:, half * 512:(half + 1) * 512], w[s][:, k],
                                             h[:, k, half * 512:(half + 1) * 512],
                                             start=(k == 0 and n == 0), stop=(k == KT - 1 and n == 2))
                last.then_inc(q_ready, 1)

            def match(i, s, turn):
                pe.wait_ge(query_ready, RING + i + 1)
                pe.wait_ge(keys_loaded[s], 16 * (turn + 1))
                pe.wait_ge(sub_ready, RING + i - 1)
                for n in range(TT):
                    last = pe.matmul(sub_ps[s][:, n], query[s][:, n * P:(n + 1) * P], keys[:, s],
                                     start=True, stop=True)
                last.then_inc(products_ready, 1)

            project(0, 0)
            with pe.Fori(0, HC // 2 - 1) as pair:
                for s in range(2):
                    project(2 * pair + s + 1, 1 - s)
                    match(2 * pair + s, s, pair)
            project(HC - 1, 1)
            match(HC - 2, 0, HC // 2 - 1)
            match(HC - 1, 1, HC // 2 - 1)

        @block.scalar
        def _(act):
            act.sem_inc(query_ready, RING)
            act.sem_inc(sub_ready, RING)

            def split(i, s, turn):
                act.wait_ge(w_loaded[s], 16 * (turn + 1))
                act.wait_ge(q_ready, RING + i - 1)
                act.activation(w_hi[s][:], w_raw[s][:], ACT.Copy).then_inc(w_hi_ready, 1)

            def copies(i, s, turn=None):
                act.wait_ge(q_ready, RING + i + 1)
                act.wait_ge(products_ready, RING + i - 1)
                act.activation(query[s][:], q_ps[s][:], ACT.Copy).then_inc(query_ready, 1)
                if turn is not None:
                    split(i + 2, s, turn)
                act.wait_ge(products_ready, RING + i + 1)
                act.wait_ge(taken, i + 1)
                act.activation(sub[s][:], sub_ps[s][:], ACT.Copy).then_inc(sub_ready, 1)

            split(0, 0, 0)
            split(1, 1, 0)
            with act.Fori(0, HC // 2 - 1) as pair:
                for s in range(2):
                    copies(2 * pair + s, s, pair + 1)
            copies(HC - 2, 0)
            copies(HC - 1, 1)

        @block.vector
        def _(dve):
            dve.sem_inc(w_ready, RING)
            dve.sem_inc(taken, RING)

            def split(i, s):
                dve.wait_ge(w_hi_ready, i + 1)
                dve.tensor_tensor(w_lo[s][:], w_raw[s][:], w_hi[s][:].bitcast(F32), ALU.subtract).then_inc(w_ready, 1)

            def pick(i, s):
                STEPS = 4
                dve.wait_ge(sub_ready, RING + i + 1)
                dve.sem_inc(passed, 1)
                for half in range(2):
                    eight = slice(8 * half, 8 * half + 8)
                    for n in range(TT):
                        last = dve.max(best[:, n, eight], sub[s][:, n])
                    last.then_inc(picked, 1)
                    dve.wait_ge(picked, STEPS * i + 2 * half + 1)
                    dve.sem_inc(passed, 1)
                    for n in range(TT):
                        last = dve.max_index(best_at[:, n, eight], best[:, n, eight], sub[s][:, n])
                    if half == 0:
                        last.then_inc(picked, 1)
                        dve.wait_ge(picked, STEPS * i + 2)
                        dve.sem_inc(passed, 1)
                        for n in range(TT):
                            last = dve.match_replace(sub[s][:, n], best[:, n, eight], sub[s][:, n], TAKEN)
                        last.then_inc(replaced, 1)
                        dve.wait_ge(replaced, i + 1)
                        dve.sem_inc(passed, 1)
                    else:
                        last.then_inc(picked, 1)
                        dve.wait_ge(picked, STEPS * i + 4)
                dve.tensor_copy(top_s[:, :, i], best[:])
                dve.tensor_copy(top_i[:, :, i], best_at[:]).then_inc(taken, 1)
                dve.wait_ge(taken, RING + i + 1)

            split(0, 0)
            split(1, 1)
            with dve.Fori(0, HC // 2 - 1) as pair:
                for s in range(2):
                    split(2 * pair + s + 2, s)
                    pick(2 * pair + s, s)
            pick(HC - 2, 0)
            pick(HC - 1, 1)


def gates_phase(nc, mem, top_s, top_i, gates, h2_hi, h2_lo, peer_ut, early_gelu):
    PER_ROUND = GROUPS // TT
    CH = PH * TOPK
    BATCH = 8
    PER_TILE = P // BATCH
    RING = 4
    iota = mem.sb("iota", [P, P], F32)
    ident = mem.sb("ident", [P, P], F32)
    index = mem.sb("index", [P, 2, PH, TOPK], BF16)
    cand = mem.sb("cand", [P, PH, TOPK * TOPK], F32)
    sel_s = mem.sb("sel_s", [P, PH, TOPK], F32)
    sel_at = mem.sb("sel_at", [P, PH, TOPK], U32)
    sel_ab = mem.sb("sel_ab", [P, 2, CH], U32)
    ab = sel_ab[:].bitcast(F32)
    pick_of = mem.sb("pick_of", [P, CH, TOPK], BF16)
    chosen = mem.sb("chosen", [P, 3, CH], F32)
    total = mem.sb("total", [P, PH], F32)
    per_choice = mem.sb("per_choice", [P, 3, P], F32)
    is_1 = [mem.sb(f"is_1{s}", [P, BATCH, P], BF16) for s in range(2)]
    hot_1 = [mem.sb(f"hot_1{s}", [P, BATCH, P], F32) for s in range(RING)]
    hot_2 = [mem.sb(f"hot_2{s}", [P, BATCH, P], F32) for s in range(RING)]
    stage = [mem.sb(f"stage{s}", [P, P, GB], F32) for s in range(2)]
    e_raw = [mem.sb(f"e_raw{s}", [P, KT, P], F32) for s in range(2)]
    e_hi = [mem.sb(f"e_hi{s}", [P, KT, P], F32R) for s in range(2)]
    e_lo = [mem.sb(f"e_lo{s}", [P, KT, P], F32R) for s in range(2)]
    e_gelu = mem.sb("e_gelu", [P, SEQ], F32)
    iota_i = e_gelu[:, 0:P].bitcast(I32)
    with ExitStack() as ctx:
        sem = lambda name: ctx.enter_context(nc.semaphore(name))
        e_ps = ctx.enter_context(nc.psum_tensor("e_ps", [P, SEQ], F32))
        e_hi_ready, e_lo_ready, e_ready = sem("e_hi_ready"), sem("e_lo_ready"), sem("e_ready")
        e_gelu_ready, e_stored = sem("e_gelu_ready"), sem("e_stored")
        e_loaded = [sem(f"e_loaded{s}") for s in range(2)]
        turn_ps = ctx.enter_context(nc.psum_tensor("turn_ps", [P, 3, P], F32))
        gate_ps = [ctx.enter_context(nc.psum_tensor(f"gate_ps{s}", [P, BATCH, P], F32)) for s in range(2)]
        made, chain, summed = sem("made"), sem("chain"), sem("summed")
        passed = sem("passed_g")
        chosen_ready, turned, per_choice_ready = sem("chosen_ready"), sem("turned"), sem("per_choice_ready")
        exp_asked, exp_ready = sem("exp_asked"), sem("exp_ready")
        cand_ready, cand_free = sem("cand_ready"), sem("cand_free")
        is_ready, hot_2_ready = sem("is_ready"), sem("hot_2_ready")
        hot_ready, gate_ready, gate_copied = sem("hot_ready"), sem("gate_ready"), sem("gate_copied")
        stored = [sem(f"gates_stored{s}") for s in range(2)]
        block = ctx.enter_context(nc.Block())

        @block.gpsimd
        def _(pool):
            pool.iota(iota_i, pattern=[[1, P]], base=0, channel_multiplier=0).then_inc(made, 1)
            pool.memset(ident[:], 0.0).then_inc(made, 1)
            pool.wait_ge(made, 2)
            pool.tensor_copy(iota[:], iota_i).then_inc(made, 1)
            pool.affine_select(out=ident[:], in_=ident[:], compare_op=ALU.not_equal, fill=1.0, base=0,
                               pattern=[[-1, P]], channel_multiplier=1).then_inc(made, 1)
            pool.wait_ge(made, 4)
            pool.sem_inc(hot_ready, RING)

            def sums(n):
                pool.wait_ge(cand_free, n + 1)
                pair = top_s[:, n].rearrange("p (h c) k -> p h c k", c=2)
                for h in range(PH):
                    last = pool.tensor_tensor(cand[:, h].rearrange("p (a b) -> p a b", a=TOPK),
                                              pair[:, h, 0].unsqueeze(2).broadcast_to([P, TOPK, TOPK]),
                                              pair[:, h, 1].unsqueeze(1).broadcast_to([P, TOPK, TOPK]), ALU.add)
                last.then_inc(cand_ready, 1)

            def weigh(n, b, s):
                q = PER_TILE * n + b
                pool.wait_ge(is_ready, q + 1)
                pool.wait_ge(gate_ready, q + 1)
                pool.tensor_tensor(hot_1[s][:], is_1[s % 2][:],
                                   per_choice[:, 2, bass.ds(BATCH * b, BATCH)].unsqueeze(2).broadcast_to([P, BATCH, P]),
                                   ALU.mult).then_inc(hot_ready, 1)

            def weigh_tile(n):
                with pool.Fori(0, PER_TILE // RING) as turn:
                    for s in range(RING):
                        weigh(n, RING * turn + s, s)

            def split(m, s):
                pool.wait_ge(e_hi_ready, m + 1)
                pool.tensor_tensor(e_lo[s][:], e_raw[s][:], e_hi[s][:].bitcast(F32), ALU.subtract).then_inc(e_lo_ready, 1)

            def splits(r):
                for c in range(1, PER_ROUND):
                    split(PER_ROUND * r + c, c % 2)

            pool.sem_inc(e_lo_ready, 2)
            split(0, 0)
            sums(0)
            splits(0)
            sums(1)
            split(PER_ROUND, 0)
            with pool.Fori(1, TT - 1) as r:
                splits(r)
                sums(r + 1)
                split(PER_ROUND * (r + 1), 0)
                weigh_tile(r - 1)
            splits(TT - 1)
            weigh_tile(TT - 2)
            weigh_tile(TT - 1)

        @block.vector
        def _(dve):
            CHAIN = 14
            gate = chosen[:, 2].rearrange("p (h k) -> p h k", h=PH)
            dve.wait_ge(made, 4)

            def choose(n):
                steps = [0]

                def then(ins):
                    steps[0] += 1
                    ins.then_inc(chain, 1)
                    dve.wait_ge(chain, CHAIN * n + steps[0])
                    dve.sem_inc(passed, 1)

                then(dve.tensor_copy(index[:].rearrange("p c h k -> p h c k"),
                                     top_i[:, n].rearrange("p (h c) k -> p h c k", c=2)))
                dve.wait_ge(cand_ready, n + 1)
                dve.sem_inc(passed, 1)
                for half in range(2):
                    eight = slice(8 * half, 8 * half + 8)
                    for h in range(PH):
                        last = dve.max(sel_s[:, h, eight], cand[:, h])
                    then(last)
                    for h in range(PH):
                        last = dve.max_index(sel_at[:, h, eight], sel_s[:, h, eight], cand[:, h])
                    then(last)
                    if half == 0:
                        for h in range(PH):
                            last = dve.match_replace(cand[:, h], sel_s[:, h, eight], cand[:, h], TAKEN)
                        then(last)
                dve.sem_inc(cand_free, 1)
                flat = sel_at[:].rearrange("p h k -> p (h k)")
                dve.tensor_scalar(sel_ab[:, 0], flat, 4, None, ALU.logical_shift_right)
                then(dve.tensor_scalar(sel_ab[:, 1], flat, TOPK - 1, None, ALU.bitwise_and))
                then(dve.tensor_copy(ab, sel_ab[:]))
                dve.wait_ge(turned, n + 1)
                for side in range(2):
                    rank = ab[:, side].unsqueeze(2).broadcast_to([P, CH, TOPK])
                    ranks = iota[:, 0:TOPK].unsqueeze(1).broadcast_to([P, CH, TOPK])
                    then(dve.tensor_tensor(pick_of[:], rank, ranks, ALU.is_equal))
                    hk = pick_of[:].rearrange("p (h k) j -> p h k j", h=PH)
                    for h in range(PH):
                        last = dve.tensor_tensor(hk[:, h], hk[:, h],
                                                 index[:, side, h].unsqueeze(1).broadcast_to([P, TOPK, TOPK]),
                                                 ALU.mult)
                    then(last)
                    then(dve.tensor_reduce(chosen[:, side], pick_of[:], AX.X, ALU.add))
                dve.tensor_tensor(gate, sel_s[:], sel_s[:, :, 0:1].broadcast_to([P, PH, TOPK]),
                                  ALU.subtract).then_inc(exp_asked, 1)
                assert steps[0] == CHAIN, steps

            def normalise(n):
                dve.wait_ge(exp_ready, n + 1)
                dve.tensor_reduce(total[:], gate, AX.X, ALU.add).then_inc(summed, 1)
                dve.wait_ge(summed, 2 * n + 1)
                dve.reciprocal(total[:], total[:]).then_inc(summed, 1)
                dve.wait_ge(summed, 2 * n + 2)
                dve.tensor_tensor(gate, gate, total[:].unsqueeze(2).broadcast_to([P, PH, TOPK]),
                                  ALU.mult).then_inc(chosen_ready, 1)

            def one_hots(n, b, s):
                q = PER_TILE * n + b
                dve.wait_ge(gate_ready, q + 1)
                dve.wait_ge(hot_ready, RING + q - 1)
                keys = iota[:].unsqueeze(1).broadcast_to([P, BATCH, P])
                key = lambda side: per_choice[:, side, bass.ds(BATCH * b, BATCH)].unsqueeze(2).broadcast_to([P, BATCH, P])
                dve.tensor_tensor(is_1[s % 2][:], keys, key(0), ALU.is_equal).then_inc(is_ready, 1)
                dve.tensor_tensor(hot_2[s][:], keys, key(1), ALU.is_equal).then_inc(hot_2_ready, 1)

            def one_hots_tile(n):
                dve.wait_ge(per_choice_ready, 1 + n + 1)
                dve.sem_inc(passed, 1)
                with dve.Fori(0, PER_TILE // RING) as turn:
                    for s in range(RING):
                        one_hots(n, RING * turn + s, s)

            dve.sem_inc(cand_free, 1)
            choose(0)
            normalise(0)
            with dve.Fori(1, TT) as r:
                choose(r)
                one_hots_tile(r - 1)
                normalise(r)
            one_hots_tile(TT - 1)

        @block.tensor
        def _(pe):
            pe.wait_ge(made, 4)
            pe.sem_inc(turned, 1)
            pe.sem_inc(gate_ready, RING)

            def turn(n):
                pe.wait_ge(chosen_ready, n + 1)
                pe.wait_ge(per_choice_ready, n + 1)
                for k in range(3):
                    last = pe.transpose(turn_ps[:, k], chosen[:, k], ident[:])
                last.then_inc(turned, 1)

            def products(n):
                with pe.Fori(0, PER_TILE // RING) as round_:
                    for s in range(RING):
                        q = PER_TILE * n + RING * round_ + s
                        pe.wait_ge(hot_2_ready, q + 1)
                        pe.wait_ge(hot_ready, RING + q + 1)
                        pe.wait_ge(gate_copied, 2 + q - 1)
                        for t in range(BATCH):
                            last = pe.matmul(gate_ps[s % 2][:, t], hot_2[s][:, t], hot_1[s][:, t], start=True, stop=True)
                        last.then_inc(gate_ready, 1)

            def project(r):
                for c in range(PER_ROUND):
                    m, s = PER_ROUND * r + c, c % 2
                    pe.wait_ge(e_lo_ready, 2 + m + 1)
                    for half in range(2):
                        at = slice(512 * half, 512 * (half + 1))
                        pe.wait_ge(e_gelu_ready, 2 * m + half + 1)
                        for k in range(KT):
                            for j, (u, h) in enumerate(((e_hi, h2_hi), (e_hi, h2_lo), (e_lo, h2_hi))):
                                last = pe.matmul(e_ps[:, at], u[s][:, k], h[:, k, at], start=(k == 0 and j == 0),
                                                 stop=(k == KT - 1 and j == 2))
                        last.then_inc(e_ready, 1)

            pe.sem_inc(e_ready, 4)
            project(0)
            turn(0)
            with pe.Fori(1, TT) as r:
                project(r)
                products(r - 1)
                turn(r)
            products(TT - 1)

        @block.scalar
        def _(act):
            act.sem_inc(gate_copied, 2)
            gate = chosen[:, 2]

            def split(m, s, turn):
                act.wait_ge(e_loaded[s], 16 * (turn + 1))
                act.wait_ge(e_ready, 2 * m + 2)
                act.activation(e_hi[s][:], e_raw[s][:], ACT.Copy).then_inc(e_hi_ready, 1)

            def gelu(m):
                act.wait_ge(e_stored, 16 * (m + 1))
                for half in range(2):
                    at = slice(512 * half, 512 * (half + 1))
                    act.wait_ge(e_ready, 4 + 2 * m + half + 1)
                    act.activation(e_gelu[:, at], e_ps[:, at], ACT.Gelu).then_inc(e_gelu_ready, 1)
                act.wait_ge(e_gelu_ready, 2 + 2 * (m + 1))
                act.dma_start(early_gelu[m], e_gelu[:]).then_inc(e_stored, 16)

            def early(r, more=True):
                for c in range(PER_ROUND):
                    m = PER_ROUND * r + c
                    if more or c < PER_ROUND - 1:
                        split(m + 1, (c + 1) % 2, PER_ROUND // 2 * r + (c + 1) // 2)
                    gelu(m)

            def exp(n):
                act.wait_ge(exp_asked, n + 1)
                act.activation(gate, gate, ACT.Exp).then_inc(exp_ready, 1)

            def turned_choices(n):
                act.wait_ge(turned, n + 2)
                act.activation(per_choice[:], turn_ps[:], ACT.Copy).then_inc(per_choice_ready, 1)

            def copies(n):
                for part in range(2):
                    act.wait_ge(stored[part], 16 * (n + 1))
                    with act.Fori(0, GB // BATCH // 2) as pair:
                        for s in range(2):
                            b = 2 * pair + s
                            q = PER_TILE * n + (GB // BATCH) * part + b
                            act.wait_ge(gate_ready, RING + q + 1)
                            act.activation(stage[part][:, :, bass.ds(BATCH * b, BATCH)].rearrange("p k t -> p t k"),
                                           gate_ps[s][:], ACT.Copy).then_inc(gate_copied, 1)

            act.sem_inc(per_choice_ready, 1)
            act.sem_inc(e_gelu_ready, 2)
            act.sem_inc(e_stored, 16)
            split(0, 0, 0)
            early(0)
            exp(0)
            turned_choices(0)
            with act.Fori(1, TT - 1) as r:
                early(r)
                exp(r)
                copies(r - 1)
                turned_choices(r)
            early(TT - 1, more=False)
            exp(TT - 1)
            copies(TT - 2)
            turned_choices(TT - 1)
            copies(TT - 1)
            act.wait_ge(e_stored, 16 * (GROUPS + 1))

        @block.sync
        def _(sp):
            for s in range(2):
                sp.sem_inc(stored[s], 16)

            def load(m, s):
                sp.wait_ge(e_lo_ready, m + 1)
                sp.dma_start(e_raw[s][:], peer_ut[E * m + E - 1]).then_inc(e_loaded[s], 16)

            def store(n):
                for s in range(2):
                    sp.wait_ge(gate_copied, 2 + PER_TILE * n + (GB // BATCH) * (s + 1))
                    sp.dma_start(gates[2 * n + s], stage[s][:]).then_inc(stored[s], 16)

            AHEAD = 2
            for m in range(PER_ROUND + AHEAD):
                load(m, m % 2)
            with sp.Fori(1, TT - 1) as r:
                for c in range(AHEAD, PER_ROUND + AHEAD):
                    load(PER_ROUND * r + c, c % 2)
                store(r - 1)
            for c in range(AHEAD, PER_ROUND):
                load(PER_ROUND * (TT - 1) + c, c % 2)
            store(TT - 2)
            store(TT - 1)
            for s in range(2):
                sp.wait_ge(stored[s], 16 * (TT + 1))


def dense_phase(nc, mem, h2_hi, h2_lo, peer_ut, peer_v, gates, early_gelu, x_mid, out):
    HALVES = SEQ // 512
    BANKS = 4
    RING = 2
    OUTS = TT * (D // 512)

    Tile = namedtuple("Tile", "j early c slot next_turn")

    def group(pair, half):
        def tile(p):
            j = (0, 1, 3, 2)[p]
            if j == 3:
                return Tile(j, True, None, None, None)
            c = (E - 1) * half + j
            return Tile(j, False, 2 * (E - 1) * pair + c, c % 2, (E - 1) * pair + (c + 1) // 2)
        return tile

    u_raw = mem.sb("u_raw", [P, 2, KT, P], F32)
    u_hi = [mem.sb(f"u_hi{s}", [P, KT, P], F32R) for s in range(2)]
    u_lo = [mem.sb(f"u_lo{s}", [P, KT, P], F32R) for s in range(2)]
    v_raw = mem.sb("v_raw", [P, 2, D], F32)
    v_hi = mem.sb("v_hi", [P, E, D], F32R)
    v_lo = mem.sb("v_lo", [P, E, D], F32R)
    early = mem.sb("early", [P, SEQ], F32)
    gate = mem.sb("gate", [P, 2, SEQ], F32)
    weight = mem.sb("weight", [P, 2, SEQ], F32)
    w_hi = mem.sb("w_hi", [P, E, SEQ], F32R)
    w_lo = mem.sb("w_lo", [P, E, SEQ], F32R)
    acc = mem.sb("acc", [P, TT, D], F32)

    with ExitStack() as ctx:
        sem = lambda name: ctx.enter_context(nc.semaphore(name))
        z_ps = [ctx.enter_context(nc.psum_tensor(f"z_ps{s}", [P, SEQ], F32)) for s in range(2)]
        out_ps = [ctx.enter_context(nc.psum_tensor(f"out_ps{b}", [P, 512], F32)) for b in range(BANKS)]
        u_loaded = [sem(f"u_loaded{s}") for s in range(2)]
        v_loaded = [sem(f"v_loaded{s}") for s in range(2)]
        gate_loaded = [sem(f"gate_loaded{s}") for s in range(2)]
        acc_loaded, early_loaded = sem("acc_loaded"), sem("early_loaded")
        u_hi_ready, u_ready = sem("u_hi_ready"), sem("u_ready")
        v_hi_ready, v_ready = sem("v_hi_ready"), sem("v_ready")
        z_ready = sem("z_ready")
        gelu_ready, weight_ready = sem("gelu_ready"), sem("weight_ready")
        w_hi_ready, w_ready = sem("w_hi_ready"), sem("w_ready")
        out_ready, out_free, out_stored = sem("out_ready"), sem("out_free"), sem("out_stored")
        block = ctx.enter_context(nc.Block())

        @block.sync
        def _(sp):
            def load_u(g, p, kind):
                tile = kind(p)
                if tile.early:
                    sp.wait_ge(w_ready, RING + E * g - 1)
                    sp.dma_start(early[:], early_gelu[g]).then_inc(early_loaded, 16)
                else:
                    sp.wait_ge(u_ready, RING + tile.c - 1)
                    sp.dma_start(u_raw[:, tile.slot], peer_ut[E * g + tile.j]).then_inc(u_loaded[tile.slot], 16)

            def load_rest(g, p, kind):
                tile, q, s = kind(p), E * g + p, p % 2
                e = E * g + tile.j
                sp.wait_ge(weight_ready, RING + q - 1)
                sp.dma_start(gate[:, s].rearrange("p (b t) -> p b t", t=GB),
                             gates[:, :, e].rearrange("b p t -> p b t")).then_inc(gate_loaded[s], 16)
                sp.wait_ge(v_ready, RING + q - 1)
                sp.dma_start(v_raw[:, s], peer_v[e]).then_inc(v_loaded[s], 16)

            def load_group(g, pair, half, last=False):
                for p in range(E):
                    if p < E - 2:
                        load_u(g, p + 2, group(pair, half))
                    elif not last:
                        load_u(g + 1, p - 2, group(pair + half, 1 - half))
                    load_rest(g, p, group(pair, half))

            load_u(0, 0, group(0, 0))
            load_u(0, 1, group(0, 0))
            with sp.Fori(0, GROUPS // 2 - 1) as pair:
                for half in range(2):
                    load_group(2 * pair + half, pair, half)
            load_group(GROUPS - 2, GROUPS // 2 - 1, 0)
            load_group(GROUPS - 1, GROUPS // 2 - 1, 1, last=True)
            for n in range(TT):
                sp.wait_ge(out_free, BANKS + OUTS * (GROUPS - 1) + 2 * (n + 1))
                sp.dma_start(out[n * P:(n + 1) * P], acc[:, n]).then_inc(out_stored, 16)
            sp.wait_ge(out_stored, 16 * TT)

        @block.scalar
        def _(act):
            act.sem_inc(gelu_ready, RING)


            def split_u(c, slot, turn):
                act.wait_ge(u_loaded[slot], 16 * (turn + 1))
                act.wait_ge(z_ready, RING + c - 1)
                act.activation(u_hi[slot][:], u_raw[:, slot], ACT.Copy).then_inc(u_hi_ready, 1)

            def step(g, p, kind, more=True):
                tile, q, s = kind(p), E * g + p, p % 2
                turn = (E // 2) * g + p // 2
                if tile.early:
                    gelu = early[:]
                else:
                    gelu = weight[:, tile.slot]
                    if more:
                        split_u(tile.c + 1, 1 - tile.slot, tile.next_turn)
                    act.wait_ge(z_ready, RING + tile.c + 1)
                    act.wait_ge(w_ready, RING + q - 1)
                    act.activation(gelu, z_ps[tile.slot][:], ACT.Gelu).then_inc(gelu_ready, 1)
                act.wait_ge(v_loaded[s], 16 * (turn + 1))
                act.wait_ge(out_ready, OUTS * (g + 1))
                act.activation(v_hi[:, tile.j], v_raw[:, s], ACT.Copy).then_inc(v_hi_ready, 1)
                act.wait_ge(weight_ready, RING + q + 1)
                act.activation(w_hi[:, tile.j], gelu, ACT.Copy).then_inc(w_hi_ready, 1)

            split_u(0, 0, 0)
            def rest_of_group(g, pair, half):
                for p in range(1, E):
                    step(g, p, group(pair, half))
                step(g + 1, 0, group(pair + half, 1 - half))

            step(0, 0, group(0, 0))
            act.dma_start(acc[:], x_mid.rearrange("n p d -> p n d")).then_inc(acc_loaded, 16)
            with act.Fori(0, GROUPS // 2 - 1) as pair:
                for half in range(2):
                    rest_of_group(2 * pair + half, pair, half)
            rest_of_group(GROUPS - 2, GROUPS // 2 - 1, 0)
            for p in range(1, E):
                step(GROUPS - 1, p, group(GROUPS // 2 - 1, 1), more=p < E - 1)

        @block.vector
        def _(dve):
            dve.sem_inc(out_free, BANKS)
            for ready in (u_ready, v_ready, weight_ready, w_ready):
                dve.sem_inc(ready, RING)

            def split_u(c, slot):
                dve.wait_ge(u_hi_ready, c + 1)
                dve.tensor_tensor(u_lo[slot][:], u_raw[:, slot], u_hi[slot][:].bitcast(F32), ALU.subtract).then_inc(u_ready, 1)

            def step(g, p, kind, more=True, add_group=None):
                tile, q, s = kind(p), E * g + p, p % 2
                turn = (E // 2) * g + p // 2
                if tile.early:
                    weights = early[:]
                    dve.wait_ge(early_loaded, 16 * (g + 1))
                else:
                    weights = weight[:, tile.slot]
                    if more:
                        split_u(tile.c + 1, 1 - tile.slot)
                    dve.wait_ge(gelu_ready, RING + tile.c + 1)
                dve.wait_ge(gate_loaded[s], 16 * (turn + 1))
                dve.tensor_tensor(weights, weights, gate[:, s], ALU.mult).then_inc(weight_ready, 1)
                if add_group is not None:
                    add_outputs(add_group)
                dve.wait_ge(v_hi_ready, q + 1)
                dve.tensor_tensor(v_lo[:, tile.j], v_raw[:, s], v_hi[:, tile.j].bitcast(F32), ALU.subtract).then_inc(v_ready, 1)
                dve.wait_ge(w_hi_ready, q + 1)
                dve.tensor_tensor(w_lo[:, tile.j], weights, w_hi[:, tile.j].bitcast(F32), ALU.subtract).then_inc(w_ready, 1)

            def add_outputs(g):
                for o in range(OUTS):
                    dve.wait_ge(out_ready, OUTS * (g + 1) + o + 1)
                    part = acc[:, o // 2, (o % 2) * 512:(o % 2 + 1) * 512]
                    dve.tensor_tensor(part, part, out_ps[o % BANKS][:], ALU.add).then_inc(out_free, 1)

            split_u(0, 0)
            def rest_of_group(g, pair, half):
                for p in range(1, E):
                    step(g, p, group(pair, half))
                step(g + 1, 0, group(pair + half, 1 - half), add_group=g)

            step(0, 0, group(0, 0))
            dve.wait_ge(acc_loaded, 16)
            with dve.Fori(0, GROUPS // 2 - 1) as pair:
                for half in range(2):
                    rest_of_group(2 * pair + half, pair, half)
            rest_of_group(GROUPS - 2, GROUPS // 2 - 1, 0)
            for p in range(1, E):
                step(GROUPS - 1, p, group(GROUPS // 2 - 1, 1), more=p < E - 1)
            add_outputs(GROUPS - 1)

        @block.tensor
        def _(pe):
            pe.sem_inc(z_ready, RING)
            pe.sem_inc(out_ready, OUTS)

            def project_u(tile):
                s = tile.slot
                pe.wait_ge(u_ready, RING + tile.c + 1)
                pe.wait_ge(gelu_ready, RING + tile.c - 1)
                for k in range(KT):
                    for n, (u, h) in enumerate(((u_hi, h2_hi), (u_hi, h2_lo), (u_lo, h2_hi))):
                        for half in range(HALVES):
                            last = pe.matmul(z_ps[s][:, half * 512:(half + 1) * 512], u[s][:, k],
                                             h[:, k, half * 512:(half + 1) * 512],
                                             start=(k == 0 and n == 0), stop=(k == KT - 1 and n == 2))
                last.then_inc(z_ready, 1)

            def project_v(g):
                pe.wait_ge(w_ready, RING + E * (g + 1))
                pe.wait_ge(v_ready, RING + E * (g + 1))
                for o in range(OUTS):
                    n, half = o // 2, o % 2
                    pe.wait_ge(out_free, OUTS * g + o + 1)
                    for j in range(E):
                        for m, (w, v) in enumerate(((w_hi, v_hi), (w_hi, v_lo), (w_lo, v_hi))):
                            last = pe.matmul(out_ps[o % BANKS][:], w[:, j, n * P:(n + 1) * P],
                                             v[:, j, half * 512:(half + 1) * 512],
                                             start=(j == 0 and m == 0), stop=(j == E - 1 and m == 2))
                    last.then_inc(out_ready, 1)

            def rest_of_group(g, pair, half):
                for p in (1, 3):
                    project_u(group(pair, half)(p))
                project_u(group(pair + half, 1 - half)(0))
                project_v(g)

            project_u(group(0, 0)(0))
            with pe.Fori(0, GROUPS // 2 - 1) as pair:
                for half in range(2):
                    rest_of_group(2 * pair + half, pair, half)
            rest_of_group(GROUPS - 2, GROUPS // 2 - 1, 0)
            for p in (1, 3):
                project_u(group(GROUPS // 2 - 1, 1)(p))
            project_v(GROUPS - 1)
def build(nc, a, out):
    start, end = SBUF_START, nc.sbuf_usable_end
    KB = 1024
    x_mid = nc.dram_tensor("x_mid", (TT, P, D), F32, kind="Internal").ap()
    gates = nc.dram_tensor("gates", (SEQ // GB, P, N_KEYS, GB), F32, kind="Internal").ap()
    early_gelu = nc.dram_tensor("early_gelu", (GROUPS, P, SEQ), F32, kind="Internal").ap()
    x = a["x"].rearrange("b (n p) d -> (b n) p d", p=P)

    kept = Memory(nc, start, start + 88 * KB)
    qT = kept.sb("qT", [P, HEADS, SEQ], F32)
    kT = kept.sb("kT", [P, HEADS, SEQ], F32)
    values = kept.sb("values", [P, TT, DA], F32)
    convT = kept.sb("convT", [P, 5 * CT, SEQ], F32)
    mixed = Memory(nc, kept.at, end)
    mixedT = mixed.sb("mixedT", [P, KT, SEQ], F32)
    glu = mixed.sb("glu", [P, CT, CF_TAPS - 1 + SEQ], F32)
    conv = mixed.sb("conv", [P, CT, SEQ], F32)
    w_qkv_mem = Memory(nc, kept.at, mixed.at)
    taps_f = mixed.sb("taps_f", [P, CT, CF_TAPS], F32)
    cols = mixed.sb("cols", [P, CT, 3], F32)
    project_phase(nc, Memory(nc, mixed.at, end), w_qkv_mem, x, a["norm1_g"], a["w_in"], a["q_norm_g"], a["k_norm_g"],
                  a["cf_dw"], a["cf_cols"], qT, kT, values, convT, glu, conv, taps_f, cols)
    mix_phase(nc, mixed, a["lam_vectors"], a["subln_g"], a["sc_w"],
              qT, kT, values, convT, glu, conv, cols, mixedT)

    h2 = Memory(nc, start, start + 64 * KB)
    h2_hi = h2.sb("h2_hi", [P, KT, SEQ], F32R)
    h2_lo = h2.sb("h2_lo", [P, KT, SEQ], F32R)
    output_phase(nc, Memory(nc, kept.at + 32 * KB, end), Memory(nc, h2.at, kept.at), x, a["norm2_g"], a["w_out"], mixedT, x_mid, h2_hi, h2_lo)

    tops = Memory(nc, h2.at, end)
    top_s = tops.sb("top_s", [P, TT, 2 * PH, TOPK], F32)
    top_i = tops.sb("top_i", [P, TT, 2 * PH, TOPK], BF16)
    keys_phase(nc, Memory(nc, tops.at, end), h2_hi, h2_lo, a["peer_wqt"], a["keys_t"], top_s, top_i)
    gates_phase(nc, Memory(nc, tops.at, end), top_s, top_i, gates, h2_hi, h2_lo, a["peer_ut"], early_gelu)
    dense_phase(nc, Memory(nc, h2.at, end), h2_hi, h2_lo, a["peer_ut"], a["peer_v"], gates, early_gelu, x_mid, out)


def kernel(x, norm1_g, w_in, q_norm_g, k_norm_g, lam_q1, lam_k1, lam_q2, lam_k2, subln_g,
           cf_dw, cf_dw_b, cf_ln_g, cf_ln_b, sc_w, w_out, norm2_g,
           peer_wq, peer_keys, peer_u, peer_v):
    import concourse.bacc as bacc
    from concourse.bass_utils import run_bass_kernel_spmd

    def by_partition(v):
        return v.reshape(-1, P).T

    arrays = {
        "x": x,
        "norm1_g": by_partition(norm1_g[0]),
        "w_in": w_in[0],
        "q_norm_g": q_norm_g[0].reshape(DH, 1),
        "k_norm_g": k_norm_g[0].reshape(DH, 1),
        "lam_vectors": np.stack([lam_q1[0], lam_k1[0], lam_q2[0], lam_k2[0]]),
        "subln_g": subln_g[0].reshape(DV, 1),
        "cf_dw": cf_dw[0].reshape(CF_TAPS, CT, P).transpose(2, 1, 0),
        "cf_cols": np.stack([by_partition(v[0]) for v in (cf_dw_b, cf_ln_g, cf_ln_b)], axis=-1),
        "sc_w": sc_w[0].reshape(SC_TAPS, CT, P).transpose(2, 1, 0),
        "w_out": w_out[0],
        "norm2_g": by_partition(norm2_g[0]),
        "peer_wqt": peer_wq[0].reshape(KT, P, 2 * PH, P).transpose(2, 1, 0, 3),
        "keys_t": peer_keys[0].reshape(2 * PH, N_KEYS, P).transpose(0, 2, 1),
        "peer_ut": peer_u[0].reshape(N_KEYS, N_KEYS, KT, P).transpose(0, 3, 2, 1),
        "peer_v": peer_v[0].reshape(N_KEYS, N_KEYS, D),
    }
    arrays = {name: np.ascontiguousarray(v) for name, v in arrays.items()}
    nc = bacc.Bacc("TRN2", target_bir_lowering=False, num_devices=1, dynamic_dma_scratch_size=DMA_SCRATCH)
    args = {name: nc.dram_tensor(f"in_{name}", v.shape, mybir.dt.from_np(v.dtype), kind="ExternalInput").ap()
            for name, v in arrays.items()}
    out = nc.dram_tensor("out", (1, SEQ, D), F32, kind="ExternalOutput").ap()
    build(nc, args, out.rearrange("b s d -> (b s) d"))
    result = run_bass_kernel_spmd(nc, [{f"in_{name}": v for name, v in arrays.items()}], core_ids=[0])
    return result.results[0]["out"]
```
